# Optimizing a Trainium2 kernel written in Bass

```python
import jax, jax.numpy as jnp
from jax import lax
import numpy as np

D_MODEL = 1024
BATCH = 1
SEQ = 256
DEPTH = 2

CHUNK = 64
Q_BLOCK = 128
RMS_EPS = 1e-6
D_FF = 2816
POOL_WINDOWS = (2, 4, 8, 16)
POOL_GROUP = D_MODEL // 8
POOL_WIDTH = POOL_GROUP * len(POOL_WINDOWS)
FOX_HEADS = 8
FOX_HEAD_DIM = D_MODEL // (2 * FOX_HEADS)
FOX_WIDTH = FOX_HEADS * FOX_HEAD_DIM
AB_IN = POOL_WIDTH + 3 * FOX_WIDTH + FOX_HEADS
AB_MIX = POOL_WIDTH + FOX_WIDTH
MLA_HEADS = 16
MLA_NOPE = 64
MLA_ROPE = 32
MLA_V = 64
MLA_Q_LORA = 256
MLA_KV_LORA = 128
MLA_IN = MLA_Q_LORA + MLA_KV_LORA + MLA_ROPE
ROPE_THETA = 10000.0
N_EVEN = (DEPTH + 1) // 2
N_ODD = DEPTH // 2


def rms_norm(x, g):
    xf = x.astype(jnp.float32)
    y = xf * lax.rsqrt(jnp.mean(xf * xf, axis=-1, keepdims=True) + RMS_EPS)
    return (y * g.astype(jnp.float32)).astype(x.dtype)

def swiglu(x, w_gate, w_up, w_down):
    return (jax.nn.silu(x @ w_gate) * (x @ w_up)) @ w_down

def rope_tables(positions):
    inv_freq = ROPE_THETA ** (-jnp.arange(0, MLA_ROPE, 2, dtype=jnp.float32) / MLA_ROPE)
    ang = positions.astype(jnp.float32)[..., None] * inv_freq
    return jnp.cos(ang), jnp.sin(ang)

def apply_rope(x, cos, sin):
    xf = x.astype(jnp.float32)
    half = xf.shape[-1] // 2
    x1, x2 = xf[..., :half], xf[..., half:]
    return jnp.concatenate([x1 * cos - x2 * sin, x2 * cos + x1 * sin], axis=-1).astype(x.dtype)

def blocked_attention(q, k, v, scale, chunk, log_decay=None):
    b, s, h, dk = q.shape
    dv = v.shape[-1]
    nb = s // Q_BLOCK
    q = q * scale
    qb = q.reshape(b, nb, Q_BLOCK, h, dk).transpose(1, 0, 2, 3, 4)
    k_chunk = jnp.arange(s) // chunk
    xs = (qb, jnp.arange(nb))
    if log_decay is not None:
        fk = log_decay.transpose(0, 2, 1)
        fqb = log_decay.reshape(b, nb, Q_BLOCK, h).transpose(1, 0, 3, 2)
        xs = xs + (fqb,)

    def attend(args):
        q_blk, blk = args[0], args[1]
        logits = jnp.einsum('bqhd,bkhd->bhqk', q_blk, k).astype(jnp.float32)
        if log_decay is not None:
            logits = logits + (args[2][..., None] - fk[:, :, None, :])
        t_pos = blk * Q_BLOCK + jnp.arange(Q_BLOCK)
        allowed = k_chunk[None, :] <= (t_pos // chunk)[:, None]
        logits = jnp.where(allowed, logits, -jnp.inf)
        p = jax.nn.softmax(logits, axis=-1)
        return jnp.einsum('bhqk,bkhd->bqhd', p.astype(v.dtype), v)

    out = lax.map(attend, xs)
    return out.transpose(1, 0, 2, 3, 4).reshape(b, s, h, dv)

def pool_mixer(u, w_pool, pool_scale):
    s = u.shape[1]
    cs = jnp.cumsum(u.astype(jnp.float32), axis=1)
    t_count = jnp.arange(s) + 1
    outs = []
    for g, w in enumerate(POOL_WINDOWS):
        lo, hi = g * POOL_GROUP, (g + 1) * POOL_GROUP
        cs_g = cs[..., lo:hi]
        lagged = jnp.pad(cs_g, ((0, 0), (w, 0), (0, 0)))[:, :s]
        count = jnp.minimum(t_count, w).astype(jnp.float32)[None, :, None]
        diff = (cs_g - lagged) / count - u[..., lo:hi].astype(jnp.float32)
        outs.append(diff.astype(u.dtype) @ w_pool[g])
    return jnp.concatenate(outs, axis=-1) * pool_scale

def pool_fox_mixer(h, w_in, b_forget, w_pool, pool_scale, w_out):
    b, s, _ = h.shape
    proj = h @ w_in
    o1 = POOL_WIDTH
    o2 = o1 + FOX_WIDTH
    o3 = o2 + FOX_WIDTH
    o4 = o3 + FOX_WIDTH
    u = proj[..., :o1]
    q = proj[..., o1:o2].reshape(b, s, FOX_HEADS, FOX_HEAD_DIM)
    k = proj[..., o2:o3].reshape(b, s, FOX_HEADS, FOX_HEAD_DIM)
    v = proj[..., o3:o4].reshape(b, s, FOX_HEADS, FOX_HEAD_DIM)
    f_logit = proj[..., o4:] + b_forget
    y_pool = pool_mixer(u, w_pool, pool_scale)
    log_f = jax.nn.log_sigmoid(f_logit.astype(jnp.float32))
    cum_log_f = jnp.cumsum(log_f, axis=1)
    y_fox = blocked_attention(q, k, v, FOX_HEAD_DIM ** -0.5, 1, cum_log_f)
    y = jnp.concatenate([y_pool, y_fox.reshape(b, s, FOX_WIDTH)], axis=-1)
    return y @ w_out

def mla_mixer(h, cos, sin, w_in, q_norm, kv_norm, w_q_b, w_kv_b, w_out):
    b, s, _ = h.shape
    proj = h @ w_in
    c_q = proj[..., :MLA_Q_LORA]
    c_kv = proj[..., MLA_Q_LORA:MLA_Q_LORA + MLA_KV_LORA]
    k_rope = apply_rope(proj[..., MLA_Q_LORA + MLA_KV_LORA:], cos, sin)
    q = (rms_norm(c_q, q_norm) @ w_q_b).reshape(b, s, MLA_HEADS, MLA_NOPE + MLA_ROPE)
    q_rope = apply_rope(q[..., MLA_NOPE:], cos[:, :, None, :], sin[:, :, None, :])
    qk = jnp.concatenate([q[..., :MLA_NOPE], q_rope], axis=-1)
    kv = (rms_norm(c_kv, kv_norm) @ w_kv_b).reshape(b, s, MLA_HEADS, MLA_NOPE + MLA_V)
    k = jnp.concatenate(
        [kv[..., :MLA_NOPE], jnp.broadcast_to(k_rope[:, :, None, :], (b, s, MLA_HEADS, MLA_ROPE))],
        axis=-1)
    v = kv[..., MLA_NOPE:]
    y = blocked_attention(qk, k, v, (MLA_NOPE + MLA_ROPE) ** -0.5, CHUNK)
    return y.reshape(b, s, MLA_HEADS * MLA_V) @ w_out

def first_inputs(seed: int = 0) -> dict:
    key = jax.random.key(seed)
    ks = jax.random.split(key, 20)

    def normal(k, shape, scale):
        return scale * jax.random.normal(k, shape, jnp.float32)

    x = normal(ks[0], (BATCH, SEQ, D_MODEL), 1.0)
    start = jax.random.randint(ks[1], (BATCH, 1), 0, 64, dtype=jnp.int32) * CHUNK
    positions = (start + jnp.arange(SEQ, dtype=jnp.int32)[None, :]).astype(jnp.int32)
    norm_ffn = 1.0 + normal(ks[2], (DEPTH, 2, D_MODEL), 0.05)
    norm_mix = 1.0 + normal(ks[3], (DEPTH, D_MODEL), 0.05)
    norm_final = 1.0 + normal(ks[4], (D_MODEL,), 0.05)
    ffn_w_gate = normal(ks[5], (DEPTH, 2, D_MODEL, D_FF), D_MODEL ** -0.5)
    ffn_w_up = normal(ks[6], (DEPTH, 2, D_MODEL, D_FF), D_MODEL ** -0.5)
    ffn_w_down = normal(ks[7], (DEPTH, 2, D_FF, D_MODEL), D_FF ** -0.5)
    ab_w_in = normal(ks[8], (N_EVEN, D_MODEL, AB_IN), D_MODEL ** -0.5)
    ab_b_forget = jax.random.uniform(ks[9], (N_EVEN, FOX_HEADS), jnp.float32, 1.0, 6.0)
    pool_w = normal(ks[10], (N_EVEN, len(POOL_WINDOWS), POOL_GROUP, POOL_GROUP), POOL_GROUP ** -0.5)
    pool_scale = 1.0 + normal(ks[11], (N_EVEN, POOL_WIDTH), 0.1)
    ab_w_out = normal(ks[12], (N_EVEN, AB_MIX, D_MODEL), AB_MIX ** -0.5)
    mla_w_in = normal(ks[13], (N_ODD, D_MODEL, MLA_IN), D_MODEL ** -0.5)
    mla_q_norm = 1.0 + normal(ks[14], (N_ODD, MLA_Q_LORA), 0.05)
    mla_kv_norm = 1.0 + normal(ks[15], (N_ODD, MLA_KV_LORA), 0.05)
    mla_w_q_b = normal(ks[16], (N_ODD, MLA_Q_LORA, MLA_HEADS * (MLA_NOPE + MLA_ROPE)), MLA_Q_LORA ** -0.5)
    mla_w_kv_b = normal(ks[17], (N_ODD, MLA_KV_LORA, MLA_HEADS * (MLA_NOPE + MLA_V)), MLA_KV_LORA ** -0.5)
    mla_w_out = normal(ks[18], (N_ODD, MLA_HEADS * MLA_V, D_MODEL), (MLA_HEADS * MLA_V) ** -0.5)
    return {'x': x, 'positions': positions, 'norm_ffn': norm_ffn, 'norm_mix': norm_mix,
            'norm_final': norm_final, 'ffn_w_gate': ffn_w_gate, 'ffn_w_up': ffn_w_up,
            'ffn_w_down': ffn_w_down, 'ab_w_in': ab_w_in, 'ab_b_forget': ab_b_forget,
            'pool_w': pool_w, 'pool_scale': pool_scale, 'ab_w_out': ab_w_out,
            'mla_w_in': mla_w_in, 'mla_q_norm': mla_q_norm, 'mla_kv_norm': mla_kv_norm,
            'mla_w_q_b': mla_w_q_b, 'mla_w_kv_b': mla_w_kv_b, 'mla_w_out': mla_w_out}

def first_block(x, positions, norm_ffn, norm_mix, norm_final, ffn_w_gate, ffn_w_up, ffn_w_down,
              ab_w_in, ab_b_forget, pool_w, pool_scale, ab_w_out,
              mla_w_in, mla_q_norm, mla_kv_norm, mla_w_q_b, mla_w_kv_b, mla_w_out):
    cos, sin = rope_tables(positions)
    h = x
    for layer in range(DEPTH):
        h = h + 0.5 * swiglu(rms_norm(h, norm_ffn[layer, 0]), ffn_w_gate[layer, 0],
                             ffn_w_up[layer, 0], ffn_w_down[layer, 0])
        hn = rms_norm(h, norm_mix[layer])
        i = layer // 2
        if layer % 2 == 0:
            h = h + pool_fox_mixer(hn, ab_w_in[i], ab_b_forget[i], pool_w[i], pool_scale[i], ab_w_out[i])
        else:
            h = h + mla_mixer(hn, cos, sin, mla_w_in[i], mla_q_norm[i], mla_kv_norm[i],
                              mla_w_q_b[i], mla_w_kv_b[i], mla_w_out[i])
        h = h + 0.5 * swiglu(rms_norm(h, norm_ffn[layer, 1]), ffn_w_gate[layer, 1],
                             ffn_w_up[layer, 1], ffn_w_down[layer, 1])
    return rms_norm(h, norm_final)


N_A_LAYERS = DEPTH // 2
N_B_LAYERS = DEPTH - N_A_LAYERS
EPS = 1e-6
NEG = -1e30

M_HEADS = 8
M_DV = D_MODEL // M_HEADS
M_DQK = M_DV // 2
M_CHUNK = 64

N_QH = 16
N_KVH = 4
HEAD_DIM = 64
CMP_BLOCK = 32
CMP_STRIDE = 16
CMP_HIDDEN = 256
SEL_BLOCK = 64
SEL_TOPK = 16
WINDOW = 512
Q_BLOCK_2 = 64
FORCE_SCORE = 1e4


def rmsnorm(x, g):
    xf = x.astype(jnp.float32)
    y = xf * lax.rsqrt(jnp.mean(xf * xf, axis=-1, keepdims=True) + EPS)
    return (y * g.astype(jnp.float32)).astype(x.dtype)

def swiglu_2(h, w_in, w_out):
    a, b = jnp.split(h @ w_in, 2, axis=-1)
    return (jax.nn.silu(a) * b) @ w_out

def masked_softmax(s, mask):
    s = jnp.where(mask, s.astype(jnp.float32), NEG)
    e = jnp.where(mask, jnp.exp(s - jnp.max(s, axis=-1, keepdims=True)), 0.0)
    z = jnp.sum(e, axis=-1, keepdims=True)
    return e / jnp.where(z > 0, z, 1.0)

def mlstm_mixer(h, w_in, b_if, g_head, w_out):
    B, T, _ = h.shape
    H, L = M_HEADS, M_CHUNK
    NC = T // L
    qk_w, v_w = H * M_DQK, H * M_DV
    proj = h @ w_in
    q, k, v, ig, fg, og = jnp.split(
        proj, [qk_w, 2 * qk_w, 2 * qk_w + v_w, 2 * qk_w + v_w + H, 2 * qk_w + v_w + 2 * H], axis=-1)

    def to_chunks(a, d):
        return a.astype(jnp.float32).reshape(B, NC, L, H, d).transpose(0, 3, 1, 2, 4)

    q = to_chunks(q, M_DQK) * (M_DQK ** -0.5)
    k = to_chunks(k, M_DQK)
    v = to_chunks(v, M_DV)
    bif = b_if.astype(jnp.float32)
    log_i = to_chunks(ig, 1)[..., 0] + bif[0][:, None, None]
    log_f = jax.nn.log_sigmoid(to_chunks(fg, 1)[..., 0] + bif[1][:, None, None])

    b = jnp.cumsum(log_f, axis=-1)
    g_tot = b[..., -1]
    a = g_tot[..., None] - b + log_i
    m_loc = jnp.max(a, axis=-1)
    w_loc = jnp.exp(a - m_loc[..., None])
    C_loc = jnp.einsum('bhcl,bhclk,bhclv->bhckv', w_loc, k, v)
    n_loc = jnp.einsum('bhcl,bhclk->bhck', w_loc, k)

    def step(carry, inp):
        C, n, m = carry
        g, Cl, nl, ml = inp
        m_new = jnp.maximum(g + m, ml)
        s_old = jnp.exp(g + m - m_new)
        s_new = jnp.exp(ml - m_new)
        C_new = s_old[..., None, None] * C + s_new[..., None, None] * Cl
        n_new = s_old[..., None] * n + s_new[..., None] * nl
        return (C_new, n_new, m_new), (C, n, m)

    init = (jnp.zeros((B, H, M_DQK, M_DV), jnp.float32),
            jnp.zeros((B, H, M_DQK), jnp.float32),
            jnp.zeros((B, H), jnp.float32))
    xs = (jnp.moveaxis(g_tot, 2, 0), jnp.moveaxis(C_loc, 2, 0),
          jnp.moveaxis(n_loc, 2, 0), jnp.moveaxis(m_loc, 2, 0))
    _, (C_prev, n_prev, m_prev) = lax.scan(step, init, xs)
    C_prev = jnp.moveaxis(C_prev, 0, 2)
    n_prev = jnp.moveaxis(n_prev, 0, 2)
    m_prev = jnp.moveaxis(m_prev, 0, 2)

    causal = jnp.tril(jnp.ones((L, L), bool))
    D = jnp.where(causal, b[..., :, None] - b[..., None, :] + log_i[..., None, :], -jnp.inf)
    inter = b + m_prev[..., None]
    m_t = jnp.maximum(inter, jnp.max(D, axis=-1))
    W = jnp.exp(D - m_t[..., None]) * jnp.einsum('bhctk,bhcsk->bhcts', q, k)
    s_inter = jnp.exp(inter - m_t)
    num = (s_inter[..., None] * jnp.einsum('bhctk,bhckv->bhctv', q, C_prev)
           + jnp.einsum('bhcts,bhcsv->bhctv', W, v))
    den = s_inter * jnp.einsum('bhctk,bhck->bhct', q, n_prev) + jnp.sum(W, axis=-1)
    h_out = num / jnp.maximum(jnp.abs(den), jnp.exp(-m_t))[..., None]
    h_out = h_out.astype(h.dtype).transpose(0, 2, 3, 1, 4).reshape(B, T, H, M_DV)
    h_out = rmsnorm(h_out, g_head).reshape(B, T, H * M_DV)
    return (h_out * jax.nn.sigmoid(og)) @ w_out

def nsa_shared_kv(s, kv_norm, kv_w, cmp_pe, cmp_w1, cmp_w2, k_norm):
    B, T, _ = s.shape
    n_cmp = (T - CMP_BLOCK) // CMP_STRIDE + 1
    kv = rmsnorm(s, kv_norm) @ kv_w
    kc, vc, ks, vs, kw, vw = [a.reshape(B, T, N_KVH, HEAD_DIM) for a in jnp.split(kv, 6, axis=-1)]
    idx = jnp.arange(n_cmp)[:, None] * CMP_STRIDE + jnp.arange(CMP_BLOCK)[None, :]

    def compress(a, pe, w1, w2):
        blk = a[:, idx] + pe[:, None, :]
        flat = blk.transpose(0, 1, 3, 2, 4).reshape(B, n_cmp, N_KVH, CMP_BLOCK * HEAD_DIM)
        return jax.nn.silu(flat @ w1) @ w2

    k_cmp = rmsnorm(compress(kc, cmp_pe[0], cmp_w1[0], cmp_w2[0]), k_norm[0])
    v_cmp = compress(vc, cmp_pe[1], cmp_w1[1], cmp_w2[1])
    ks = rmsnorm(ks, k_norm[1])
    kw = rmsnorm(kw, k_norm[2])
    return (k_cmp, v_cmp, ks, vs, kw, vw)

def cmp_sel_overlap(n_cmp, n_sel):
    c0 = jnp.arange(n_cmp) * CMP_STRIDE
    s0 = jnp.arange(n_sel) * SEL_BLOCK
    ov = (c0[:, None] < s0[None, :] + SEL_BLOCK) & (c0[:, None] + CMP_BLOCK > s0[None, :])
    return ov.astype(jnp.float32)

def nsa_mixer(h, kv, w_in, q_norm, w_out):
    k_cmp, v_cmp, k_sel, v_sel, k_win, v_win = kv
    B, T, _ = h.shape
    G = N_QH // N_KVH
    n_cmp = k_cmp.shape[1]
    n_sel = T // SEL_BLOCK
    top = min(SEL_TOPK, n_sel)
    proj = h @ w_in
    q = proj[..., :N_QH * HEAD_DIM].reshape(B, T, N_KVH, G, HEAD_DIM)
    q = rmsnorm(q, q_norm) * (HEAD_DIM ** -0.5)
    gates = jax.nn.sigmoid(proj[..., N_QH * HEAD_DIM:].astype(jnp.float32)).reshape(B, T, 3, N_KVH, G)

    overlap = cmp_sel_overlap(n_cmp, n_sel)
    cmp_end = jnp.arange(n_cmp) * CMP_STRIDE + CMP_BLOCK - 1
    sel_id = jnp.arange(n_sel)
    ks_blk = k_sel.reshape(B, n_sel, SEL_BLOCK, N_KVH, HEAD_DIM).transpose(0, 3, 1, 2, 4)
    vs_blk = v_sel.reshape(B, n_sel, SEL_BLOCK, N_KVH, HEAD_DIM).transpose(0, 3, 1, 2, 4)
    kw_pad = jnp.pad(k_win, ((0, 0), (WINDOW, 0), (0, 0), (0, 0)))
    vw_pad = jnp.pad(v_win, ((0, 0), (WINDOW, 0), (0, 0), (0, 0)))
    b_ix = jnp.arange(B)[:, None, None, None]
    h_ix = jnp.arange(N_KVH)[None, None, :, None]
    dt = v_sel.dtype

    def block(qb):
        s0 = qb * Q_BLOCK_2
        t = s0 + jnp.arange(Q_BLOCK_2)
        qq = lax.dynamic_slice_in_dim(q, s0, Q_BLOCK_2, axis=1)
        gb = lax.dynamic_slice_in_dim(gates, s0, Q_BLOCK_2, axis=1).astype(dt)
        s_c = jnp.einsum('bqhgd,bchd->bqhgc', qq, k_cmp)
        p_c = masked_softmax(s_c, (cmp_end[None, :] <= t[:, None])[None, :, None, None, :])
        o_c = jnp.einsum('bqhgc,bchd->bqhgd', p_c.astype(dt), v_cmp)
        imp = jnp.einsum('bqhgc,cj->bqhj', p_c, overlap)
        valid = (sel_id[None, :] * SEL_BLOCK <= t[:, None])
        cur = (t // SEL_BLOCK)[:, None]
        forced = (sel_id[None, :] == 0) | (sel_id[None, :] == cur) | (sel_id[None, :] == cur - 1)
        score = jnp.where((forced & valid)[None, :, None, :], FORCE_SCORE,
                          jnp.where(valid[None, :, None, :], imp, -1.0))
        val, idx = lax.top_k(score, top)
        k_g = ks_blk[b_ix, h_ix, idx]
        v_g = vs_blk[b_ix, h_ix, idx]
        pos = idx[..., None] * SEL_BLOCK + jnp.arange(SEL_BLOCK)
        m_s = (pos <= t[None, :, None, None, None]) & (val >= 0)[..., None]
        s_s = jnp.einsum('bqhgd,bqhksd->bqhgks', qq, k_g).reshape(B, Q_BLOCK_2, N_KVH, G, top * SEL_BLOCK)
        p_s = masked_softmax(s_s, m_s.reshape(B, Q_BLOCK_2, N_KVH, 1, top * SEL_BLOCK))
        o_s = jnp.einsum('bqhgn,bqhnd->bqhgd', p_s.astype(dt),
                         v_g.reshape(B, Q_BLOCK_2, N_KVH, top * SEL_BLOCK, HEAD_DIM))
        k_w = lax.dynamic_slice_in_dim(kw_pad, s0, WINDOW + Q_BLOCK_2, axis=1)
        v_w = lax.dynamic_slice_in_dim(vw_pad, s0, WINDOW + Q_BLOCK_2, axis=1)
        kpos = s0 - WINDOW + jnp.arange(WINDOW + Q_BLOCK_2)
        m_w = (kpos[None, :] <= t[:, None]) & (kpos[None, :] > t[:, None] - WINDOW) & (kpos[None, :] >= 0)
        s_w = jnp.einsum('bqhgd,bkhd->bqhgk', qq, k_w)
        p_w = masked_softmax(s_w, m_w[None, :, None, None, :])
        o_w = jnp.einsum('bqhgk,bkhd->bqhgd', p_w.astype(dt), v_w)
        return (gb[:, :, 0, :, :, None] * o_c + gb[:, :, 1, :, :, None] * o_s
                + gb[:, :, 2, :, :, None] * o_w)

    o = lax.map(block, jnp.arange(T // Q_BLOCK_2))
    o = jnp.moveaxis(o, 0, 1).reshape(B, T, N_QH * HEAD_DIM)
    return o @ w_out

def second_inputs(seed: int = 0) -> dict:
    key = jax.random.key(seed)
    k = jax.random.split(key, 20)
    f32 = jnp.float32

    def w(kk, shape, fan_in):
        return jax.random.normal(kk, shape, f32) * fan_in ** -0.5

    def gain(kk, shape):
        return 1.0 + 0.02 * jax.random.normal(kk, shape, f32)

    a_in = 2 * M_HEADS * M_DQK + M_HEADS * M_DV + 2 * M_HEADS + D_MODEL
    b_in = N_QH * HEAD_DIM + 3 * N_QH
    nb = jax.random.normal(k[6], (N_A_LAYERS, 2, M_HEADS), f32)
    return {
        "x": jax.random.normal(k[0], (BATCH, SEQ, D_MODEL), f32),
        "ffn_norm": gain(k[1], (DEPTH, 2, D_MODEL)),
        "ffn_w_in": w(k[2], (DEPTH, 2, D_MODEL, 2 * D_FF), D_MODEL),
        "ffn_w_out": w(k[3], (DEPTH, 2, D_FF, D_MODEL), D_FF),
        "mix_norm": gain(k[4], (DEPTH, D_MODEL)),
        "a_w_in": w(k[5], (N_A_LAYERS, D_MODEL, a_in), D_MODEL),
        "a_b_if": jnp.stack([-1.0 + 0.1 * nb[:, 0], 3.0 + 0.5 * nb[:, 1]], axis=1),
        "a_g_head": gain(k[7], (N_A_LAYERS, M_HEADS, M_DV)),
        "a_w_out": w(k[8], (N_A_LAYERS, M_HEADS * M_DV, D_MODEL), M_HEADS * M_DV),
        "kv_norm": gain(k[9], (D_MODEL,)),
        "kv_w": w(k[10], (D_MODEL, 6 * N_KVH * HEAD_DIM), D_MODEL),
        "cmp_pe": 0.02 * jax.random.normal(k[11], (2, CMP_BLOCK, HEAD_DIM), f32),
        "cmp_w1": w(k[12], (2, CMP_BLOCK * HEAD_DIM, CMP_HIDDEN), CMP_BLOCK * HEAD_DIM),
        "cmp_w2": w(k[13], (2, CMP_HIDDEN, HEAD_DIM), CMP_HIDDEN),
        "k_norm": gain(k[14], (3, HEAD_DIM)),
        "b_w_in": w(k[15], (N_B_LAYERS, D_MODEL, b_in), D_MODEL),
        "b_q_norm": gain(k[16], (N_B_LAYERS, HEAD_DIM)),
        "b_w_out": w(k[17], (N_B_LAYERS, N_QH * HEAD_DIM, D_MODEL), N_QH * HEAD_DIM),
    }

def second_block(x, ffn_norm, ffn_w_in, ffn_w_out, mix_norm, a_w_in, a_b_if, a_g_head, a_w_out,
              kv_norm, kv_w, cmp_pe, cmp_w1, cmp_w2, k_norm, b_w_in, b_q_norm, b_w_out):
    h = x
    kv = None
    for layer in range(DEPTH):
        h = h + 0.5 * swiglu_2(rmsnorm(h, ffn_norm[layer, 0]), ffn_w_in[layer, 0], ffn_w_out[layer, 0])
        hn = rmsnorm(h, mix_norm[layer])
        if layer < N_A_LAYERS:
            h = h + mlstm_mixer(hn, a_w_in[layer], a_b_if[layer], a_g_head[layer], a_w_out[layer])
        else:
            j = layer - N_A_LAYERS
            h = h + nsa_mixer(hn, kv, b_w_in[j], b_q_norm[j], b_w_out[j])
        h = h + 0.5 * swiglu_2(rmsnorm(h, ffn_norm[layer, 1]), ffn_w_in[layer, 1], ffn_w_out[layer, 1])
        if layer == N_A_LAYERS - 1:
            kv = nsa_shared_kv(h, kv_norm, kv_w, cmp_pe, cmp_w1, cmp_w2, k_norm)
    return h


def setup_inputs(seed=0):
    out = dict(first_inputs(seed))
    for name, value in second_inputs(seed + 1).items():
        if name != "x":
            out[name + "_2"] = value
    return out


def reference(
    x, positions, norm_ffn, norm_mix, norm_final, ffn_w_gate, ffn_w_up, ffn_w_down, ab_w_in,
    ab_b_forget, pool_w, pool_scale, ab_w_out, mla_w_in, mla_q_norm, mla_kv_norm, mla_w_q_b,
    mla_w_kv_b, mla_w_out, ffn_norm_2, ffn_w_in_2, ffn_w_out_2, mix_norm_2, a_w_in_2, a_b_if_2,
    a_g_head_2, a_w_out_2, kv_norm_2, kv_w_2, cmp_pe_2, cmp_w1_2, cmp_w2_2, k_norm_2, b_w_in_2,
    b_q_norm_2, b_w_out_2,
):
    x = first_block(
        x, positions, norm_ffn, norm_mix, norm_final, ffn_w_gate, ffn_w_up, ffn_w_down, ab_w_in,
        ab_b_forget, pool_w, pool_scale, ab_w_out, mla_w_in, mla_q_norm, mla_kv_norm, mla_w_q_b,
        mla_w_kv_b, mla_w_out,
    )
    return second_block(
        x, ffn_norm_2, ffn_w_in_2, ffn_w_out_2, mix_norm_2, a_w_in_2, a_b_if_2, a_g_head_2,
        a_w_out_2, kv_norm_2, kv_w_2, cmp_pe_2, cmp_w1_2, cmp_w2_2, k_norm_2, b_w_in_2,
        b_q_norm_2, b_w_out_2,
    )


_drawn_inputs = setup_inputs


def setup_inputs(seed=0):
    import zlib

    import numpy as np

    out = dict(_drawn_inputs(seed))
    spreads = {}
    factors = {'mla_q_norm': 6.131,
     'mla_kv_norm': 4.02,
     'ffn_norm_2': 3.245,
     'a_g_head_2': 5.45,
     'kv_norm_2': 8.0,
     'cmp_pe_2': 8.0,
     'k_norm_2': 8.0,
     'b_q_norm_2': 8.0}
    for name, (base, spread) in spreads.items():
        noise = np.random.default_rng([zlib.crc32(name.encode()), seed]).standard_normal(out[name].shape)
        drawn = base * np.exp(spread * noise) if base else spread * noise
        out[name] = __import__('jax').numpy.asarray(drawn.astype(out[name].dtype))
    for name, factor in factors.items():
        out[name] = (out[name] * factor).astype(out[name].dtype)
    return out
```

```python
from contextlib import ExitStack

import numpy as np

import concourse.bass as bass
from concourse import mybir

F32 = mybir.dt.float32
F32R = mybir.dt.float32r
I32 = mybir.dt.int32
ALU = mybir.AluOpType
ACT = mybir.ActivationFunctionType
AX = mybir.AxisListType

P = 128
S = 256
NT = S // P
D = 1024
KC = D // P
F = 2816
EPS = 1e-6
NEG = -1e30

FOX_H, FOX_D = 8, 64
MLA_H, NOPE, ROPE, MLA_V = 16, 64, 32, 64
QK = NOPE + ROPE
Q_LORA, KV_LORA = 256, 128
MLA_IN = Q_LORA + KV_LORA + ROPE
ML_H, ML_DK, ML_DV = 8, 64, 128
NQ, NKV, HD = 16, 4, 64
CMP_BLOCK, CMP_STRIDE, CMP_HID = 32, 16, 256
NCMP = (S - CMP_BLOCK) // CMP_STRIDE + 1
CP = 32
POOL_W = (2, 4, 8, 16)
PADT = 16

FFN_BLOCKS = F // 256
FT = 2 * FFN_BLOCKS
LOOPS = (FT - 2) // 4
TRI = 3 * P

CONST = {}
_at = 0
for _name, _n in (("ident", P), ("tri", S), ("causal", TRI + 2 * CP), ("chunk64", TRI), ("cmp_row_ok", 2),
                  ("inv_count", 4 * PADT), ("head_row", FOX_H * P), ("inv_freq", ROPE // 2), ("neg_half", 32)):
    CONST[_name] = (_at, _n)
    _at += _n
NCONST = _at


def shape_constants():
    c = np.zeros((P, NCONST), np.float32)

    def put(name, a):
        at, n = CONST[name]
        c[:a.shape[0], at:at + n] = a.reshape(a.shape[0], n)

    r = np.arange(P)
    put("ident", np.eye(P, dtype=np.float32))
    put("tri", (r[:, None] <= np.arange(S)[None, :]).astype(np.float32))
    q1, keys = P + r, np.arange(S)
    blocks = lambda g: np.concatenate([np.where(r[None, :] // g <= r[:, None] // g, 0.0, NEG),
                                       np.where(keys[None, :] // g <= q1[:, None] // g, 0.0, NEG)], axis=1)
    ends = np.arange(CP) * CMP_STRIDE + CMP_BLOCK - 1
    real = np.arange(CP) < NCMP
    cmp = [np.where(real[None, :] & (ends[None, :] <= t[:, None]), 0.0, NEG) for t in (r, q1)]
    put("causal", np.concatenate([blocks(1), *cmp], axis=1).astype(np.float32))
    put("chunk64", blocks(64).astype(np.float32))
    put("cmp_row_ok", np.stack([(t >= CMP_BLOCK - 1) for t in (r, q1)], axis=1).astype(np.float32))
    inv = np.stack([1.0 / np.minimum(np.arange(PADT) + 1, w) for w in POOL_W]).astype(np.float32)
    put("inv_count", np.broadcast_to(inv[None], (P, 4, PADT)))
    put("head_row", np.stack([np.repeat(np.arange(FOX_H) == h, P) for h in range(FOX_H)]).astype(np.float32))
    freq = np.float32(10000.0) ** (-np.arange(0, ROPE, 2, dtype=np.float32) / np.float32(ROPE))
    put("inv_freq", np.broadcast_to(freq.astype(np.float32)[None], (P, ROPE // 2)))
    put("neg_half", np.full((P, 32), -0.5, np.float32))
    return c


GAIN_ROWS = {}
_at = 0
for _name, _n in (("norm_ffn", 32), ("norm_mix", 16), ("ffn_norm_2", 32), ("mix_norm_2", 16), ("kv_norm_2", 8),
                  ("mla_q_norm", 2), ("mla_kv_norm", 1), ("pool_scale", 4), ("a_g_head_2", 8), ("k_norm_2", 3),
                  ("b_q_norm_2", 1)):
    GAIN_ROWS[_name] = (_at, _n)
    _at += _n
NGAIN = _at

KINDS = (0, 1, 2)
"""The stream of weights: for every block its three units, each (name, how it is cut, half's shape)."""


def unit(src, cut, half):
    return dict(src=src, cut=cut, half=half)


def mixer_units(W):
    def cols(w, c0):
        return unit(w[:, c0:c0 + 256].rearrange("(c p) n -> p c n", p=P), "cols", (KC, P))

    def rows(w, k0, nk, c0, n):
        return unit(w[k0 * P:(k0 + nk) * P, c0:c0 + n].rearrange("(c p) n -> p c n", p=P), "rows", (nk // 2, n))

    def wide(w, n0, n):
        r = w.shape[0] // P
        return unit(w[:, n0:n0 + n].rearrange("(c p) n -> p c n", p=P), "cols", (r, n // 2))

    ab, abo = W["ab_w_in"], W["ab_w_out"]
    o = lambda w, i: rows(w, 2 * i, 2, 0, D)
    fox = [[cols(ab, 0), cols(ab, 256), cols(ab, 512)], [cols(ab, 768), cols(ab, 1024), cols(ab, 1280)],
           [rows(ab, 0, 4, 1536, 512), rows(ab, 4, 4, 1536, 512), o(abo, 0)], [o(abo, 1), o(abo, 2), o(abo, 3)]]
    mi, qb, kvb, mo = W["mla_w_in"], W["mla_w_q_b"], W["mla_w_kv_b"], W["mla_w_out"]
    last_q = unit(qb[:, 1024:1536].rearrange("(c p) n -> p c n", p=P), "one", (2, 512))
    mla = [[rows(mi, 0, 4, 0, MLA_IN), rows(mi, 4, 4, 0, MLA_IN), wide(qb, 0, 1024)],
           [last_q, wide(kvb, 0, 2048), o(mo, 0)], [o(mo, 1), o(mo, 2), o(mo, 3)]]
    a, ao = W["a_w_in_2"], W["a_w_out_2"]
    v = lambda i: rows(a, 2 * i, 2, 1024, D)
    og = lambda i: cols(a, 2064 + 256 * i)
    mls = [[cols(a, 0), cols(a, 256), cols(a, 512)], [cols(a, 768), v(0), v(1)], [v(2), v(3), og(0)],
           [og(1), og(2), og(3)], [o(ao, 0), o(ao, 1), o(ao, 2)], [o(ao, 3), None, None]]
    kw, w1 = W["kv_w_2"], W["cmp_w1_2"]
    g = lambda i, half: rows(kw, 4 * half, 4, 512 * i, 512)
    c1 = lambda kind, half: rows(w1[kind], 8 * half, 8, 0, CMP_HID)
    kv = [[g(0, 0), g(0, 1), g(1, 0)], [g(1, 1), g(2, 0), g(2, 1)], [c1(0, 0), c1(0, 1), c1(1, 0)],
          [c1(1, 1), None, None]]
    b, bo = W["b_w_in_2"], W["b_w_out_2"]
    q = lambda i: rows(b, 2 * i, 2, 0, D)
    nsa = [[q(0), q(1), q(2)], [q(3), o(bo, 0), o(bo, 1)], [o(bo, 2), o(bo, 3), None]]
    return dict(fox=fox, mla=mla, mlstm=mls, kv=kv, nsa=nsa)


PHASES = ("ffn0", "fox", "ffn1", "ffn2", "mla", "ffn3", "ffn4", "mlstm", "ffn5", "kv", "ffn6", "nsa", "ffn7")


class Stream:

    def __init__(self, units):
        self.first, self.blocks = {}, []
        for name in PHASES:
            self.first[name] = 2 * len(self.blocks)
            self.blocks += [("ffn",) * 3] * FFN_BLOCKS if name.startswith("ffn") else units[name]
        self.tiles = 2 * len(self.blocks)
        self.count, self.slot_last, self.landing, self.raw_last = {}, {}, {}, {}
        for u in KINDS:
            n, last, raw, raw_before = 0, {}, [0, 0], [0, 0]
            for b, block in enumerate(self.blocks):
                x = block[u]
                if x is not None:
                    raw[b % 2] += 1
                    self.landing[b, u] = 16 * raw[b % 2]
                    self.raw_last[b, u] = raw_before[b % 2]
                for t in (0, 1):
                    if x is None or (t == 1 and x != "ffn" and x["cut"] == "one"):
                        continue
                    n += 1
                    self.count[2 * b + t, u] = n
                    self.slot_last[2 * b + t, u] = last.get(t, 0)
                    last[t] = n
                if x is not None:
                    raw_before[b % 2] = n

    def real(self, tile, u):
        return (tile, u) in self.count

CHUNKS = (0, 2, 1, 3, 4, 6, 5, 7)

NORMS = ("ffn0", "fox", "ffn1", "ffn2", "mla", "ffn3", "final", "ffn4", "mlstm", "ffn5", "kv", "ffn6", "nsa", "ffn7")
NORM = {name: n for n, name in enumerate(NORMS)}
TRANSPOSED = {name: n for n, name in enumerate(x for x in NORMS if x != "final")}
RESIDUAL = {name: n for n, name in enumerate(x for x in PHASES if x != "kv")}
READY = {}
_at = 0
for _name in NORMS:
    READY[_name] = (_at - 2, _at) if _at else (0, 0)
    if _name == "final":
        _at += 2
        READY["after_final"] = (_at - 1, _at)
    elif _name != "kv":
        _at += 4
READY["ffn4"] = READY["after_final"]
READY["out"] = (_at - 2, _at)

SMALL = {"fox_f": (0, FOX_H), "ml_if": (64, 2 * ML_H), "nsa_g": (192, 3 * NQ)}
NSMALL = 192 + 8 * 48


def blocks_program(nc, W, out):
    units = mixer_units(W)
    stream = Stream(units)
    n_of, slot_last, landing, raw_last = stream.count, stream.slot_last, stream.landing, stream.raw_last

    ctx = ExitStack()
    with ctx:
        def sb(name, shape, dt=F32):
            return ctx.enter_context(nc.sbuf_tensor(name, shape, dt))

        def sem(name):
            return ctx.enter_context(nc.semaphore(name))

        raw = sb("raw", [P, 2, 3, 2048])
        wh = sb("wh", [P, 2, 3, 1024], F32R)
        wl = sb("wl", [P, 2, 3, 1024], F32R)
        h = sb("h", [P, NT, D])
        y = sb("y", [P, NT, D])
        xh = sb("xh", [P, KC, S], F32R)
        xl = sb("xl", [P, KC, S], F32R)
        mh = sb("mh", [P, KC, S], F32R)
        ml = sb("ml", [P, KC, S], F32R)
        const = sb("const", [P, NCONST])
        gain = sb("gain", [P, NGAIN])
        pe_col = sb("pe_col", [P, 2 * CMP_BLOCK // 2])
        work = sb("work", [P, 2368])
        hidh = sb("hidh", [P, 2, S], F32R)
        hidl = sb("hidl", [P, 2, S], F32R)
        arena = sb("arena", [P, 8192])
        small_h = sb("small_h", [P, NSMALL], F32R)
        small_l = sb("small_l", [P, NSMALL], F32R)
        w2 = sb("w2", [P, 2, 2, HD])
        st = sb("st", [P, 400])

        A = [ctx.enter_context(nc.psum_tensor(f"A{i}", [P, 512], F32)) for i in range(4)]
        G = [ctx.enter_context(nc.psum_tensor(f"G{i}", [P, 512], F32)) for i in range(2)]
        X = [ctx.enter_context(nc.psum_tensor(f"X{i}", [P, 512], F32)) for i in range(2)]
        TB = [G[0], G[1], X[0], X[1]]

        def cut(buf, at, *shape):
            n = int(np.prod(shape))
            flat = buf[:, at:at + n]
            if len(shape) == 1:
                return flat
            names = "abcd"[:len(shape)]
            return flat.rearrange(f"p ({' '.join(names)}) -> p {' '.join(names)}", **dict(zip(names, shape)))

        def cst(name, *shape):
            at, n = CONST[name]
            return cut(const, at, *(shape or (n,)))

        ident, tri = cst("ident"), cst("tri")

        def gcol(name, i):
            at = GAIN_ROWS[name][0] + i
            return gain[:, at:at + 1]

        _st = [0]

        def stat(*shape):
            at = _st[0]
            _st[0] += int(np.prod(shape))
            assert _st[0] <= 400
            return cut(st, at, *shape)

        yf = y[:].rearrange("p t n -> p (t n)")
        mhf, mlf = mh[:].rearrange("p c n -> p (c n)"), ml[:].rearrange("p c n -> p (c n)")

        sumsq, meansq, rstd = stat(2), stat(2), stat(2)
        zsum, zinv, nmax = stat(3, 4), stat(3, 4), stat(3, 4)
        sig = cut(work, 0, 2, S)
        gated, hid = cut(work, 512, S), cut(work, 768, S)
        L = cut(work, 0, 3, TRI + 2 * CP)
        PT = cut(work, 3 * (TRI + 2 * CP), 2, 512)

        x_landed = [sem(f"x_landed{t}") for t in range(NT)]
        const_landed, rows_landed, small_landed, w2_landed = (sem("const_landed"), sem("rows_landed"),
                                                              sem("small_landed"), sem("w2_landed"))
        gfin_landed = sem("gfin_landed")
        rows_turned, gain_ready = sem("rows_turned"), sem("gain_ready")
        small_hi, small_ready = sem("small_hi"), sem("small_ready")
        raw_landed = [[sem(f"raw{p}{u}_landed") for u in KINDS] for p in (0, 1)]
        hi_done = [sem(f"hi{u}_done") for u in KINDS]
        lo_done = [sem(f"lo{u}_done") for u in KINDS]
        used = [sem(f"used{u}") for u in KINDS]
        h_ready, sq_done, ms_ready, rstd_ready = sem("h_ready"), sem("sq_done"), sem("ms_ready"), sem("rstd_ready")
        y0_ready, y1_ready, turned = sem("y0_ready"), sem("y1_ready"), sem("turned")
        xhi_done, xlo_done, acc_done = sem("xhi_done"), sem("xlo_done"), sem("acc_done")
        sig_ready, hid_steps = sem("sig_ready"), sem("hid_steps")
        stored = sem("stored")
        tlin_out, small_done, row_out = sem("tlin_out"), sem("small_done"), sem("row_out")
        dve_chain, act_chain = sem("dve_chain"), sem("act_chain")
        s_ready, l_done, max_done, e_done, p_done = (sem("s_ready"), sem("l_done"), sem("max_done"), sem("e_done"),
                                                     sem("p_done"))
        pt_ready, pt_out, pv_done = sem("pt_ready"), sem("pt_out"), sem("pv_done")
        o_hi, o_lo, qk_turned, qk_out = sem("o_hi"), sem("o_lo"), sem("qk_turned"), sem("qk_out")
        d_ready = sem("d_ready")
        mx_ready, mx_pow = sem("mx_ready"), sem("mx_pow")
        ev = {}

        def event(name):
            if name not in ev:
                ev[name] = sem(name)
            return ev[name]

        T0 = stream.first
        UP = PADT + S
        fox = dict(u=cut(arena, 0, 4, UP), s1=cut(arena, 1088, 4, UP), s2=cut(arena, 2176, 4, UP),
                   q=cut(arena, 3264, 4, S), k=cut(arena, 4288, 4, S), v=cut(arena, 5312, NT, 512),
                   pw=cut(arena, 6336, 4, P), diff=cut(arena, 6848, 4, S),
                   z=cut(yf, 0, 16), e=cut(yf, 16, 16), logf=cut(yf, 32, 16), F=cut(yf, 48, 16), nz=cut(yf, 64, 16),
                   nFT=cut(yf, 256, S), fix=cut(yf, 512, 64), bf=stat(FOX_H))
        mla = dict(q=cut(arena, 0, NT, MLA_H * QK), k=cut(arena, 3072, NT, MLA_H * QK), v=cut(arena, 6144, NT, D),
                   cin=cut(yf, 0, NT, MLA_IN), cn=cut(yf, 832, NT, Q_LORA + KV_LORA), qkT=cut(yf, 0, 2, 512),
                   cos=stat(NT, 16), sin=stat(NT, 16), ss=stat(NT, 2), ms=stat(NT, 2), rs=stat(NT, 2),
                   rs_in=cut(yf, 1600, NT, 16), rc_in=cut(yf, 1632, NT, 16), ang=cut(yf, 1664, NT, 16),
                   turn=cut(yf, 1696, NT, 16), kr=cut(yf, 1760, NT, ROPE),
                   t1=cut(work, 0, 16, 16), t2=cut(work, 256, 16, 16), pos=stat(2), posi=stat(2))
        mls = dict(q=cut(arena, 0, 4, S), k=cut(arena, 1024, 4, S), v=cut(arena, 2048, NT, D),
                   og=cut(arena, 4096, KC, S), o=cut(arena, 6144, NT, D),
                   z=cut(yf, 0, NT, 16), F=cut(yf, 32, NT, 8), e=cut(yf, 48, NT, 8), logf=cut(yf, 64, NT, 8),
                   nz=cut(yf, 80, NT, 8), R=cut(yf, 256, S), m=cut(yf, 96, NT, 8), den=cut(yf, 112, NT, 8),
                   ssq=cut(yf, 128, NT, 8), a=cut(yf, 144, NT, 8), b=cut(yf, 160, NT, 8), c=cut(yf, 176, NT, 8),
                   d=cut(yf, 192, NT, 8), nf=cut(yf, 208, NT, 8), bif=stat(2 * ML_H), junk=cut(work, 0, P), sc=cut(work, 256, 2, 512))
        nsa = dict(kS=cut(arena, 0, NKV, S), kW=cut(arena, 1024, NKV, S), kC=cut(arena, 2048, NKV, CP),
                   vS=cut(arena, 2176, NT, S), vW=cut(arena, 2688, NT, S), vC=cut(arena, 3200, NT, S),
                   kvc=cut(arena, 3712, NT, 8, P), cT=cut(arena, 5760, 8, S),
                   hk=cut(arena, 7808, 2, 2, 60), kcn=cut(arena, 8048, P),
                   blk=cut(work, 0, 16, 60), ksw=cut(work, 1024, NT, 8, HD),
                   q=cut(arena, 3712, NT, D), g=cut(arena, 5760, NT, 48), qT=cut(arena, 5856, 2, S),
                   ss=stat(32), ms=stat(32), rs=stat(32), sc=stat(2))
        ksw_dup = yf.rearrange("p (t g d n) -> p t g d n", t=NT, g=8, d=2)

        def raw_view(block, u):
            spec = stream.blocks[block][u]
            if spec == "ffn":
                shape = (2, D) if u == 2 else (KC, 256)
            else:
                shape = tuple(spec["src"].shape[1:])
            return raw[:, block % 2, u, 0:shape[0] * shape[1]].rearrange("p (c n) -> p c n", c=shape[0])

        def half_views(tile, u):
            block, t = tile // 2, tile % 2
            spec = stream.blocks[block][u]
            r = raw_view(block, u)
            if spec == "ffn":
                mode, shape = ("rows", (1, D)) if u == 2 else ("cols", (KC, P))
            else:
                mode, shape = spec["cut"], spec["half"]
            if mode == "rows":
                r = r[:, t * shape[0]:(t + 1) * shape[0], :]
            elif mode == "cols":
                r = r[:, :, t * shape[1]:(t + 1) * shape[1]]
            n = shape[0] * shape[1]
            view = lambda b: b[:, t, u, 0:n].rearrange("p (c n) -> p c n", c=shape[0])
            return r, view(wh), view(wl)

        def prepare_hi(tile, u, turn=None):
            if tile >= stream.tiles or not stream.real(tile, u):
                return
            r, hi, _ = half_views(tile, u)
            at = 0 if turn is None else turn
            nc.scalar.wait_ge(raw_landed[tile // 2 % 2][u], landing[tile // 2, u] + 16 * at)
            if slot_last[tile, u]:
                nc.scalar.wait_ge(used[u], slot_last[tile, u] + 4 * at)
            nc.scalar.activation(hi, r, ACT.Copy).then_inc(hi_done[u], 1)

        def prepare_lo(tile, u, turn=None):
            if tile >= stream.tiles or not stream.real(tile, u):
                return
            r, hi, lo = half_views(tile, u)
            at = 0 if turn is None else turn
            nc.vector.wait_ge(hi_done[u], n_of[tile, u] + 4 * at)
            nc.vector.tensor_tensor(lo, r, hi.bitcast(F32), ALU.subtract).then_inc(lo_done[u], 1)

        def mm3(o, sh, sl, rh, rl, start, stop):
            nc.tensor.matmul(o, sh, rh, start=start, stop=False)
            nc.tensor.matmul(o, sh, rl, start=False, stop=False)
            return nc.tensor.matmul(o, sl, rh, start=False, stop=stop)

        WOUT = {
            "fox": [(4, 2, 0), (5, 2, 1), (6, 0, 2), (7, 0, 3), (6, 1, 4), (7, 1, 5), (6, 2, 6), (7, 2, 7)],
            "mla": [(2, 2, 0), (3, 2, 1), (4, 0, 2), (5, 0, 3), (4, 1, 4), (5, 1, 5), (4, 2, 6), (5, 2, 7)],
            "mlstm": [(8, 0, 0), (8, 1, 2), (8, 2, 4), (9, 0, 1), (9, 1, 3), (9, 2, 5), (10, 0, 6), (11, 0, 7)],
            "nsa": [(2, 1, 0), (3, 1, 1), (2, 2, 2), (3, 2, 3), (4, 0, 4), (5, 0, 5), (4, 1, 6), (5, 1, 7)],
        }
        TLIN = {
            "fox": [(0, 0, "u", 0), (0, 1, "u", 2), (0, 2, "q", 0), (1, 0, "u", 1), (1, 1, "u", 3), (1, 2, "q", 1),
                    (2, 0, "q", 2), (2, 1, "k", 0), (2, 2, "k", 2), (3, 0, "q", 3), (3, 1, "k", 1), (3, 2, "k", 3)],
            "mlstm": [(0, 0, "q", 0), (0, 1, "q", 2), (0, 2, "k", 0), (1, 0, "q", 1), (1, 1, "q", 3), (1, 2, "k", 1),
                      (2, 0, "k", 2), (3, 0, "k", 3), (4, 2, "og", 0), (5, 2, "og", 1), (6, 0, "og", 2),
                      (6, 1, "og", 4), (6, 2, "og", 6), (7, 0, "og", 3), (7, 1, "og", 5), (7, 2, "og", 7)],
        }
        MLA_B = [(0, 2, 0, 0, 2), (1, 2, 0, 0, 2), (2, 0, 0, 0, 2),
                 (2, 1, 0, 2, 1), (2, 1, 1, 2, 1), (3, 1, 0, 2, 1), (3, 1, 1, 2, 1)]
        ROWS = {
            "fox": [(4, 0, 0, 2, 0), (4, 1, 4, 2, 0), (5, 0, 2, 2, 0), (5, 1, 6, 2, 0)],
            "mla": [(0, 0, 0, 2, 0), (0, 1, 4, 2, 0), (1, 0, 2, 2, 0), (1, 1, 6, 2, 0)],
            "mlstm": [(2, 1, 0, 1, 0), (2, 2, 2, 1, 0), (3, 1, 1, 1, 0), (3, 2, 3, 1, 0), (4, 0, 4, 1, 0),
                      (4, 1, 6, 1, 0), (5, 0, 5, 1, 0), (5, 1, 7, 1, 0)],
            "kv": [(0, 0, 0, 2, 0), (0, 1, 4, 2, 0), (0, 2, 0, 2, 1), (1, 0, 2, 2, 0), (1, 1, 6, 2, 0), (1, 2, 2, 2, 1),
                   (2, 0, 4, 2, 1), (2, 1, 0, 2, 2), (2, 2, 4, 2, 2), (3, 0, 6, 2, 1), (3, 1, 2, 2, 2),
                   (3, 2, 6, 2, 2)],
            "nsa": [(0, 0, 0, 1, 0), (0, 1, 2, 1, 0), (0, 2, 4, 1, 0), (1, 0, 1, 1, 0), (1, 1, 3, 1, 0), (1, 2, 5, 1, 0),
                    (2, 0, 6, 1, 0), (3, 0, 7, 1, 0)],
        }

        def wait_half(eng, name, tile, u):
            eng.wait_ge(used[u], n_of[T0[name] + tile, u])

        def wait_rows(eng, name, g=0):
            tile, u = [e[:2] for e in ROWS[name] if e[4] == g][-1]
            wait_half(eng, name, tile, u)

        def wait_latent(eng, q):
            ends = [(g < 3 or w0 == 1) and i == 1 for g, (_, _, w0, _, _) in enumerate(MLA_B) for i in range(NT)]
            if ends[q]:
                wait_half(eng, "mla", *MLA_B[q // 2][:2])
            else:
                eng.wait_ge(event("mla_b_done"), q + 1 - sum(ends[:q]))

        block = ctx.enter_context(nc.Block())

        @block.sync
        def _(sp):
            x_tiles = W["x"].rearrange("b (t p) n -> (b t) p n", p=P)
            for t in range(NT):
                sp.dma_start(h[:, t, :], x_tiles[t]).then_inc(x_landed[t], 16)

            def load(block_no, u, src, turn=None):
                at = 0 if turn is None else turn
                if raw_last[block_no, u]:
                    sp.wait_ge(lo_done[u], raw_last[block_no, u] + 4 * at)
                sp.dma_start(raw_view(block_no, u), src).then_inc(raw_landed[block_no % 2][u], 16)

            def ffn_block(gate, up, down, base, b, turn=None):
                c0 = 256 * b if turn is None else 512 * turn + 256 * b
                for u, w in ((0, gate), (1, up)):
                    load(base + b, u, w.rearrange("(c p) n -> p c n", p=P)[:, :, bass.ds(c0, 256)], turn)
                load(base + b, 2, down[bass.ds(c0, 256), :].rearrange("(t p) n -> p t n", p=P), turn)

            for name in PHASES:
                base = T0[name] // 2
                if name.startswith("ffn"):
                    f = int(name[3:])
                    if f < 4:
                        gate, up, down = (W[k][f // 2, f % 2] for k in ("ffn_w_gate", "ffn_w_up", "ffn_w_down"))
                    else:
                        w_in = W["ffn_w_in_2"][(f - 4) // 2, f % 2]
                        gate, up, down = w_in[:, 0:F], w_in[:, F:2 * F], W["ffn_w_out_2"][(f - 4) // 2, f % 2]
                    for b in range(3):
                        ffn_block(gate, up, down, base, b)
                    with sp.Fori(0, (FFN_BLOCKS - 3) // 2) as m:
                        for b in (3, 4):
                            ffn_block(gate, up, down, base, b, m)
                else:
                    for b, blk in enumerate(units[name]):
                        for u in KINDS:
                            if blk[u] is not None:
                                load(base + b, u, blk[u]["src"])

            out_tiles = out.rearrange("b (t p) n -> (b t) p n", p=P)
            for t in range(NT):
                sp.wait_ge(h_ready, READY["out"][t])
                sp.dma_start(out_tiles[t], h[:, t, :]).then_inc(stored, 16)
            sp.wait_ge(stored, 16 * NT)

        @block.gpsimd
        def _(pool):
            def row(dram, n):
                return dram.rearrange("(a n) -> a n", a=1).to_broadcast([P, n])

            at = 0
            rows = yf[:, 0:P]
            for name in GAIN_ROWS:
                first, n = GAIN_ROWS[name]
                if name in ("k_norm_2", "b_q_norm_2"):
                    for d in (0, HD):
                        pool.dma_start(y[first:first + n, 0, d:d + HD], W[name]).then_inc(rows_landed, 16)
                        at += 16
                else:
                    src = W[name]
                    while len(src.shape) > 2:
                        src = src.rearrange("a b c -> (a b) c") if len(src.shape) == 3 else src
                    if len(src.shape) == 1:
                        src = src.rearrange("(r p) -> r p", p=P)
                    elif src.shape[1] != P:
                        src = src.rearrange("a (r p) -> (a r) p", p=P)
                    pool.dma_start(y[first:first + n, 0, 0:P], src).then_inc(rows_landed, 16)
                    at += 16
            pool.dma_start(y[0:32, 0, P:2 * P], W["cmp_pe_2"].rearrange("k (j e) d -> (k j) (e d)", e=2)
                           ).then_inc(rows_landed, 16)
            at += 16
            assert at == ROWS_COUNT
            for name, src in (("fox_f", W["ab_w_in"][:, 2048:2056]), ("ml_if", W["a_w_in_2"][:, 2048:2064]),
                              ("nsa_g", W["b_w_in_2"][:, NQ * HD:NQ * HD + 3 * NQ])):
                c0, n = SMALL[name]
                pool.dma_start(y[:, 1, c0:c0 + KC * n].rearrange("p (c n) -> p c n", n=n),
                               src.rearrange("(c p) n -> p c n", p=P)).then_inc(small_landed, 16)
            pool.dma_start(fox["bf"], row(W["ab_b_forget"], FOX_H)).then_inc(small_landed, 16)
            pool.dma_start(mls["bif"], row(W["a_b_if_2"], 2 * ML_H)).then_inc(small_landed, 16)
            pool.dma_start(fox["pw"], W["pool_w"].rearrange("g p n -> p g n")).then_inc(small_landed, 16)
            pool.dma_start(w2[:], W["cmp_w2_2"].rearrange("k (c p) n -> p k c n", p=P)).then_inc(w2_landed, 16)
            pool.dma_start(mla["posi"].bitcast(I32), W["positions"].rearrange("b (t p) -> p (b t)", p=P), allow_slow_non_contiguous=True
                           ).then_inc(w2_landed, 16)

            def power(o, a, n, wait, count, done):
                pool.wait_ge(wait, count)
                nc.gpsimd.tensor_tensor(o, a, cst("neg_half")[0:a.shape[0], 0:n], ALU.pow).then_inc(done, 1)

            pool.wait_ge(const_landed, 16)
            for n, name in enumerate(NORMS):
                if name == "final":
                    pool.wait_ge(h_ready, READY["ffn3"][1])
                    pool.dma_start(arena[:, 0:D], row(W["norm_final"], D)).then_inc(gfin_landed, 16)
                for t in range(NT):
                    power(rstd[:, t:t + 1], meansq[:, t:t + 1], 1, ms_ready, NT * n + t + 1, rstd_ready)
                if name == "mla":
                    power(mla["rs"].rearrange("p a b -> p (a b)"), mla["ms"].rearrange("p a b -> p (a b)"), 4, mx_ready, 1, mx_pow)
                if name == "mlstm":
                    power(cut(yf, 192, 16), cut(yf, 144, 16), 16, mx_ready, 2, mx_pow)
                if name == "kv":
                    power(nsa["rs"][:, 0:16], nsa["ms"][:, 0:16], 16, mx_ready, 3, mx_pow)
                    power(nsa["rs"][0:60, 16:17], nsa["ms"][0:60, 16:17], 1, mx_ready, 4, mx_pow)
                if name == "nsa":
                    power(nsa["rs"], nsa["ms"], 32, mx_ready, 5, mx_pow)

        @block.tensor
        def _(pe):
            mm = nc.tensor.matmul

            def turn_norm(name):
                k = TRANSPOSED[name]
                n = NORM[name]
                if k == 0:
                    pe.wait_ge(const_landed, 16)
                    pe.wait_ge(gain_ready, 1)
                for t in range(NT):
                    pe.wait_ge((y0_ready, y1_ready)[t], k + 1)
                    for b in range(4):
                        for i in range(2):
                            c = 2 * b + i
                            last = nc.tensor.transpose(TB[b][:, i * S + t * P:i * S + (t + 1) * P],
                                                       y[:, t, c * P:(c + 1) * P], ident)
                        if t == 1:
                            last.then_inc(turned, 1)

            def wait_chunk(name, i):
                pe.wait_ge(xlo_done, KC * TRANSPOSED[name] + i + 1)

            def ffn(name):
                f, base = int(name[3:]), T0[name]

                def gate_up(k, turn=None, first=False):
                    at = 0 if turn is None else 4 * turn
                    t = base + k
                    bank = G[k % 2]
                    if first:
                        wait_chunk(name, 2)
                    elif k == 1:
                        wait_chunk(name, 7)
                    if k >= 2:
                        pe.wait_ge(hid_steps, 4 * (FT * f + k - 1) + 4 * at)
                    for u in (0, 1):
                        _, sh, sl = half_views(t, u)
                        pe.wait_ge(lo_done[u], n_of[t, u] + at)
                        for i, c in enumerate(CHUNKS):
                            if first and u == 0:
                                wait_chunk(name, i)
                            last = mm3(bank[:, u * S:(u + 1) * S], sh[:, c, :], sl[:, c, :], xh[:, c, :], xl[:, c, :],
                                       i == 0, i == KC - 1)
                        last.then_inc(used[u], 1)

                def down(k, turn=None, start=False, stop=False):
                    at = 0 if turn is None else 4 * turn
                    t = base + k
                    _, sh, sl = half_views(t, 2)
                    pe.wait_ge(lo_done[2], n_of[t, 2] + at)
                    pe.wait_ge(hid_steps, 4 * (FT * f + k + 1) + 4 * at)
                    for i in range(NT):
                        for n in range(2):
                            tok, col = slice(i * P, (i + 1) * P), slice(n * 512, (n + 1) * 512)
                            last = mm3(A[2 * i + n][:, :], hidh[:, k % 2, tok], hidl[:, k % 2, tok], sh[:, 0, col],
                                       sl[:, 0, col], start, stop)
                            if stop and 2 * i + n < 3:
                                last.then_inc(acc_done, 1)
                    last.then_inc(used[2], 1)

                gate_up(0, first=True)
                gate_up(1)
                down(0, start=True)
                with pe.Fori(0, LOOPS) as m:
                    for k in range(2, 6):
                        gate_up(k, m)
                        down(k - 1, m)
                down(FT - 1, stop=True)

            tl = [0]

            def tlin(name, entry, firsts):
                tile, u, _, _ = entry
                t = T0[name] + tile
                _, sh, sl = half_views(t, u)
                q = tl[0]
                tl[0] += 1
                if firsts:
                    wait_chunk(name, 2)
                elif q >= 4:
                    pe.wait_ge(tlin_out, q - 3)
                pe.wait_ge(lo_done[u], n_of[t, u])
                for i, c in enumerate(CHUNKS):
                    if firsts:
                        wait_chunk(name, i)
                    last = mm3(TB[q % 4][:, 0:S], sh[:, c, :], sl[:, c, :], xh[:, c, :], xl[:, c, :], i == 0, i == KC - 1)
                last.then_inc(used[u], 1)

            def rows(name, entry, banks, seen, total):
                tile, u, c0, nch, g = entry
                t = T0[name] + tile
                _, sh, sl = half_views(t, u)
                pe.wait_ge(lo_done[u], n_of[t, u])
                n = sh.shape[2]
                for j in range(nch):
                    c = c0 + j
                    start, stop = seen[g] == 0, seen[g] == total - 1
                    for i in range(NT):
                        for w0 in range(0, n, 512):
                            w1 = min(w0 + 512, n)
                            tok = slice(i * P, (i + 1) * P)
                            last = mm3(banks[g][i][w0 // 512][:, 0:w1 - w0], xh[:, c, tok], xl[:, c, tok],
                                       sh[:, j, w0:w1], sl[:, j, w0:w1], start, stop)
                    seen[g] += 1
                last.then_inc(used[u], 1)

            def small(name, key, bank_cols):
                c0, n = SMALL[key]
                pe.wait_ge(small_ready, 1)
                sh = small_h[:, c0:c0 + KC * n].rearrange("p (c n) -> p c n", n=n)
                sl = small_l[:, c0:c0 + KC * n].rearrange("p (c n) -> p c n", n=n)
                for i in range(NT):
                    for c in range(KC):
                        tok = slice(i * P, (i + 1) * P)
                        last = mm3(bank_cols(i), xh[:, c, tok], xl[:, c, tok], sh[:, c, :], sl[:, c, :], c == 0,
                                   c == KC - 1)
                return last

            def w_out(name):
                for i, (tile, u, c) in enumerate(WOUT[name]):
                    t = T0[name] + tile
                    _, sh, sl = half_views(t, u)
                    pe.wait_ge(lo_done[u], n_of[t, u])
                    if i == 0:
                        pe.wait_ge(o_lo, o_count[name])
                    for j in range(NT):
                        for n in range(2):
                            tok, col = slice(j * P, (j + 1) * P), slice(n * 512, (n + 1) * 512)
                            last = mm3(A[2 * j + n][:, :], mh[:, c, tok], ml[:, c, tok], sh[:, 0, col], sl[:, 0, col],
                                       i == 0, i == 7)
                            if i == 7 and 2 * j + n < 3:
                                last.then_inc(acc_done, 1)
                    last.then_inc(used[u], 1)

            def attend(base, n, scores, values, before=None):
                for i in range(n + 2):
                    if i < n:
                        if before:
                            before(i)
                        if base + i >= 2:
                            pe.wait_ge(l_done, base + i - 1)
                        scores(i).then_inc(s_ready, 1)
                    if 1 <= i <= n:
                        j = i - 1
                        pe.wait_ge(p_done, base + j + 1)
                        if base + j >= 2:
                            pe.wait_ge(pt_out, base + j - 1)
                        bank, src = X[j % 2], L[:, j % 3, :]
                        for b in range(3):
                            last = nc.tensor.transpose(bank[:, b * P:(b + 1) * P], src[:, b * P:(b + 1) * P], ident)
                        if n == 2 * NQ and j % 2 == 0:
                            last = nc.tensor.transpose(bank[0:2 * CP, TRI:TRI + P], src[:, TRI:TRI + 2 * CP], ident)
                        last.then_inc(pt_ready, 1)
                    if i >= 2:
                        pe.wait_ge(pt_out, base + i - 1)
                        values(i - 2).then_inc(pv_done, 1)

            def pv(o, v, j, dv0, start=True, stop=True):
                mm(o, v(0), PT[:, j % 2, 0:S], start=start, stop=False)
                return mm(o[:, P:S], v(1), PT[:, j % 2, S:TRI], start=False, stop=stop)

            pe.wait_ge(const_landed, 16)
            pe.wait_ge(rows_landed, ROWS_COUNT)
            nc.tensor.transpose(G[0][:, 0:NGAIN], y[0:NGAIN, 0, 0:P], ident[0:NGAIN, 0:NGAIN])
            nc.tensor.transpose(G[0][:, P:P + 32], y[0:32, 0, P:2 * P], ident[0:32, 0:32]).then_inc(rows_turned, 1)

            def fox_mixer():
                turn_norm("fox")
                for i, e in enumerate(TLIN["fox"]):
                    tlin("fox", e, i == 0)
                seen = [0]
                for e in ROWS["fox"]:
                    rows("fox", e, [[[A[0]], [A[1]]]], seen, KC)
                small("fox", "fox_f", lambda i: A[2][:, 8 * i:8 * i + 8]).then_inc(small_done, 1)
                for g in range(4):
                    pe.wait_ge(tlin_out, tl[0] - 3 + g)
                    pe.wait_ge(event("fox_diff"), 1)
                    pe.wait_ge(small_landed, SMALL_COUNT)
                    mm(TB[g][:, 0:S], fox["pw"][:, g, :], fox["diff"][:, g, :], start=True, stop=True
                       ).then_inc(event("fox_pooled"), 1)
                pe.wait_ge(event("fox_logf"), 1)
                running_sums(fox["logf"].rearrange("p (t n) -> p t n", t=NT), A[2][:, 16:32], A[3][0:8, 0:S],
                             event("fox_sums"))
                pe.wait_ge(event("fox_sums_out"), 2)
                pe.wait_ge(o_lo, 4)

                def scores(i):
                    half = slice(HD * (i % 2), HD * (i % 2 + 1))
                    q, k, bank = fox["q"][half, i // 2, :], fox["k"][half, i // 2, :], G[i % 2]
                    row = cst("head_row", FOX_H, P)[0:8, i, :]
                    mm(bank[:, 0:P], row, fox["nFT"][0:8, 0:P], start=True, stop=False)
                    mm(bank[:, 0:P], q[:, 0:P], k[:, 0:P], start=False, stop=True)
                    mm(bank[:, P:TRI], row, fox["nFT"][0:8, 0:S], start=True, stop=False)
                    return mm(bank[:, P:TRI], q[:, P:S], k[:, 0:S], start=False, stop=True)

                def values(i):
                    if i % 2 == 0 and i >= 4:
                        pe.wait_ge(o_lo, 4 + (i - 4) // 2 + 1)
                    half = slice(HD * (i % 2), HD * (i % 2 + 1))
                    return pv(A[i // 2 % 2][half, 0:S], lambda kt: fox["v"][:, kt, HD * i:HD * (i + 1)], i, HD)

                attend(STEPS["fox"], FOX_H, scores, values)
                w_out("fox")

            def running_sums(logf, by_token, by_head, done, extra=None):
                mm(by_token[:, 0:8], tri[:, 0:P], logf[:, 0, 0:8], start=True, stop=True)
                mm(by_token[:, 8:16], tri[:, P:S], logf[:, 0, 0:8], start=True, stop=False)
                mm(by_token[:, 8:16], tri[:, 0:P], logf[:, 1, 0:8], start=False, stop=True)
                mm(by_head[:, 0:S], logf[:, 0, 0:8], tri, start=True, stop=False)
                mm(by_head[:, P:S], logf[:, 1, 0:8], tri[:, 0:P], start=False, stop=True).then_inc(done, 1)

            def mla_mixer():
                turn_norm("mla")
                wait_chunk("mla", 7)
                seen = [0]
                for e in ROWS["mla"]:
                    rows("mla", e, [[[A[0]], [A[1]]]], seen, KC)
                pe.wait_ge(event("mla_cn"), 2)
                for c in range(3):
                    for t in range(NT):
                        last = nc.tensor.transpose(TB[c][:, t * P:(t + 1) * P],
                                                   mla["cn"][:, t, c * P:(c + 1) * P], ident)
                    last.then_inc(event("mla_c_turned"), 1)
                cTh, cTl = (b[:, 0:3 * S].rearrange("p (c s) -> p c s", c=3) for b in (mhf, mlf))
                pe.wait_ge(event("mla_c_lo"), 3)
                for g, (tile, u, w0, c0, nch) in enumerate(MLA_B):
                    t = T0["mla"] + tile
                    _, sh, sl = half_views(t, u)
                    pe.wait_ge(lo_done[u], n_of[t, u])
                    for i in range(NT):
                        q = 2 * g + i
                        if q >= 4:
                            pe.wait_ge(event("mla_b_out"), q - 3)
                        for j in range(nch):
                            tok, col = slice(i * P, (i + 1) * P), slice(512 * w0, 512 * (w0 + 1))
                            last = mm3(A[q % 4][:, :], cTh[:, c0 + j, tok], cTl[:, c0 + j, tok], sh[:, j, col],
                                       sl[:, j, col], j == 0, j == nch - 1)
                        if i == NT - 1 and (g < 3 or w0 == 1):
                            last.then_inc(used[u], 1)
                        else:
                            last.then_inc(event("mla_b_done"), 1)
                pe.wait_ge(event("mla_b_out"), 14)
                pe.wait_ge(event("mla_roped"), 1)

                def turn_heads(i):
                    if i >= 2:
                        pe.wait_ge(qk_out, i - 1)
                    for b, src in enumerate((mla["q"], mla["q"], mla["k"], mla["k"])):
                        last = nc.tensor.transpose(A[2 + i % 2][0:QK, b * P:(b + 1) * P],
                                                   src[:, b % 2, QK * i:QK * (i + 1)], ident)
                    last.then_inc(qk_turned, 1)

                def scores(i):
                    if i == 0:
                        turn_heads(0)
                    if i + 1 < MLA_H:
                        turn_heads(i + 1)
                    pe.wait_ge(qk_out, i + 1)
                    t, bank = mla["qkT"][0:QK, i % 2, :], G[i % 2]
                    mm(bank[:, 0:P], t[:, 0:P], t[:, S:S + P], start=True, stop=True)
                    return mm(bank[:, P:TRI], t[:, P:S], t[:, S:2 * S], start=True, stop=True)

                def values(i):
                    if i % 2 == 0 and i >= 4:
                        pe.wait_ge(o_lo, o_before["mla"] + (i - 4) // 2 + 1)
                    half = slice(HD * (i % 2), HD * (i % 2 + 1))
                    return pv(A[i // 2 % 2][half, 0:S], lambda kt: mla["v"][:, kt, HD * i:HD * (i + 1)], i, HD)

                attend(STEPS["mla"], MLA_H, scores, values)
                w_out("mla")

            def mlstm_mixer():
                turn_norm("mlstm")
                seen = [0]
                by_tile = sorted([(e[0], e[1], "t", e) for e in TLIN["mlstm"]] +
                                 [(e[0], e[1], "r", e) for e in ROWS["mlstm"]], key=lambda x: x[:2])
                for i, (tile, u, what, e) in enumerate(by_tile):
                    if what == "t":
                        tlin("mlstm", e, i == 0)
                    else:
                        rows("mlstm", e, [[[A[0], A[1]], [A[2], A[3]]]], seen, KC)
                pe.wait_ge(row_out, ROW_OUT["mlstm"])
                small("mlstm", "ml_if", lambda i: A[0][:, 16 * i:16 * i + 16]).then_inc(small_done, 1)
                pe.wait_ge(event("ml_logf"), 1)
                logf = mls["logf"]
                running_sums(logf, A[1][:, 0:16], A[2][0:8, 0:S], event("ml_sums"))
                for t in range(NT):
                    last = nc.tensor.transpose(A[3][0:8, t * P:(t + 1) * P], mls["z"][:, t, 0:8], ident)
                last.then_inc(event("ml_sums"), 1)
                pe.wait_ge(event("ml_rows"), 1)
                pe.wait_ge(tlin_out, tl[0])

                def scores(i):
                    half = slice(ML_DK * (i % 2), ML_DK * (i % 2 + 1))
                    q, k, bank = mls["q"][half, i // 2, :], mls["k"][half, i // 2, :], G[i % 2]
                    row, dbank = cst("head_row", ML_H, P)[0:8, i, :], A[2 + i % 2]
                    mm(dbank[:, 0:P], row, mls["R"][0:8, 0:P], start=True, stop=True)
                    mm(dbank[:, P:TRI], row, mls["R"][0:8, 0:S], start=True, stop=True)
                    mm(bank[:, 0:P], q[:, 0:P], k[:, 0:P], start=True, stop=True)
                    return mm(bank[:, P:TRI], q[:, P:S], k[:, 0:S], start=True, stop=True)

                def before(i):
                    if i >= 2:
                        pe.wait_ge(p_done, STEPS["mlstm"] + i - 1)

                def values(i):
                    if i >= 2:
                        pe.wait_ge(event("ml_o_out"), i - 1)
                    bank, v = A[i % 2], mls["v"][:, :, ML_DV * i:ML_DV * (i + 1)]
                    mm(bank[:, 0:P], PT[:, i % 2, 0:P], v[:, 0, :], start=True, stop=True)
                    mm(bank[:, P:S], PT[:, i % 2, P:S], v[:, 0, :], start=True, stop=False)
                    return mm(bank[:, P:S], PT[:, i % 2, S:TRI], v[:, 1, :], start=False, stop=True)

                attend(STEPS["mlstm"], ML_H, scores, values, before)
                pe.wait_ge(event("ml_y"), 2)
                for b in range(4):
                    for i in range(2):
                        for t in range(NT):
                            c = 2 * b + i
                            last = nc.tensor.transpose(TB[b][:, i * S + t * P:i * S + (t + 1) * P],
                                                       mls["o"][:, t, c * P:(c + 1) * P], ident)
                    last.then_inc(event("ml_turned"), 1)
                w_out("mlstm")

            def kv_stage():
                turn_norm("kv")
                wait_chunk("kv", 7)
                seen = [0, 0, 0]
                banks = [[[A[0]], [A[1]]], [[A[2]], [A[3]]], [[X[0]], [X[1]]]]
                for e in ROWS["kv"]:
                    rows("kv", e, banks, seen, KC)
                pe.wait_ge(event("kv_c_out"), 2)
                pe.wait_ge(row_out, ROW_OUT["kv"])
                turn_banks = [A[0], A[1], A[2], A[3]]
                for b in range(4):
                    for i in range(2):
                        for t in range(NT):
                            last = nc.tensor.transpose(turn_banks[b][:, i * S + t * P:i * S + (t + 1) * P],
                                                       nsa["kvc"][:, t, 2 * b + i, :], ident)
                    last.then_inc(event("kv_c_turned"), 1)
                pe.wait_ge(event("kv_dup"), 2)
                for b, bank in enumerate((X[0], X[1], G[0], G[1])):
                    for i in range(2):
                        for t in range(NT):
                            last = nc.tensor.transpose(bank[:, i * S + t * P:i * S + (t + 1) * P],
                                                       ksw_dup[:, t, 2 * b + i, :, :].rearrange("p d n -> p (d n)"),
                                                       ident)
                    last.then_inc(event("kv_k_turned"), 1)
                pe.wait_ge(event("kv_k_out"), 4)
                pe.wait_ge(event("kv_c_cols"), 4)
                hid_bank = [[G[0], G[1]], [A[0], A[1]]]
                for kind, part in ((0, [(4, 0, 0), (5, 0, 4), (4, 1, 8), (5, 1, 12)]),
                                   (1, [(4, 2, 0), (5, 2, 4), (6, 0, 8), (7, 0, 12)])):
                    pe.wait_ge(event("kv_blk_lo"), kind + 1)
                    bh, bl = (b[:, 960 * kind:960 * (kind + 1)].rearrange("p (j r) -> p j r", r=60) for b in (mhf, mlf))
                    for tile, u, j0 in part:
                        t = T0["kv"] + tile
                        _, sh, sl = half_views(t, u)
                        pe.wait_ge(lo_done[u], n_of[t, u])
                        for j in range(4):
                            for c in range(2):
                                last = mm3(hid_bank[kind][c][:, 0:60], sh[:, j, c * P:(c + 1) * P],
                                           sl[:, j, c * P:(c + 1) * P], bh[:, j0 + j, :], bl[:, j0 + j, :],
                                           j0 + j == 0, j0 + j == 15)
                        last.then_inc(used[u], 1)
                pe.wait_ge(w2_landed, 32)
                pe.wait_ge(event("kv_act"), 1)
                for c in range(2):
                    last = mm(A[2][0:60, 0:HD], nsa["hk"][:, 0, c, :], w2[:, 0, c, :], start=c == 0, stop=c == 1)
                last.then_inc(event("kv_k2"), 1)
                pe.wait_ge(event("kv_act"), 2)
                for at in (0, CP):
                    for g in range(NKV):
                        for c in range(2):
                            last = mm(A[3][at:at + NCMP, HD * g:HD * (g + 1)], nsa["hk"][:, 1, c, NCMP * g:NCMP * (g + 1)],
                                      w2[:, 1, c, :], start=c == 0, stop=c == 1)
                last.then_inc(event("kv_v2"), 1)
                pe.wait_ge(event("kv_kcn"), 1)
                nc.tensor.transpose(X[0][:, 0:60], nsa["kcn"][0:60, :], ident[0:60, 0:60]).then_inc(event("kv_kc"), 1)

            def nsa_mixer():
                turn_norm("nsa")
                wait_chunk("nsa", 7)
                seen = [0]
                for e in ROWS["nsa"]:
                    rows("nsa", e, [[[A[0], A[1]], [A[2], A[3]]]], seen, KC)
                pe.wait_ge(row_out, ROW_OUT["nsa"])
                small("nsa", "nsa_g", lambda i: A[0][:, 48 * i:48 * (i + 1)]).then_inc(small_done, 1)
                pe.wait_ge(event("nsa_q"), 2)
                pe.wait_ge(event("nsa_gates"), 1)

                def turn_pair(p):
                    if p >= 2:
                        pe.wait_ge(qk_out, MLA_H + p - 1)
                    for t in range(NT):
                        last = nc.tensor.transpose(A[2 + p % 2][:, t * P:(t + 1) * P],
                                                   nsa["q"][:, t, P * p:P * (p + 1)], ident)
                    last.then_inc(qk_turned, 1)

                def scores(s):
                    i, odd = s // 2, s % 2
                    if s == 0:
                        turn_pair(0)
                    if s % 4 == 0 and i // 2 + 1 < NQ // 2:
                        turn_pair(i // 2 + 1)
                    if s % 4 == 0:
                        pe.wait_ge(qk_out, MLA_H + i // 2 + 1)
                    half = slice(HD * (i % 2), HD * (i % 2 + 1))
                    q, g, bank = nsa["qT"][half, i // 2 % 2, :], i // 4, G[s % 2]
                    k = (nsa["kS"], nsa["kW"])[odd][half, g, :]
                    mm(bank[:, 0:P], q[:, 0:P], k[:, 0:P], start=True, stop=True)
                    last = mm(bank[:, P:TRI], q[:, P:S], k[:, 0:S], start=True, stop=True)
                    if not odd:
                        for t in range(NT):
                            last = mm(bank[:, TRI + CP * t:TRI + CP * (t + 1)], q[:, t * P:(t + 1) * P],
                                      nsa["kC"][half, g, :], start=True, stop=True)
                    return last

                def values(s):
                    i, odd = s // 2, s % 2
                    if i % 2 == 0 and i >= 4 and not odd:
                        pe.wait_ge(o_lo, o_before["nsa"] + (i - 4) // 2 + 1)
                    half, g = slice(HD * (i % 2), HD * (i % 2 + 1)), i // 4
                    o = A[i // 2 % 2][half, 0:S]
                    v = (nsa["vS"], nsa["vW"])[odd]
                    last = pv(o, lambda kt: v[:, kt, HD * g:HD * (g + 1)], s, HD, start=not odd, stop=bool(odd))
                    if not odd:
                        for t in range(NT):
                            last = mm(o[:, t * P:(t + 1) * P], nsa["vC"][0:2 * CP, t, HD * g:HD * (g + 1)],
                                      PT[0:2 * CP, s % 2, TRI:TRI + P], start=False, stop=False)
                    return last

                pe.wait_ge(event("kv_done"), 3)
                attend(STEPS["nsa"], 2 * NQ, scores, values)
                w_out("nsa")

            mixers = dict(fox=fox_mixer, mla=mla_mixer, mlstm=mlstm_mixer, kv=kv_stage, nsa=nsa_mixer)
            for name in PHASES:
                if name.startswith("ffn"):
                    turn_norm(name)
                    ffn(name)
                else:
                    mixers[name]()

        @block.scalar
        def _(act):
            A_ = nc.scalar.activation
            chain = [0]

            def link(ins):
                chain[0] += 1
                ins.then_inc(act_chain, 1)
                act.wait_ge(act_chain, chain[0])

            act.dma_start(const[:], W["const"]).then_inc(const_landed, 16)

            def prep(name, tile, kinds=KINDS):
                for u in kinds:
                    prepare_hi(T0[name] + tile, u)

            def norm(name):
                n = NORM[name]
                for t in range(NT):
                    if n == 0:
                        act.wait_ge(x_landed[t], 16)
                    else:
                        act.wait_ge(h_ready, READY[name][t])
                    A_(y[:, t, :], h[:, t, :], ACT.Square, accum_out=sumsq[:, t:t + 1]).then_inc(sq_done, 1)
                if name == "final":
                    return
                k = TRANSPOSED[name]
                act.wait_ge(rstd_ready, NT * n + 2)
                act.wait_ge(sq_done, NT * n + 2)
                A_(y[:, 1, :], h[:, 1, :], ACT.Copy, scale=rstd[:, 1:2]).then_inc(y1_ready, 1)
                gains = {"ffn": ("norm_ffn", KC * int(name[3:])) if name[:3] == "ffn" and int(name[3:]) < 4 else
                                ("ffn_norm_2", KC * (int(name[3:]) - 4)) if name[:3] == "ffn" else None,
                         "fox": ("norm_mix", 0), "mla": ("norm_mix", KC), "mls": ("mix_norm_2", 0),
                         "nsa": ("mix_norm_2", KC), "kv": ("kv_norm_2", 0)}[name[:3]]
                for i, c in enumerate(CHUNKS):
                    act.wait_ge(turned, 4 * k + c // 2 + 1)
                    if c % 2:
                        act.wait_ge(xlo_done, KC * k + CHUNKS.index(c - 1) + 1)
                    A_(xh[:, c, :], TB[c // 2][:, c % 2 * S:(c % 2 + 1) * S], ACT.Copy,
                       scale=gcol(gains[0], gains[1] + c)).then_inc(xhi_done, 1)

            def ffn(name):
                f, base = int(name[3:]), T0[name]

                def sigmoid(k, turn=None):
                    at = 0 if turn is None else 4 * turn
                    act.wait_ge(used[1], n_of[base + k, 1] + at)
                    if FT * f + k >= 2:
                        act.wait_ge(hid_steps, 4 * (FT * f + k - 1) + at * 4)
                    elif turn is not None:
                        act.wait_ge(hid_steps, 1 + at * 4)
                    A_(sig[:, k % 2, :], G[k % 2][:, 0:S], ACT.Sigmoid).then_inc(sig_ready, 1)

                prep(name, 1)
                sigmoid(0)
                with act.Fori(0, LOOPS) as m:
                    for k in range(2, 6):
                        prepare_hi(base + k, 0, m)
                        prepare_hi(base + k, 1, m)
                        sigmoid(k - 1, m)
                        prepare_hi(base + k, 2, m)
                prep(name, FT, (0, 1))
                sigmoid(FT - 1)
                prep(name, FT, (2,))

            tl = [0]

            def tlin_evac(name, entry, target, func=ACT.Copy, scale=1.0):
                q = tl[0]
                tl[0] += 1
                wait_half(act, name, *entry[:2])
                A_(target, TB[q % 4][:, 0:S], func, scale=scale).then_inc(tlin_out, 1)

            def softmax(base, n, extra=None, blocks=lambda i: ((0, 0, P), (1, P, TRI)), bias=lambda i: nmax[:, i % 3, :]):
                for i in range(n + 1):
                    if i < n:
                        act.wait_ge(max_done, base + i + 1)
                        for b, c0, c1 in blocks(i):
                            A_(L[:, i % 3, c0:c1], L[:, i % 3, c0:c1], ACT.Exp, bias=bias(i)[:, b:b + 1],
                               accum_out=zsum[:, i % 3, b:b + 1]).then_inc(e_done, 1)
                    if i >= 1:
                        j = i - 1
                        act.wait_ge(pt_ready, base + j + 1)
                        if base + j >= 2:
                            act.wait_ge(pv_done, base + j - 1)
                        w = TRI
                        A_(PT[:, j % 2, 0:w], X[j % 2][:, 0:w], ACT.Copy).then_inc(pt_out, 1)
                    if extra:
                        extra(i)

            def pair_hi(pair, base, heads, last_step):
                act.wait_ge(pv_done, last_step)
                A_(mh[:, pair, :], A[pair % 2][:, 0:S], ACT.Copy).then_inc(o_hi, 1)

            act.wait_ge(rows_turned, 1)
            A_(gain[:], G[0][:, 0:NGAIN], ACT.Copy).then_inc(gain_ready, 1)
            act.wait_ge(gain_ready, 1)
            A_(pe_col[:], G[0][:, P:P + 32], ACT.Copy).then_inc(gain_ready, 1)
            act.wait_ge(small_landed, SMALL_COUNT)
            for i, (c0, n) in enumerate(SMALL.values()):
                A_(small_h[:, c0:c0 + KC * n], y[:, 1, c0:c0 + KC * n], ACT.Copy).then_inc(small_hi, 1)
            prep("ffn0", 0)
            act.wait_ge(small_ready, 1)
            act.wait_ge(gain_ready, 2)

            def fox_mixer():
                norm("fox")
                entries = TLIN["fox"]
                for tile in range(4):
                    prep("fox", tile + 1)
                    for e in entries[3 * tile:3 * tile + 3]:
                        _, _, what, c = e
                        dst = fox[what][:, c, :] if what != "u" else fox["u"][:, c, PADT:]
                        tlin_evac("fox", e, dst, scale=FOX_D ** -0.5 if what == "q" else 1.0)
                prep("fox", 5)
                prep("fox", 6, (0, 1))
                prep("fox", 7, (0, 1))
                wait_rows(act, "fox")
                A_(fox["v"][:, 0, :], A[0][:, :], ACT.Copy)
                A_(fox["v"][:, 1, :], A[1][:, :], ACT.Copy).then_inc(row_out, 1)
                act.wait_ge(event("fox_nz"), 1)
                link(A_(fox["e"], fox["nz"], ACT.Exp))
                A_(fox["e"], fox["e"], ACT.Ln, bias=1.0).then_inc(event("fox_ln"), 1)
                for g in range(4):
                    act.wait_ge(event("fox_pooled"), g + 1)
                    A_(mh[:, g, :], TB[g][:, 0:S], ACT.Copy, scale=gcol("pool_scale", g)).then_inc(o_hi, 1)
                act.wait_ge(event("fox_sums"), 1)
                A_(fox["nFT"][0:8, :], A[3][0:8, 0:S], ACT.Copy, scale=-1.0).then_inc(event("fox_sums_out"), 1)

                def pairs(i):
                    if i >= 4 and i % 2 == 0:
                        p = i // 2 - 2
                        act.wait_ge(pv_done, STEPS["fox"] + 2 * p + 2)
                        A_(mh[:, 4 + p, :], A[p % 2][:, 0:S], ACT.Copy).then_inc(o_hi, 1)
                softmax(STEPS["fox"], FOX_H, pairs)
                act.wait_ge(pv_done, STEPS["fox"] + FOX_H)
                A_(mh[:, 7, :], A[1][:, 0:S], ACT.Copy).then_inc(o_hi, 1)
                prep("fox", 6, (2,))
                prep("fox", 7, (2,))
                prep("fox", 8)

            def mla_mixer():
                norm("mla")
                prep("mla", 1)
                prep("mla", 2, (0, 1))
                wait_rows(act, "mla")
                for t in range(NT):
                    A_(mla["cin"][:, t, :], A[t][:, 0:MLA_IN], ACT.Copy).then_inc(event("mla_cin"), 1)
                act.wait_ge(event("mla_cin"), 2)
                for t in range(NT):
                    for i, (c0, c1) in enumerate(((0, Q_LORA), (Q_LORA, Q_LORA + KV_LORA))):
                        A_(mla["cn"][:, t, c0:c1], mla["cin"][:, t, c0:c1], ACT.Square,
                           accum_out=mla["ss"][:, t, i:i + 1]).then_inc(event("mla_sq"), 1)
                act.wait_ge(event("mla_ang"), 2)
                A_(mla["sin"], mla["rs_in"], ACT.Sin).then_inc(event("mla_cs"), 1)
                A_(mla["cos"], mla["rc_in"], ACT.Sin).then_inc(event("mla_cs"), 1)
                for c in range(3):
                    act.wait_ge(event("mla_c_turned"), c + 1)
                    g = gcol("mla_q_norm", c) if c < 2 else gcol("mla_kv_norm", 0)
                    A_(mhf[:, c * S:(c + 1) * S], TB[c][:, 0:S], ACT.Copy, scale=g).then_inc(event("mla_c_hi"), 1)
                for g in range(7):
                    if g < 3:
                        for t in range(NT):
                            q = 2 * g + t
                            wait_latent(act, q)
                            A_(mla["q"][:, t, 512 * g:512 * (g + 1)], A[q % 4][:, :], ACT.Copy, scale=QK ** -0.5
                               ).then_inc(event("mla_b_out"), 1)
                    else:
                        for t in range(NT):
                            q = 2 * g + t
                            h0 = 4 * (g - 3)
                            wait_latent(act, q)
                            src = A[q % 4][:, :].rearrange("p (h n) -> p h n", h=4)
                            k = mla["k"][:, t, :].rearrange("p (h n) -> p h n", n=QK)[:, h0:h0 + 4, 0:NOPE]
                            v = mla["v"][:, t, :].rearrange("p (h n) -> p h n", n=MLA_V)[:, h0:h0 + 4, :]
                            A_(k, src[:, :, 0:NOPE], ACT.Copy)
                            A_(v, src[:, :, NOPE:], ACT.Copy).then_inc(event("mla_b_out"), 1)
                    if g == 0:
                        prep("mla", 2, (2,))
                        prep("mla", 3)
                    if g == 3:
                        prep("mla", 4, (0,))
                    if g == 5:
                        prep("mla", 4, (1,))
                        prep("mla", 5, (0,))
                act.wait_ge(event("mla_roped"), 1)

                def heads(i):
                    act.wait_ge(qk_turned, i + 1)
                    if i >= 2:
                        act.wait_ge(s_ready, STEPS["mla"] + i - 1)
                    A_(mla["qkT"][0:QK, i % 2, :], A[2 + i % 2][0:QK, :], ACT.Copy).then_inc(qk_out, 1)

                def more(i):
                    if i + 1 < MLA_H:
                        heads(i + 1)
                    if i >= 4 and i % 2 == 0:
                        pair_hi(i // 2 - 2, 0, 0, STEPS["mla"] + i - 2)
                heads(0)
                softmax(STEPS["mla"], MLA_H, more)
                pair_hi(7, 0, 0, STEPS["mla"] + MLA_H)
                prep("mla", 4, (2,))
                prep("mla", 5, (1, 2))
                prep("mla", 6)

            def mlstm_mixer():
                norm("mlstm")
                by = {}
                for e in TLIN["mlstm"]:
                    by.setdefault(e[0], []).append(e)
                for tile in range(8):
                    prep("mlstm", tile + 1)
                    for e in by.get(tile, []):
                        _, _, what, c = e
                        tlin_evac("mlstm", e, mls[what][:, c, :], ACT.Sigmoid if what == "og" else ACT.Copy,
                                  ML_DK ** -0.5 if what == "q" else 1.0)
                    if tile == 5:
                        wait_rows(act, "mlstm")
                        for t in range(NT):
                            for n in range(2):
                                last = A_(mls["v"][:, t, 512 * n:512 * (n + 1)], A[2 * t + n][:, :], ACT.Copy)
                        last.then_inc(row_out, 1)
                prep("mlstm", 9)
                act.wait_ge(event("ml_nz"), 1)
                link(A_(mls["e"], mls["nz"], ACT.Exp))
                A_(mls["e"], mls["e"], ACT.Ln, bias=1.0).then_inc(event("ml_ln"), 1)

                def heads(i):
                    if i >= 2:
                        j = i - 2
                        act.wait_ge(pv_done, STEPS["mlstm"] + j + 1)
                        A_(mls["o"][:, :, ML_DV * j:ML_DV * (j + 1)], A[j % 2][:, 0:S].rearrange("p (t n) -> p t n", t=NT),
                           ACT.Copy).then_inc(event("ml_o_out"), 1)
                softmax(STEPS["mlstm"], ML_H, heads)
                heads(ML_H + 1)
                A_(mls["b"], mls["m"], ACT.Exp, scale=-1.0).then_inc(event("ml_em"), 1)
                act.wait_ge(event("ml_o_out"), ML_H)
                for t in range(NT):
                    for i in range(ML_H):
                        if t + i:
                            act.wait_ge(event("ml_sq"), t * ML_H + i)
                        A_(mls["junk"], mls["o"][:, t, ML_DV * i:ML_DV * (i + 1)], ACT.Square,
                           accum_out=mls["ssq"][:, t, i:i + 1]).then_inc(event("ml_sq"), 1)
                for b in range(4):
                    for i in range(2):
                        c = 2 * b + i
                        act.wait_ge(event("ml_mix"), c + 1)
                        A_(mh[:, c, :], mls["sc"][:, c % 2, 0:S], ACT.Copy).then_inc(o_hi, 1)
                prep("mlstm", 10)
                prep("mlstm", 11)
                prep("mlstm", 12)

            def kv_stage():
                norm("kv")
                for tile in range(1, 4):
                    prep("kv", tile)
                wait_rows(act, "kv", 0)
                for t in range(NT):
                    for d in range(2):
                        last = A_(nsa["kvc"][:, t, :, HD * d:HD * (d + 1)],
                                  A[t][:, :].rearrange("p (g n) -> p g n", n=HD), ACT.Copy)
                    last.then_inc(event("kv_c_out"), 1)
                for br, (banks, v) in enumerate((((A[2], A[3]), nsa["vS"]), ((X[0], X[1]), nsa["vW"]))):
                    wait_rows(act, "kv", 1 + br)
                    for t in range(NT):
                        A_(nsa["ksw"][:, t, 4 * br:4 * br + 4, :], banks[t][:, 0:S].rearrange("p (g n) -> p g n", n=HD),
                           ACT.Copy).then_inc(event("kv_ksw"), 1)
                        last = A_(v[:, t, :], banks[t][:, S:2 * S], ACT.Copy)
                    last.then_inc(row_out, 1)
                prep("kv", 4)
                prep("kv", 5)
                for b in range(4):
                    act.wait_ge(event("kv_c_turned"), b + 1)
                    src = A[b][:, :].rearrange("p (g s) -> p g s", g=2)
                    dst = nsa["cT"][:, 2 * b:2 * b + 2, :]
                    A_(dst[0:HD, :, :], src[0:HD, :, :], ACT.Copy)
                    A_(dst[HD:P, :, 0:S - 1], src[HD:P, :, 1:S], ACT.Copy).then_inc(event("kv_c_cols"), 1)
                for b, bank in enumerate((X[0], X[1], G[0], G[1])):
                    act.wait_ge(event("kv_k_turned"), b + 1)
                    dst = (nsa["kS"], nsa["kW"])[b // 2][:, 2 * (b % 2):2 * (b % 2) + 2, :]
                    A_(dst, bank[:, :].rearrange("p (g s) -> p g s", g=2), ACT.Copy,
                       scale=gcol("k_norm_2", 1 + b // 2)).then_inc(event("kv_k_out"), 1)
                for kind in range(2):
                    act.wait_ge(event("kv_blk"), kind + 1)
                    A_(mhf[:, 960 * kind:960 * (kind + 1)], nsa["blk"].rearrange("p j r -> p (j r)"), ACT.Copy
                       ).then_inc(event("kv_blk_hi"), 1)
                prep("kv", 6)
                for kind in range(2):
                    wait_half(act, "kv", *((5, 1), (7, 0))[kind])
                    bank = [[G[0], G[1]], [A[0], A[1]]][kind]
                    for c in range(2):
                        A_(nsa["hk"][:, kind, c, :], bank[c][:, 0:60], ACT.Sigmoid).then_inc(event("kv_sig"), 1)
                    if kind == 0:
                        prep("kv", 7)
                act.wait_ge(event("kv_k2"), 1)
                A_(nsa["kcn"][0:60, 0:HD], A[2][0:60, 0:HD], ACT.Square, accum_out=nsa["ss"][0:60, 16:17]
                   ).then_inc(event("kv_k2sq"), 1)
                act.wait_ge(event("kv_v2"), 1)
                act.wait_ge(event("kv_zero"), 2)
                for t in range(NT):
                    at = slice(CP * t, CP * t + NCMP)
                    A_(nsa["vC"][at, t, :], A[3][at, 0:S], ACT.Copy).then_inc(event("kv_done"), 1)
                act.wait_ge(event("kv_kc"), 1)
                A_(nsa["kC"][:, :, 0:NCMP], X[0][:, 0:60].rearrange("p (g c) -> p g c", g=NKV), ACT.Copy,
                   scale=gcol("k_norm_2", 0)).then_inc(event("kv_done"), 1)
                prep("kv", 8)

            def nsa_mixer():
                norm("nsa")
                prep("nsa", 1)
                prep("nsa", 2)
                prep("nsa", 3)
                wait_rows(act, "nsa")
                for t in range(NT):
                    for n in range(2):
                        last = A_(nsa["q"][:, t, 512 * n:512 * (n + 1)], A[2 * t + n][:, :], ACT.Copy)
                last.then_inc(row_out, 1)
                prep("nsa", 4, (0,))
                prep("nsa", 5, (0,))
                act.wait_ge(small_done, 3)
                for t in range(NT):
                    last = A_(nsa["g"][:, t, :], A[0][:, 48 * t:48 * (t + 1)], ACT.Sigmoid)
                last.then_inc(event("nsa_gates"), 1)

                def pair(p):
                    act.wait_ge(qk_turned, MLA_H + p + 1)
                    if p >= 2:
                        act.wait_ge(s_ready, STEPS["nsa"] + 4 * (p - 1))
                    A_(nsa["qT"][:, p % 2, :], A[2 + p % 2][:, 0:S], ACT.Copy, scale=nsa["sc"][:, 0:1]).then_inc(qk_out, 1)

                def blocks(s):
                    own = ((0, 0, P), (1, P, TRI))
                    return own if s % 2 else own + ((2, TRI, TRI + CP), (3, TRI + CP, TRI + 2 * CP))
                act.wait_ge(event("nsa_sc"), 1)
                pair(0)
                base = STEPS["nsa"]
                n_e = [0]
                for i in range(2 * NQ + 1):
                    if i < 2 * NQ:
                        act.wait_ge(max_done, base + i + 1)
                        for b, c0, c1 in blocks(i):
                            A_(L[:, i % 3, c0:c1], L[:, i % 3, c0:c1], ACT.Exp, bias=nmax[:, i % 3, b:b + 1],
                               accum_out=zsum[:, i % 3, b:b + 1]).then_inc(e_done, 1)
                    if i >= 1:
                        j = i - 1
                        act.wait_ge(pt_ready, base + j + 1)
                        act.wait_ge(pv_done, base + j - 1)
                        if j % 2 == 0:
                            A_(PT[0:2 * CP, j % 2, TRI:TRI + P], X[j % 2][0:2 * CP, TRI:TRI + P], ACT.Copy
                               ).then_inc(event("nsa_ct_out"), 1)
                        A_(PT[:, j % 2, 0:TRI], X[j % 2][:, 0:TRI], ACT.Copy).then_inc(pt_out, 1)
                    if i % 4 == 0 and i // 4 + 1 < NQ // 2:
                        pair(i // 4 + 1)
                    if i >= 5 and i % 4 == 1:
                        pair_hi(i // 4 - 1, 0, 0, base + i - 1)
                pair_hi(7, 0, 0, base + 2 * NQ)
                prep("nsa", 4, (1,))
                prep("nsa", 5, (1,))
                prep("nsa", 6)

            mixers = dict(fox=fox_mixer, mla=mla_mixer, mlstm=mlstm_mixer, kv=kv_stage, nsa=nsa_mixer)
            for name in PHASES:
                if name == "ffn4":
                    norm("final")
                if name.startswith("ffn"):
                    norm(name)
                    ffn(name)
                else:
                    mixers[name]()

        @block.vector
        def _(dve):
            V = nc.vector
            chain = [0]

            def link(ins):
                chain[0] += 1
                ins.then_inc(dve_chain, 1)
                dve.wait_ge(dve_chain, chain[0])

            def prep(name, tile, kinds=KINDS):
                for u in kinds:
                    prepare_lo(T0[name] + tile, u)

            def wide(ap, *shape):
                return ap.to_broadcast([ap.shape[0], *shape])

            def residual(name, scale):
                r = RESIDUAL[name]
                for t in range(NT):
                    for n in range(2):
                        i = 2 * t + n
                        if i < 3:
                            dve.wait_ge(acc_done, 3 * r + i + 1)
                        else:
                            wait_half(dve, name, *((FT - 1, 2) if name[:3] == "ffn" else WOUT[name][-1][:2]))
                        col = h[:, t, 512 * n:512 * (n + 1)]
                        V.scalar_tensor_tensor(col, A[i][:, :], scale, col, ALU.mult, ALU.add).then_inc(h_ready, 1)

            def norm(name):
                n = NORM[name]
                for t in range(NT):
                    dve.wait_ge(sq_done, NT * n + t + 1)
                    V.tensor_scalar(meansq[:, t:t + 1], sumsq[:, t:t + 1], 1.0 / D, EPS, ALU.mult, ALU.add
                                    ).then_inc(ms_ready, 1)
                if name == "final":
                    dve.wait_ge(gfin_landed, 16)
                    for t in range(NT):
                        dve.wait_ge(rstd_ready, NT * n + t + 1)
                        V.scalar_tensor_tensor(h[:, t, :], h[:, t, :], rstd[:, t:t + 1], arena[:, 0:D], ALU.mult, ALU.mult
                                               ).then_inc(h_ready, 1)
                    return
                k = TRANSPOSED[name]
                dve.wait_ge(rstd_ready, NT * n + 1)
                V.tensor_scalar(y[:, 0, :], h[:, 0, :], rstd[:, 0:1], None, ALU.mult).then_inc(y0_ready, 1)
                f = int(name[3:]) if name[:3] == "ffn" else -1
                g, g0 = (("norm_ffn", KC * f) if 0 <= f < 4 else ("ffn_norm_2", KC * (f - 4)) if f >= 4 else
                         {"fox": ("norm_mix", 0), "mla": ("norm_mix", KC), "mlstm": ("mix_norm_2", 0),
                          "nsa": ("mix_norm_2", KC), "kv": ("kv_norm_2", 0)}[name])
                for i, c in enumerate(CHUNKS):
                    dve.wait_ge(xhi_done, KC * k + i + 1)
                    V.scalar_tensor_tensor(xl[:, c, :], TB[c // 2][:, c % 2 * S:(c % 2 + 1) * S], gcol(g, g0 + c),
                                           xh[:, c, :].bitcast(F32), ALU.mult, ALU.subtract).then_inc(xlo_done, 1)

            def ffn(name):
                f, base = int(name[3:]), T0[name]

                def hidden(k, turn=None):
                    at = 0 if turn is None else 4 * turn
                    n, bank = FT * f + k, G[k % 2]
                    dve.wait_ge(sig_ready, n + 1 + at)
                    if n >= 1:
                        dve.wait_ge(hid_steps, 4 * n + 4 * at)
                    V.tensor_tensor(gated, bank[:, 0:S], sig[:, k % 2, :], ALU.mult).then_inc(hid_steps, 1)
                    dve.wait_ge(hid_steps, 4 * n + 1 + 4 * at)
                    V.tensor_tensor(hid, bank[:, S:2 * S], gated, ALU.mult).then_inc(hid_steps, 1)
                    dve.wait_ge(hid_steps, 4 * n + 2 + 4 * at)
                    V.tensor_copy(hidh[:, k % 2, :], hid).then_inc(hid_steps, 1)
                    dve.wait_ge(hid_steps, 4 * n + 3 + 4 * at)
                    V.tensor_tensor(hidl[:, k % 2, :], hid, hidh[:, k % 2, :].bitcast(F32), ALU.subtract
                                    ).then_inc(hid_steps, 1)

                prep(name, 1)
                hidden(0)
                with dve.Fori(0, LOOPS) as m:
                    for k in range(2, 6):
                        prepare_lo(base + k, 0, m)
                        prepare_lo(base + k, 1, m)
                        hidden(k - 1, m)
                        prepare_lo(base + k, 2, m)
                prep(name, FT, (0, 1))
                hidden(FT - 1)
                prep(name, FT, (2,))
                residual(name, 0.5)

            def low(dst, src, hi, done):
                return V.tensor_tensor(dst, src, hi.bitcast(F32), ALU.subtract).then_inc(done, 1)

            def pair_lo(pair, count):
                dve.wait_ge(o_hi, count)
                chunk = pair if count > 8 else pair + 4
                low(ml[:, chunk, :], A[pair % 2][:, 0:S], mh[:, chunk, :], o_lo)

            def maxima(i, base, blocks):
                slot = L[:, i % 3, :]
                dve.wait_ge(l_done, base + i + 1)
                for j, (b, c0, c1) in enumerate(blocks):
                    last = V.tensor_reduce(nmax[:, i % 3, b:b + 1], slot[:, c0:c1], AX.X, ALU.max, negate=True)
                return last

            OWN = ((0, 0, P), (1, P, TRI))

            def scale_rows(i, e_count, blocks, gate=None):
                n = len(blocks)
                dve.wait_ge(e_done, e_count)
                link(V.reciprocal(zinv[:, i % 3, 0:n], zsum[:, i % 3, 0:n]))
                if gate:
                    gate()
                for b, c0, c1 in blocks:
                    last = V.tensor_scalar(L[:, i % 3, c0:c1], L[:, i % 3, c0:c1], zinv[:, i % 3, b:b + 1], None, ALU.mult)
                last.then_inc(p_done, 1)

            def attend(base, n, logits, e_of, tail, blocks=lambda i: OWN, gate=None):
                for i in range(n + 1):
                    if i < n:
                        dve.wait_ge(s_ready, base + i + 1)
                        if base + i >= 3:
                            dve.wait_ge(pt_ready, base + i - 2)
                        logits(i)
                        maxima(i, base, blocks(i)).then_inc(max_done, 1)
                    if i >= 1:
                        scale_rows(i - 1, e_of(i - 1), blocks(i - 1), gate and (lambda: gate(i - 1)))
                    tail(i)

            def fox_mixer():
                norm("fox")
                prep("fox", 1)
                prep("fox", 2)
                dve.wait_ge(tlin_out, 5)
                u, s1, s2, df, fix = (fox[k] for k in ("u", "s1", "s2", "diff", "fix"))
                body = slice(PADT, UP)
                back = lambda x, n: x[:, :, PADT - n:UP - n]
                link(V.tensor_tensor(s1[:, :, body], u[:, :, body], back(u, 1), ALU.add))
                link(V.tensor_tensor(s2[:, 1:4, body], s1[:, 1:4, body], back(s1[:, 1:4, :], 2), ALU.add))
                link(V.tensor_tensor(s1[:, 2:4, body], s2[:, 2:4, body], back(s2[:, 2:4, :], 4), ALU.add))
                link(V.tensor_tensor(s2[:, 3:4, body], s1[:, 3:4, body], back(s1[:, 3:4, :], 8), ALU.add))
                inv = cst("inv_count", 4, PADT)
                for g, w in enumerate(POOL_W):
                    win = (s1, s2)[g % 2][:, g, :]
                    V.scalar_tensor_tensor(df[:, g, :], win[:, body], 1.0 / w, u[:, g, body], ALU.mult, ALU.subtract)
                    last = V.tensor_tensor(fix[:, PADT * g:PADT * (g + 1)], win[:, PADT:2 * PADT], inv[:, g, :], ALU.mult)
                link(last)
                V.tensor_tensor(df[:, :, 0:PADT], fix.rearrange("p (g n) -> p g n", g=4), u[:, :, PADT:2 * PADT],
                                ALU.subtract).then_inc(event("fox_diff"), 1)
                for tile in (3, 4, 5):
                    prep("fox", tile)
                prep("fox", 6, (0, 1))
                prep("fox", 7, (0, 1))
                dve.wait_ge(small_done, 1)
                for t in range(NT):
                    last = V.tensor_tensor(fox["z"][:, 8 * t:8 * t + 8], A[2][:, 8 * t:8 * t + 8], fox["bf"], ALU.add)
                link(last)
                V.scalar_tensor_tensor(fox["nz"], fox["z"], -1.0, fox["z"], ALU.mult, ALU.min).then_inc(event("fox_nz"), 1)
                dve.wait_ge(event("fox_ln"), 1)
                V.scalar_tensor_tensor(fox["logf"], fox["z"], 0.0, fox["e"], ALU.min, ALU.subtract
                                       ).then_inc(event("fox_logf"), 1)
                for g in range(4):
                    dve.wait_ge(o_hi, g + 1)
                    V.scalar_tensor_tensor(ml[:, g, :], TB[g][:, 0:S], gcol("pool_scale", g),
                                           mh[:, g, :].bitcast(F32), ALU.mult, ALU.subtract
                                           ).then_inc(o_lo, 1)
                dve.wait_ge(event("fox_sums"), 1)
                V.tensor_copy(fox["F"], A[2][:, 16:32]).then_inc(event("fox_sums_out"), 1)
                dve.wait_ge(event("fox_sums_out"), 2)
                base, mask = STEPS["fox"], cst("causal")

                def logits(i):
                    for t, (b, c0, c1) in enumerate(OWN):
                        last = V.scalar_tensor_tensor(L[:, i % 3, c0:c1], G[i % 2][:, c0:c1], fox["F"][:, 8 * t + i:8 * t + i + 1],
                                                      mask[:, c0:c1], ALU.add, ALU.add)
                    last.then_inc(l_done, 1)

                def tail(i):
                    if i >= 4 and i % 2 == 0:
                        fox_lo(i // 2 - 2)

                def fox_lo(p):
                    dve.wait_ge(o_hi, 5 + p)
                    low(ml[:, 4 + p, :], A[p % 2][:, 0:S], mh[:, 4 + p, :], o_lo)

                attend(base, FOX_H, logits, lambda i: E0["fox"] + 2 * i + 2, tail)
                fox_lo(3)
                prep("fox", 6, (2,))
                prep("fox", 7, (2,))
                prep("fox", 8)
                residual("fox", 1.0)

            def mla_mixer():
                norm("mla")
                prep("mla", 1)
                prep("mla", 2, (0, 1))
                dve.wait_ge(w2_landed, 32)
                link(V.tensor_copy(mla["pos"], mla["posi"].bitcast(I32)))
                for t in range(NT):
                    last = V.tensor_scalar(mla["ang"][:, t, :], cst("inv_freq"), mla["pos"][:, t:t + 1], None, ALU.mult)
                link(last)
                two_pi, big = 2.0 * np.pi, 1.5 * 2.0 ** 23
                parts = (6.28125, 0.0019350051879882812, two_pi - 6.28125 - 0.0019350051879882812)
                for off, dst in ((0.0, mla["rs_in"]), (0.25, mla["rc_in"])):
                    link(V.tensor_scalar(mla["turn"], mla["ang"], 1.0 / two_pi, off, ALU.mult, ALU.add))
                    link(V.tensor_scalar(mla["turn"], mla["turn"], big, big, ALU.add, ALU.subtract))
                    src = mla["ang"]
                    for c in parts:
                        link(V.scalar_tensor_tensor(dst, mla["turn"], -c, src, ALU.mult, ALU.add))
                        src = dst
                    if off:
                        link(V.tensor_scalar(dst, dst, np.pi / 2, None, ALU.add))
                    V.tensor_scalar(dst, dst, -3.1415925, 3.1415925, ALU.max, ALU.min).then_inc(event("mla_ang"), 1)
                    dve.wait_ge(event("mla_ang"), 1 if off == 0.0 else 2)
                dve.wait_ge(event("mla_sq"), 4)
                for i, n in enumerate((Q_LORA, KV_LORA)):
                    last = V.tensor_scalar(mla["ms"][:, :, i], mla["ss"][:, :, i], 1.0 / n, EPS, ALU.mult, ALU.add)
                last.then_inc(mx_ready, 1)
                dve.wait_ge(mx_pow, 1)
                for t in range(NT):
                    for i, (c0, c1) in enumerate(((0, Q_LORA), (Q_LORA, Q_LORA + KV_LORA))):
                        last = V.tensor_scalar(mla["cn"][:, t, c0:c1], mla["cin"][:, t, c0:c1], mla["rs"][:, t, i:i + 1],
                                               None, ALU.mult)
                    last.then_inc(event("mla_cn"), 1)
                for c in range(3):
                    g = gcol("mla_q_norm", c) if c < 2 else gcol("mla_kv_norm", 0)
                    dve.wait_ge(event("mla_c_hi"), c + 1)
                    V.scalar_tensor_tensor(mlf[:, c * S:(c + 1) * S], TB[c][:, 0:S], g,
                                           mhf[:, c * S:(c + 1) * S].bitcast(F32), ALU.mult, ALU.subtract
                                           ).then_inc(event("mla_c_lo"), 1)
                dve.wait_ge(event("mla_cs"), 2)
                R2 = ROPE // 2

                def rotate(x1, x2, o1, o2, cos, sin, t1, t2, done=None):
                    V.tensor_tensor(t1, x1, sin, ALU.mult)
                    link(V.tensor_tensor(t2, x2, sin, ALU.mult))
                    V.tensor_tensor(o1, x1, cos, ALU.mult)
                    link(V.tensor_tensor(o2, x2, cos, ALU.mult))
                    V.tensor_tensor(o1, o1, t2, ALU.subtract)
                    last = V.tensor_tensor(o2, o2, t1, ALU.add)
                    last.then_inc(done, 1) if done is not None else link(last)

                at = Q_LORA + KV_LORA
                cin, kr = mla["cin"], mla["kr"]
                rotate(cin[:, :, at:at + R2], cin[:, :, at + R2:at + ROPE], kr[:, :, 0:R2], kr[:, :, R2:ROPE],
                       mla["cos"], mla["sin"], mla["t1"][:, 0:NT, :], mla["t2"][:, 0:NT, :])
                for t in range(NT):
                    k = mla["k"][:, t, :].rearrange("p (h n) -> p h n", n=QK)[:, :, NOPE:QK]
                    last = V.tensor_copy(k, wide(kr[:, t, :].unsqueeze(1), MLA_H, ROPE))
                prep("mla", 2, (2,))
                prep("mla", 3)
                prep("mla", 4, (0,))
                dve.wait_ge(event("mla_b_out"), 6)
                for t in range(NT):
                    q = mla["q"][:, t, :].rearrange("p (h n) -> p h n", n=QK)
                    x1, x2 = q[:, :, NOPE:NOPE + R2], q[:, :, NOPE + R2:QK]
                    rotate(x1, x2, x1, x2, wide(mla["cos"][:, t, :].unsqueeze(1), MLA_H, R2),
                           wide(mla["sin"][:, t, :].unsqueeze(1), MLA_H, R2), mla["t1"], mla["t2"],
                           event("mla_roped") if t == NT - 1 else None)
                prep("mla", 4, (1,))
                prep("mla", 5, (0,))
                base, mask = STEPS["mla"], cst("chunk64")

                def logits(i):
                    V.tensor_tensor(L[:, i % 3, 0:TRI], G[i % 2][:, 0:TRI], mask, ALU.add).then_inc(l_done, 1)

                def tail(i):
                    if i >= 4 and i % 2 == 0:
                        pair_lo(i // 2 - 2, 9 + i // 2 - 2)

                attend(base, MLA_H, logits, lambda i: E0["mla"] + 2 * i + 2, tail)
                pair_lo(7, 16)
                prep("mla", 4, (2,))
                prep("mla", 5, (1, 2))
                prep("mla", 6)
                residual("mla", 1.0)

            def mlstm_mixer():
                norm("mlstm")
                for tile in range(1, 10):
                    prep("mlstm", tile)
                z, F_, m = mls["z"], mls["F"], mls["m"]
                dve.wait_ge(small_done, 2)
                for t in range(NT):
                    last = V.tensor_tensor(z[:, t, :], A[0][:, 16 * t:16 * t + 16], mls["bif"], ALU.add)
                link(last)
                V.scalar_tensor_tensor(mls["nz"], z[:, :, 8:16], -1.0, z[:, :, 8:16], ALU.mult, ALU.min).then_inc(event("ml_nz"), 1)
                dve.wait_ge(event("ml_ln"), 1)
                V.scalar_tensor_tensor(mls["logf"], z[:, :, 8:16], 0.0, mls["e"], ALU.min, ALU.subtract
                                       ).then_inc(event("ml_logf"), 1)
                dve.wait_ge(event("ml_sums"), 2)
                V.tensor_copy(F_, A[1][:, 0:16].rearrange("p (t n) -> p t n", t=NT))
                link(V.tensor_copy(mls["R"][0:8, :], A[3][0:8, 0:S]))
                V.tensor_tensor(mls["R"][0:8, :], mls["R"][0:8, :], A[2][0:8, 0:S], ALU.subtract
                                ).then_inc(event("ml_rows"), 1)
                base, mask = STEPS["mlstm"], cst("causal")

                for i in range(ML_H + 1):
                    if i < ML_H:
                        dve.wait_ge(s_ready, base + i + 1)
                        dve.wait_ge(pt_ready, base + i - 2)
                        slot = L[:, i % 3, :]
                        for t, (b, c0, c1) in enumerate(OWN):
                            last = V.scalar_tensor_tensor(slot[:, c0:c1], A[2 + i % 2][:, c0:c1], F_[:, t, i:i + 1],
                                                          mask[:, c0:c1], ALU.add, ALU.add)
                        last.then_inc(l_done, 1)
                        dve.wait_ge(l_done, base + i + 1)
                        for t, (b, c0, c1) in enumerate(OWN):
                            last = V.tensor_reduce(m[:, t, i:i + 1], slot[:, c0:c1], AX.X, ALU.max)
                        link(last)
                        link(V.tensor_tensor(m[:, :, i], m[:, :, i], F_[:, :, i], ALU.max))
                        V.tensor_scalar(nmax[:, i % 3, 0:2], m[:, :, i], -1.0, None, ALU.mult).then_inc(max_done, 1)
                    if i >= 1:
                        j = i - 1
                        dve.wait_ge(e_done, E0["mlstm"] + 2 * j + 2)
                        for t, (b, c0, c1) in enumerate(OWN):
                            slot = L[:, j % 3, c0:c1]
                            last = V.tensor_tensor_reduce(slot, slot, G[j % 2][:, c0:c1], 1.0, 0.0, ALU.mult, ALU.add,
                                                          mls["den"][:, t, j:j + 1])
                        last.then_inc(p_done, 1)
                dve.wait_ge(event("ml_em"), 1)
                dve.wait_ge(p_done, base + ML_H)
                link(V.scalar_tensor_tensor(mls["den"], mls["den"], -1.0, mls["den"], ALU.mult, ALU.max))
                link(V.tensor_tensor(mls["c"], mls["den"], mls["b"], ALU.max))
                link(V.reciprocal(mls["c"], mls["c"]))
                dve.wait_ge(event("ml_sq"), NT * ML_H)
                link(V.tensor_tensor(mls["a"], mls["ssq"], mls["c"], ALU.mult))
                link(V.tensor_tensor(mls["a"], mls["a"], mls["c"], ALU.mult))
                V.tensor_scalar(mls["a"], mls["a"], 1.0 / ML_DV, EPS, ALU.mult, ALU.add).then_inc(mx_ready, 1)
                dve.wait_ge(mx_pow, 2)
                link(V.tensor_tensor(mls["c"], mls["c"], mls["d"], ALU.mult))
                for t in range(NT):
                    o = mls["o"][:, t, :].rearrange("p (h n) -> p h n", h=ML_H)
                    V.tensor_tensor(o, o, wide(mls["c"][:, t, :].unsqueeze(2), ML_H, ML_DV), ALU.mult
                                    ).then_inc(event("ml_y"), 1)
                for c in range(ML_H):
                    dve.wait_ge(event("ml_turned"), c // 2 + 1)
                    if c >= 2:
                        dve.wait_ge(o_lo, 16 + c - 1)
                    sc = mls["sc"][:, c % 2, 0:S]
                    V.scalar_tensor_tensor(sc, TB[c // 2][:, c % 2 * S:(c % 2 + 1) * S], gcol("a_g_head_2", c),
                                           mls["og"][:, c, :], ALU.mult, ALU.mult).then_inc(event("ml_mix"), 1)
                    if c >= 1:
                        ml_lo(c - 1)
                ml_lo(ML_H - 1)
                for tile in (10, 11, 12):
                    prep("mlstm", tile)
                residual("mlstm", 1.0)

            def ml_lo(c):
                dve.wait_ge(o_hi, 16 + c + 1)
                low(ml[:, c, :], mls["sc"][:, c % 2, 0:S], mh[:, c, :], o_lo)

            def kv_stage():
                norm("kv")
                V.memset(nsa["kC"], 0.0).then_inc(event("kv_zero"), 1)
                V.memset(nsa["vC"][0:2 * CP, :, :], 0.0).then_inc(event("kv_zero"), 1)
                for tile in range(1, 4):
                    prep("kv", tile)
                dve.wait_ge(event("kv_ksw"), 4)
                k = nsa["ksw"].rearrange("p t g n -> p (t g) n")
                sq = yf[:, 0:1024].rearrange("p (r n) -> p r n", n=HD)
                link(V.tensor_tensor(sq, k, k, ALU.mult))
                link(V.tensor_reduce(nsa["ss"][:, 0:16], sq, AX.X, ALU.add))
                V.tensor_scalar(nsa["ms"][:, 0:16], nsa["ss"][:, 0:16], 1.0 / HD, EPS, ALU.mult, ALU.add
                                ).then_inc(mx_ready, 1)
                dve.wait_ge(mx_pow, 3)
                dup = yf.rearrange("p (r d n) -> p r d n", d=2, n=HD)
                for d in range(2):
                    V.tensor_tensor(dup[:, :, d, :], k, wide(nsa["rs"][:, 0:16].unsqueeze(2), 16, HD), ALU.mult
                                    ).then_inc(event("kv_dup"), 1)
                prep("kv", 4)
                prep("kv", 5)
                dve.wait_ge(event("kv_dup"), 2)
                blk = nsa["blk"]
                for kind in range(2):
                    dve.wait_ge(event("kv_c_cols"), 4 if kind else 2)
                    for jh in range(2):
                        src = nsa["cT"][:, 4 * kind:4 * kind + 4, 16 * jh:16 * jh + CMP_STRIDE * NCMP]
                        src = src.rearrange("p g (c j e) -> p j g c e", c=NCMP, e=2)[:, :, :, :, 0]
                        pos = pe_col[:, 16 * kind + 8 * jh:16 * kind + 8 * jh + 8]
                        pos = wide(pos.unsqueeze(2).unsqueeze(3), 8, NKV, NCMP)
                        dst = blk[:, 8 * jh:8 * jh + 8, :].rearrange("p j (g c) -> p j g c", g=NKV)
                        last = V.tensor_tensor(dst, src, pos, ALU.add)
                    last.then_inc(event("kv_blk"), 1)
                    at = slice(960 * kind, 960 * (kind + 1))
                    dve.wait_ge(event("kv_blk_hi"), kind + 1)
                    low(mlf[:, at], blk.rearrange("p j r -> p (j r)"), mhf[:, at], event("kv_blk_lo"))
                    dve.wait_ge(event("kv_blk_lo"), kind + 1)
                prep("kv", 6)
                for kind in range(2):
                    bank = [[G[0], G[1]], [A[0], A[1]]][kind]
                    for c in range(2):
                        dve.wait_ge(event("kv_sig"), 2 * kind + c + 1)
                        x = nsa["hk"][:, kind, c, :]
                        last = V.tensor_tensor(x, x, bank[c][:, 0:60], ALU.mult)
                    last.then_inc(event("kv_act"), 1)
                    if kind == 0:
                        prep("kv", 7)
                dve.wait_ge(event("kv_k2sq"), 1)
                V.tensor_scalar(nsa["ms"][0:60, 16:17], nsa["ss"][0:60, 16:17], 1.0 / HD, EPS, ALU.mult, ALU.add
                                ).then_inc(mx_ready, 1)
                dve.wait_ge(mx_pow, 4)
                for d in range(2):
                    last = V.tensor_scalar(nsa["kcn"][0:60, HD * d:HD * (d + 1)], A[2][0:60, 0:HD],
                                           nsa["rs"][0:60, 16:17], None, ALU.mult)
                last.then_inc(event("kv_kcn"), 1)
                prep("kv", 8)

            def nsa_mixer():
                norm("nsa")
                prep("nsa", 1)
                prep("nsa", 2)
                prep("nsa", 3)
                V.tensor_scalar(nsa["sc"][:, 0:1], gcol("b_q_norm_2", 0), HD ** -0.5, None, ALU.mult
                                ).then_inc(event("nsa_sc"), 1)
                dve.wait_ge(row_out, 5)
                for t in range(NT):
                    last = V.tensor_tensor(y[:, t, :], nsa["q"][:, t, :], nsa["q"][:, t, :], ALU.mult)
                link(last)
                link(V.tensor_reduce(nsa["ss"], yf.rearrange("p (r n) -> p r n", n=HD), AX.X, ALU.add))
                V.tensor_scalar(nsa["ms"], nsa["ss"], 1.0 / HD, EPS, ALU.mult, ALU.add).then_inc(mx_ready, 1)
                dve.wait_ge(mx_pow, 5)
                for t in range(NT):
                    q = nsa["q"][:, t, :].rearrange("p (r n) -> p r n", n=HD)
                    V.tensor_tensor(q, q, wide(nsa["rs"][:, 16 * t:16 * t + 16].unsqueeze(2), NQ, HD), ALU.mult
                                    ).then_inc(event("nsa_q"), 1)
                prep("nsa", 4, (0,))
                prep("nsa", 5, (0,))
                dve.wait_ge(event("nsa_gates"), 1)
                for t in range(NT):
                    last = V.tensor_scalar(nsa["g"][:, t, 0:NQ], nsa["g"][:, t, 0:NQ], cst("cmp_row_ok")[:, t:t + 1], None,
                                           ALU.mult)
                link(last)
                base, mask = STEPS["nsa"], cst("causal")

                def blocks(s):
                    return OWN if s % 2 else OWN + ((2, TRI, TRI + CP), (3, TRI + CP, TRI + 2 * CP))

                def logits(s):
                    w = TRI if s % 2 else TRI + 2 * CP
                    V.tensor_tensor(L[:, s % 3, 0:w], G[s % 2][:, 0:w], mask[:, 0:w], ALU.add).then_inc(l_done, 1)

                def gate(s):
                    i, z = s // 2, zinv[:, s % 3, :]
                    g = nsa["g"]
                    if s % 2:
                        link(V.tensor_tensor(z[:, 0:2], z[:, 0:2], g[:, :, 2 * NQ + i], ALU.mult))
                    else:
                        V.tensor_tensor(z[:, 2:4], z[:, 2:4], g[:, :, i], ALU.mult)
                        link(V.tensor_tensor(z[:, 0:2], z[:, 0:2], g[:, :, NQ + i], ALU.mult))

                def tail(i):
                    if i >= 5 and i % 4 == 1:
                        nsa_lo(i // 4 - 1)

                def nsa_lo(p):
                    dve.wait_ge(o_hi, 24 + p + 1)
                    low(ml[:, p, :], A[p % 2][:, 0:S], mh[:, p, :], o_lo)

                attend(base, 2 * NQ, logits, lambda s: E0["nsa"] + 6 * (s // 2) + (6 if s % 2 else 4), tail, blocks, gate)
                nsa_lo(7)
                prep("nsa", 4, (1,))
                prep("nsa", 5, (1,))
                prep("nsa", 6)
                residual("nsa", 1.0)

            for i, (c0, n) in enumerate(SMALL.values()):
                dve.wait_ge(small_hi, i + 1)
                last = V.tensor_tensor(small_l[:, c0:c0 + KC * n], y[:, 1, c0:c0 + KC * n],
                                       small_h[:, c0:c0 + KC * n].bitcast(F32), ALU.subtract)
            last.then_inc(small_ready, 1)
            for x in ("u", "s1", "s2"):
                last = V.memset(fox[x][:, :, 0:PADT], 0.0)
            link(last)
            prep("ffn0", 0)
            mixers = dict(fox=fox_mixer, mla=mla_mixer, mlstm=mlstm_mixer, kv=kv_stage, nsa=nsa_mixer)
            for name in PHASES:
                if name == "ffn4":
                    norm("final")
                if name.startswith("ffn"):
                    norm(name)
                    ffn(name)
                else:
                    mixers[name]()


STEPS = {"fox": 0, "mla": FOX_H, "mlstm": FOX_H + MLA_H, "nsa": FOX_H + MLA_H + ML_H}
E0 = {k: 2 * v for k, v in STEPS.items()}
o_count = {"fox": 8, "mla": 16, "mlstm": 24, "nsa": 32}
o_before = {"mla": 8, "nsa": 24}
ROW_OUT = {"mlstm": 2, "kv": 4, "nsa": 5}
ROWS_COUNT = 16 * (len(GAIN_ROWS) + 2 + 1)
SMALL_COUNT = 16 * 6

_OUT = (1, S, D)


def kernel(**inputs):
    import concourse.bacc as bacc
    from concourse.bass_utils import run_bass_kernel_spmd

    nc = bacc.Bacc("TRN2", target_bir_lowering=False, num_devices=1)
    arrays, W = {}, {}

    def given(name, a):
        arrays[f"in_{name}"] = a
        return nc.dram_tensor(f"in_{name}", a.shape, mybir.dt.from_np(a.dtype), kind="ExternalInput").ap()

    for name, a in inputs.items():
        a = np.ascontiguousarray(a)
        W[name] = given(name, a)
    W["const"] = given("const", shape_constants())
    for name in ("ab_w_in", "ab_b_forget", "pool_w", "pool_scale", "ab_w_out", "mla_w_in", "mla_q_norm", "mla_kv_norm",
                 "mla_w_q_b", "mla_w_kv_b", "mla_w_out", "a_w_in_2", "a_b_if_2", "a_g_head_2", "a_w_out_2",
                 "b_w_in_2", "b_q_norm_2", "b_w_out_2"):
        W[name] = W[name][0]
    W["a_b_if_2"] = W["a_b_if_2"].rearrange("a b -> (a b)")
    W["b_q_norm_2"] = W["b_q_norm_2"].rearrange("(a n) -> a n", a=1)
    W["norm_ffn"] = W["norm_ffn"].rearrange("a b d -> (a b) d")
    W["ffn_norm_2"] = W["ffn_norm_2"].rearrange("a b d -> (a b) d")
    out = nc.dram_tensor("out", _OUT, F32, kind="ExternalOutput").ap()
    blocks_program(nc, W, out)
    r = run_bass_kernel_spmd(nc, [arrays], core_ids=[0])
    return r.results[0]["out"]
```

```python
from contextlib import ExitStack

import numpy as np

import concourse.bass as bass
from concourse import mybir

F32 = mybir.dt.float32
F32R = mybir.dt.float32r
I32 = mybir.dt.int32
ALU = mybir.AluOpType
ACT = mybir.ActivationFunctionType
AX = mybir.AxisListType

P = 128
S = 256
NT = S // P
D = 1024
KC = D // P
F = 2816
EPS = 1e-6
NEG = -1e30

FOX_H, FOX_D = 8, 64
MLA_H, NOPE, ROPE, MLA_V = 16, 64, 32, 64
QK = NOPE + ROPE
Q_LORA, KV_LORA = 256, 128
MLA_IN = Q_LORA + KV_LORA + ROPE
ML_H, ML_DK, ML_DV = 8, 64, 128
NQ, NKV, HD = 16, 4, 64
CMP_BLOCK, CMP_STRIDE, CMP_HID = 32, 16, 256
NCMP = (S - CMP_BLOCK) // CMP_STRIDE + 1
CP = 32
POOL_W = (2, 4, 8, 16)
PADT = 16
ARENA = 8224

FFN_BLOCKS = F // 256
FT = 2 * FFN_BLOCKS
LOOPS = (FT - 2) // 4
TRI = 3 * P

CONST = {}
_at = 0
for _name, _n in (("ident", P), ("pick", 8), ("tri", S),
                  ("cmp_mask", 2 * CP), ("cmp_row_ok", 2), ("inv_count", 4 * PADT), ("inv_freq", ROPE // 2),
                  ("neg_half", 32)):
    CONST[_name] = (_at, _n)
    _at += _n
NCONST = _at
MASKS = {"causal": (NCONST, 1), "chunk64": (NCONST + 3 * P, 64)}


def shape_constants():
    c = np.zeros((P, NCONST + 6 * P), np.float32)

    def put(name, a):
        at, n = CONST[name]
        c[:a.shape[0], at:at + n] = a.reshape(a.shape[0], n)

    r = np.arange(P)
    put("ident", np.eye(P, dtype=np.float32))
    put("tri", (r[:, None] <= np.arange(S)[None, :]).astype(np.float32))
    put("pick", ((r[:, None] == np.arange(8)) | (r[:, None] == 32 + np.arange(8))).astype(np.float32))
    for at, g in MASKS.values():
        mask = np.where(r[None, :] // g <= r[:, None] // g, 0.0, NEG)
        c[:, at:at + P], c[:, at + 2 * P:at + 3 * P] = mask.T, mask
    q1 = P + r
    ends = np.arange(CP) * CMP_STRIDE + CMP_BLOCK - 1
    real = np.arange(CP) < NCMP
    put("cmp_mask", np.concatenate([np.where(real[None, :] & (ends[None, :] <= t[:, None]), 0.0, NEG)
                                    for t in (r, q1)], axis=1))
    put("cmp_row_ok", np.stack([(t >= CMP_BLOCK - 1) for t in (r, q1)], axis=1).astype(np.float32))
    inv = np.stack([1.0 / np.minimum(np.arange(PADT) + 1, w) for w in POOL_W]).astype(np.float32)
    put("inv_count", np.broadcast_to(inv[None], (P, 4, PADT)))
    freq = np.float32(10000.0) ** (-np.arange(0, ROPE, 2, dtype=np.float32) / np.float32(ROPE))
    put("inv_freq", np.broadcast_to(freq.astype(np.float32)[None], (P, ROPE // 2)))
    put("neg_half", np.full((P, 32), -0.5, np.float32))
    return c


GAIN_ROWS = {}
_at = 0
for _name, _n in (("norm_ffn", 32), ("norm_mix", 16), ("ffn_norm_2", 32), ("mix_norm_2", 16), ("kv_norm_2", 8),
                  ("mla_q_norm", 2), ("mla_kv_norm", 1), ("pool_scale", 4), ("a_g_head_2", 8), ("k_norm_2", 3),
                  ("b_q_norm_2", 1)):
    GAIN_ROWS[_name] = (_at, _n)
    _at += _n
NGAIN = _at
FIRST_GAINS = 32

KINDS = (0, 1, 2)
"""The stream of weights: for every block its three units, each (name, how it is cut, half's shape)."""


def unit(src, cut, half):
    return dict(src=src, cut=cut, half=half)


def mixer_units(W):
    def cols(w, c0):
        return unit(w[:, c0:c0 + 256].rearrange("(c p) n -> p c n", p=P), "cols", (KC, P))

    def rows(w, k0, nk, c0, n):
        return unit(w[k0 * P:(k0 + nk) * P, c0:c0 + n].rearrange("(c p) n -> p c n", p=P), "rows", (nk // 2, n))

    def wide(w, n0, n):
        r = w.shape[0] // P
        return unit(w[:, n0:n0 + n].rearrange("(c p) n -> p c n", p=P), "cols", (r, n // 2))

    ab, abo = W["ab_w_in"], W["ab_w_out"]
    o = lambda w, i: rows(w, 2 * i, 2, 0, D)
    fox = [[cols(ab, 0), cols(ab, 256), cols(ab, 512)], [cols(ab, 768), cols(ab, 1024), cols(ab, 1280)],
           [rows(ab, 0, 4, 1536, 512), rows(ab, 4, 4, 1536, 512), o(abo, 0)], [o(abo, 1), o(abo, 2), o(abo, 3)]]
    mi, qb, kvb, mo = W["mla_w_in"], W["mla_w_q_b"], W["mla_w_kv_b"], W["mla_w_out"]
    last_q = unit(qb[:, 1024:1536].rearrange("(c p) n -> p c n", p=P), "one", (2, 512))
    mla = [[rows(mi, 0, 4, 0, MLA_IN), rows(mi, 4, 4, 0, MLA_IN), wide(qb, 0, 1024)],
           [last_q, wide(kvb, 0, 2048), o(mo, 0)], [o(mo, 1), o(mo, 2), o(mo, 3)]]
    a, ao = W["a_w_in_2"], W["a_w_out_2"]
    v = lambda i: rows(a, 2 * i, 2, 1024, D)
    og = lambda i: cols(a, 2064 + 256 * i)
    mls = [[cols(a, 0), cols(a, 256), cols(a, 512)], [cols(a, 768), v(0), v(1)], [v(2), v(3), og(0)],
           [og(1), og(2), og(3)], [o(ao, 0), o(ao, 1), o(ao, 2)], [o(ao, 3), None, None]]
    kw, w1 = W["kv_w_2"], W["cmp_w1_2"]
    g = lambda i, half: rows(kw, 4 * half, 4, 512 * i, 512)
    c1 = lambda kind, half: rows(w1[kind], 8 * half, 8, 0, CMP_HID)
    kv = [[g(0, 0), g(0, 1), g(1, 0)], [g(1, 1), g(2, 0), g(2, 1)], [c1(0, 0), c1(0, 1), c1(1, 0)],
          [c1(1, 1), None, None]]
    b, bo = W["b_w_in_2"], W["b_w_out_2"]
    q = lambda i: rows(b, 2 * i, 2, 0, D)
    nsa = [[q(0), q(1), q(2)], [q(3), o(bo, 0), o(bo, 1)], [o(bo, 2), o(bo, 3), None]]
    return dict(fox=fox, mla=mla, mlstm=mls, kv=kv, nsa=nsa)


PHASES = ("ffn0", "fox", "ffn1", "ffn2", "mla", "ffn3", "ffn4", "mlstm", "ffn5", "kv", "ffn6", "nsa", "ffn7")


class Stream:

    def __init__(self, units):
        self.first, self.blocks = {}, []
        for name in PHASES:
            self.first[name] = 2 * len(self.blocks)
            self.blocks += [("ffn",) * 3] * FFN_BLOCKS if name.startswith("ffn") else units[name]
        self.tiles = 2 * len(self.blocks)
        self.count, self.slot_last, self.landing, self.raw_last = {}, {}, {}, {}
        for u in KINDS:
            n, last, raw, raw_before = 0, {}, [0, 0], [0, 0]
            for b, block in enumerate(self.blocks):
                x = block[u]
                if x is not None:
                    raw[b % 2] += 1
                    self.landing[b, u] = 16 * raw[b % 2]
                    self.raw_last[b, u] = raw_before[b % 2]
                for t in (0, 1):
                    if x is None or (t == 1 and x != "ffn" and x["cut"] == "one"):
                        continue
                    n += 1
                    self.count[2 * b + t, u] = n
                    self.slot_last[2 * b + t, u] = last.get(t, 0)
                    last[t] = n
                if x is not None:
                    raw_before[b % 2] = n

    def real(self, tile, u):
        return (tile, u) in self.count

CHUNKS = (0, 2, 1, 3, 4, 6, 5, 7)

NORMS = ("ffn0", "fox", "ffn1", "ffn2", "mla", "ffn3", "final", "ffn4", "mlstm", "ffn5", "kv", "ffn6", "nsa", "ffn7")
NORM = {name: n for n, name in enumerate(NORMS)}
TRANSPOSED = {name: n for n, name in enumerate(x for x in NORMS if x != "final")}
RESIDUAL = {name: n for n, name in enumerate(x for x in PHASES if x != "kv")}
READY = {}
_at = 0
for _name in NORMS:
    READY[_name] = (_at - 2, _at) if _at else (0, 0)
    if _name == "final":
        _at += 2
        READY["after_final"] = (_at - 1, _at)
    elif _name != "kv":
        _at += 4
READY["ffn4"] = READY["after_final"]
READY["out"] = (_at - 2, _at)

SMALL = {"fox_f": (0, FOX_H), "ml_if": (64, 2 * ML_H), "nsa_g": (192, 3 * NQ)}
NSMALL = 192 + 8 * 48


def blocks_program(nc, W, out):
    units = mixer_units(W)
    stream = Stream(units)
    n_of, slot_last, landing, raw_last = stream.count, stream.slot_last, stream.landing, stream.raw_last

    ctx = ExitStack()
    with ctx:
        def sb(name, shape, dt=F32):
            return ctx.enter_context(nc.sbuf_tensor(name, shape, dt))

        def sem(name):
            return ctx.enter_context(nc.semaphore(name))

        raw = sb("raw", [P, 2, 3, 2048])
        wh = sb("wh", [P, 2, 3, 1024], F32R)
        wl = sb("wl", [P, 2, 3, 1024], F32R)
        h = sb("h", [P, NT, D])
        y = sb("y", [P, NT, D])
        xh = sb("xh", [P, KC, S], F32R)
        xl = sb("xl", [P, KC, S], F32R)
        mh = sb("mh", [P, KC, S], F32R)
        ml = sb("ml", [P, KC, S], F32R)
        const = sb("const", [P, NCONST])
        const_r = sb("const_r", [P, P + 8 + 10 * P], F32R)
        gain = sb("gain", [P, NGAIN])
        pe_col = sb("pe_col", [P, 2 * CMP_BLOCK // 2])
        work = sb("work", [P, 2368])
        hidh = sb("hidh", [P, 2, S], F32R)
        hidl = sb("hidl", [P, 2, S], F32R)
        arena = sb("arena", [P, ARENA])
        small_h = sb("small_h", [P, NSMALL], F32R)
        small_l = sb("small_l", [P, NSMALL], F32R)
        w2 = sb("w2", [P, 2, 2, HD])
        st = sb("st", [P, 400])

        A = [ctx.enter_context(nc.psum_tensor(f"A{i}", [P, 512], F32)) for i in range(4)]
        G = [ctx.enter_context(nc.psum_tensor(f"G{i}", [P, 512], F32)) for i in range(2)]
        X = [ctx.enter_context(nc.psum_tensor(f"X{i}", [P, 512], F32)) for i in range(2)]
        TB = [G[0], G[1], X[0], X[1]]
        NB = A

        def cut(buf, at, *shape):
            n = int(np.prod(shape))
            flat = buf[:, at:at + n]
            if len(shape) == 1:
                return flat
            names = "abcd"[:len(shape)]
            return flat.rearrange(f"p ({' '.join(names)}) -> p {' '.join(names)}", **dict(zip(names, shape)))

        def cst(name, *shape):
            at, n = CONST[name]
            return cut(const, at, *(shape or (n,)))

        ident, tri = cst("ident"), cst("tri")
        ident_r = const_r[:, 0:P]
        pick_r = const_r[:, P:P + 8]
        masks_r = {name: const_r[:, P + 8 + 5 * P * i:P + 8 + 5 * P * (i + 1)] for i, name in enumerate(MASKS)}

        def gcol(name, i):
            at = GAIN_ROWS[name][0] + i
            return gain[:, at:at + 1]

        _st = [0]

        def stat(*shape):
            at = _st[0]
            _st[0] += int(np.prod(shape))
            assert _st[0] <= 400
            return cut(st, at, *shape)

        yf = y[:].rearrange("p t n -> p (t n)")
        mhf, mlf = mh[:].rearrange("p c n -> p (c n)"), ml[:].rearrange("p c n -> p (c n)")

        sumsq, meansq, rstd = stat(2), stat(2), stat(2)
        zinv = stat(4)
        nmax = stat(2, NT, 4)
        sig = cut(work, 0, 2, S)
        gated, hid = cut(work, 512, S), cut(work, 768, S)
        PT = cut(work, 0, 2, TRI)
        x_landed = [sem(f"x_landed{t}") for t in range(NT)]
        masks_landed = sem("masks_landed")
        const_landed, rows_landed, small_landed, w2_landed = (sem("const_landed"), sem("rows_landed"),
                                                              sem("small_landed"), sem("w2_landed"))
        gfin_landed = sem("gfin_landed")
        gain0_landed, gain0_turned = sem("gain0_landed"), sem("gain0_turned")
        rows_turned, gain_ready = sem("rows_turned"), sem("gain_ready")
        small_hi, small_ready = sem("small_hi"), sem("small_ready")
        raw_landed = [[sem(f"raw{p}{u}_landed") for u in KINDS] for p in (0, 1)]
        hi_done = [sem(f"hi{u}_done") for u in KINDS]
        lo_done = [sem(f"lo{u}_done") for u in KINDS]
        used = [sem(f"used{u}") for u in KINDS]
        h_ready, sq_done, ms_ready, rstd_ready = sem("h_ready"), sem("sq_done"), sem("ms_ready"), sem("rstd_ready")
        y0_ready, y1_ready, turned = sem("y0_ready"), sem("y1_ready"), sem("turned")
        xhi_done, xlo_done, acc_done = sem("xhi_done"), sem("xlo_done"), sem("acc_done")
        sig_ready, hid_steps = sem("sig_ready"), sem("hid_steps")
        stored = sem("stored")
        tlin_out, small_done, row_out = sem("tlin_out"), sem("small_done"), sem("row_out")
        small_sum, small_out = sem("small_sum"), sem("small_out")
        dve_chain, act_chain = sem("dve_chain"), sem("act_chain")
        s_ready, max_done = sem("s_ready"), sem("max_done")
        max_turned, max_hi, max_lo = sem("max_turned"), sem("max_hi"), sem("max_lo")
        st_ready, e_done, w_done, pv_done, o_out = (sem("st_ready"), sem("e_done"), sem("w_done"), sem("pv_done"),
                                                    sem("o_out"))
        o_turned, o_hi, o_lo, qk_turned, qk_out = (sem("o_turned"), sem("o_hi"), sem("o_lo"), sem("qk_turned"),
                                                   sem("qk_out"))
        mx_ready, mx_pow = sem("mx_ready"), sem("mx_pow")
        ev = {}

        def event(name):
            if name not in ev:
                ev[name] = sem(name)
            return ev[name]

        T0 = stream.first
        UP = PADT + S
        rows_in, masks_in, small_in = cut(arena, 3264, S), cut(arena, 3264 + S, 6 * P), cut(arena, 4288, NSMALL)
        small_t = cut(work, 2048, S)
        k_odd = cut(work, 768, 4, S)
        fox = dict(u=cut(arena, 0, 4, UP), s1=cut(arena, 1088, 4, UP), s2=cut(arena, 2176, 4, UP),
                   q=cut(arena, 3264, 4, S), k=cut(arena, 4288, 4, S), v=cut(arena, 5312, NT, FOX_H, HD + 1),
                   pw=cut(arena, 6352, 4, P), diff=cut(arena, 6864, 4, S), o=cut(yf, 1024, NT, FOX_H * HD),
                   z=cut(yf, 0, 16), e=cut(yf, 16, 16), logf=cut(yf, 32, 16), nF=cut(yf, 48, NT, 8), nz=cut(yf, 64, 16),
                   nFT=cut(yf, 256, S), fix=cut(yf, 512, 64), bf=stat(FOX_H))
        mla = dict(q=cut(arena, 0, NT, MLA_H * QK), k=cut(arena, 3072, NT, MLA_H * QK),
                   v=cut(arena, 6144, NT, MLA_H, MLA_V + 1),
                   cin=cut(yf, 0, NT, MLA_IN), cn=cut(yf, 832, NT, Q_LORA + KV_LORA),
                   qkT=(cut(yf, 0, 4, 512), cut(work, 0, 4, 512)),
                   o=cut(arena, 3072, NT, MLA_H * QK)[:, :, 0:MLA_H * MLA_V],
                   PT=cut(arena, 0, NT, MLA_H * QK)[:, :, 0:TRI],
                   cos=stat(NT, 16), sin=stat(NT, 16), ss=stat(NT, 2), ms=stat(NT, 2), rs=stat(NT, 2),
                   rs_in=cut(yf, 1600, NT, 16), rc_in=cut(yf, 1632, NT, 16), ang=cut(yf, 1664, NT, 16),
                   turn=cut(yf, 1696, NT, 16), kr=cut(yf, 1760, NT, ROPE),
                   t1=cut(work, 0, 16, 16), t2=cut(work, 256, 16, 16), pos=stat(2), posi=stat(2))
        mls = dict(q=cut(arena, 0, 4, S), k=cut(arena, 1024, 4, S), v=cut(arena, 2048, NT, ML_H, ML_DV + 1),
                   og=cut(arena, 4112, KC, S), o=cut(arena, 6160, NT, ML_H, ML_DV + 1),
                   z=cut(yf, 0, NT, 16), F=cut(yf, 32, NT, 8), e=cut(yf, 48, NT, 8), logf=cut(yf, 64, NT, 8),
                   nz=cut(yf, 80, NT, 8), R=cut(yf, 96, NT, 8), den=cut(yf, 112, NT, 8),
                   ssq=cut(yf, 128, NT, 8), a=cut(yf, 144, NT, 8), b=cut(yf, 160, NT, 8), c=cut(yf, 176, NT, 8),
                   d=cut(yf, 192, NT, 8), m=cut(yf, 208, NT, 8), top=cut(yf, 512, 2, P + S), li=cut(yf, 1280, S),
                   bif=stat(2 * ML_H), junk=cut(work, 1792, P), sc=cut(work, 1024, 2, 512))
        nsa = dict(kS=cut(arena, 0, NKV, S), kW=cut(arena, 1024, NKV, S), kC=cut(arena, 2048, NKV, CP),
                   vS=cut(arena, 2176, NT, NKV, HD + 1), vW=cut(arena, 2696, NT, NKV, HD + 1),
                   vC=cut(arena, 7168, NKV, 4, HD),
                   kvc=cut(arena, 3712, NT, 8, P), cT=cut(arena, 5760, 8, S),
                   hkr=cut(work, 1024, 2, CMP_HID), hk=cut(work, 1536, 2, 2, 60), kcn=cut(work, 2100, P),
                   blk=cut(work, 0, 16, 60), ksw=cut(work, 1024, NT, 8, HD),
                   qd=cut(arena, 0, 16, 2, HD), q=cut(arena, 3712, NT, D), g=cut(arena, 5760, NT, 48), pc=cut(arena, 5856, NT, 4, CP),
                   cPT=cut(work, 768, NT, P), tmp=cut(work, 1792, 2, NT, HD), o=y[:],
                   ss=stat(32), ms=stat(32), rs=stat(32), sc=stat(2))
        ksw_dup = yf.rearrange("p (t g d n) -> p t g d n", t=NT, g=8, d=2)

        def raw_view(block, u):
            spec = stream.blocks[block][u]
            if spec == "ffn":
                shape = (2, D) if u == 2 else (KC, 256)
            else:
                shape = tuple(spec["src"].shape[1:])
            return raw[:, block % 2, u, 0:shape[0] * shape[1]].rearrange("p (c n) -> p c n", c=shape[0])

        def half_views(tile, u):
            block, t = tile // 2, tile % 2
            spec = stream.blocks[block][u]
            r = raw_view(block, u)
            if spec == "ffn":
                mode, shape = ("rows", (1, D)) if u == 2 else ("cols", (KC, P))
            else:
                mode, shape = spec["cut"], spec["half"]
            if mode == "rows":
                r = r[:, t * shape[0]:(t + 1) * shape[0], :]
            elif mode == "cols":
                r = r[:, :, t * shape[1]:(t + 1) * shape[1]]
            n = shape[0] * shape[1]
            view = lambda b: b[:, t, u, 0:n].rearrange("p (c n) -> p c n", c=shape[0])
            return r, view(wh), view(wl)

        def prepare_hi(tile, u, turn=None):
            if tile >= stream.tiles or not stream.real(tile, u):
                return
            r, hi, _ = half_views(tile, u)
            at = 0 if turn is None else turn
            nc.scalar.wait_ge(raw_landed[tile // 2 % 2][u], landing[tile // 2, u] + 16 * at)
            if slot_last[tile, u]:
                nc.scalar.wait_ge(used[u], slot_last[tile, u] + 4 * at)
            nc.scalar.activation(hi, r, ACT.Copy).then_inc(hi_done[u], 1)

        def prepare_lo(tile, u, turn=None):
            if tile >= stream.tiles or not stream.real(tile, u):
                return
            r, hi, lo = half_views(tile, u)
            at = 0 if turn is None else turn
            nc.vector.wait_ge(hi_done[u], n_of[tile, u] + 4 * at)
            nc.vector.tensor_tensor(lo, r, hi.bitcast(F32), ALU.subtract).then_inc(lo_done[u], 1)

        def mm3(o, sh, sl, rh, rl, start, stop):
            nc.tensor.matmul(o, sh, rh, start=start, stop=False)
            nc.tensor.matmul(o, sh, rl, start=False, stop=False)
            return nc.tensor.matmul(o, sl, rh, start=False, stop=stop)

        WOUT = {
            "fox": [(4, 2, 0), (5, 2, 1), (6, 0, 2), (7, 0, 3), (6, 1, 4), (7, 1, 5), (6, 2, 6), (7, 2, 7)],
            "mla": [(2, 2, 0), (3, 2, 1), (4, 0, 2), (5, 0, 3), (4, 1, 4), (5, 1, 5), (4, 2, 6), (5, 2, 7)],
            "mlstm": [(8, 0, 0), (8, 1, 2), (8, 2, 4), (9, 0, 1), (9, 1, 3), (9, 2, 5), (10, 0, 6), (11, 0, 7)],
            "nsa": [(2, 1, 0), (3, 1, 1), (2, 2, 2), (3, 2, 3), (4, 0, 4), (5, 0, 5), (4, 1, 6), (5, 1, 7)],
        }
        TLIN = {
            "fox": [(0, 0, "u", 0), (0, 1, "u", 2), (0, 2, "q", 0), (1, 0, "u", 1), (1, 1, "u", 3), (1, 2, "q", 1),
                    (2, 0, "q", 2), (2, 1, "k", 0), (2, 2, "k", 2), (3, 0, "q", 3), (3, 1, "k", 1), (3, 2, "k", 3)],
            "mlstm": [(0, 0, "q", 0), (0, 1, "q", 2), (0, 2, "k", 0), (1, 0, "q", 1), (1, 1, "q", 3), (1, 2, "k", 1),
                      (2, 0, "k", 2), (3, 0, "k", 3), (4, 2, "og", 0), (5, 2, "og", 1), (6, 0, "og", 2),
                      (6, 1, "og", 4), (6, 2, "og", 6), (7, 0, "og", 3), (7, 1, "og", 5), (7, 2, "og", 7)],
        }
        MLA_B = [(0, 2, 0, 0, 2), (1, 2, 0, 0, 2), (2, 0, 0, 0, 2),
                 (2, 1, 0, 2, 1), (2, 1, 1, 2, 1), (3, 1, 0, 2, 1), (3, 1, 1, 2, 1)]
        ROWS = {
            "fox": [(4, 0, 0, 2, 0), (4, 1, 4, 2, 0), (5, 0, 2, 2, 0), (5, 1, 6, 2, 0)],
            "mla": [(0, 0, 0, 2, 0), (0, 1, 4, 2, 0), (1, 0, 2, 2, 0), (1, 1, 6, 2, 0)],
            "mlstm": [(2, 1, 0, 1, 0), (2, 2, 2, 1, 0), (3, 1, 1, 1, 0), (3, 2, 3, 1, 0), (4, 0, 4, 1, 0),
                      (4, 1, 6, 1, 0), (5, 0, 5, 1, 0), (5, 1, 7, 1, 0)],
            "kv": [(0, 0, 0, 2, 0), (0, 1, 4, 2, 0), (0, 2, 0, 2, 1), (1, 0, 2, 2, 0), (1, 1, 6, 2, 0), (1, 2, 2, 2, 1),
                   (2, 0, 4, 2, 1), (2, 1, 0, 2, 2), (2, 2, 4, 2, 2), (3, 0, 6, 2, 1), (3, 1, 2, 2, 2),
                   (3, 2, 6, 2, 2)],
            "nsa": [(0, 0, 0, 1, 0), (0, 1, 2, 1, 0), (0, 2, 4, 1, 0), (1, 0, 1, 1, 0), (1, 1, 3, 1, 0), (1, 2, 5, 1, 0),
                    (2, 0, 6, 1, 0), (3, 0, 7, 1, 0)],
        }

        SCHED = {}
        step = group = 0
        for name, n in (("fox", FOX_H), ("mla", MLA_H), ("nsa", 2 * NQ)):
            SCHED[name] = (step, group, n // 4)
            step, group = step + n, group + n // 4
        WPV = {"fox": 0, "mla": FOX_H, "mlstm": FOX_H + MLA_H, "nsa": FOX_H + MLA_H + ML_H}
        OUT = {"fox": 0, "mla": 4, "mlstm": 12, "nsa": 20}

        def schedule(groups):
            yield "scores", 0
            for g in range(groups):
                if g + 1 < groups:
                    yield "scores", g + 1
                yield "turn", g
                yield "values", g

        def wait_half(eng, name, tile, u):
            eng.wait_ge(used[u], n_of[T0[name] + tile, u])

        def wait_rows(eng, name, g=0):
            tile, u = [e[:2] for e in ROWS[name] if e[4] == g][-1]
            wait_half(eng, name, tile, u)

        def wait_latent(eng, q):
            ends = [(g < 3 or w0 == 1) and i == 1 for g, (_, _, w0, _, _) in enumerate(MLA_B) for i in range(NT)]
            if ends[q]:
                wait_half(eng, "mla", *MLA_B[q // 2][:2])
            else:
                eng.wait_ge(event("mla_b_done"), q + 1 - sum(ends[:q]))

        block = ctx.enter_context(nc.Block())

        @block.sync
        def _(sp):
            x_tiles = W["x"].rearrange("b (t p) n -> (b t) p n", p=P)
            for t in range(NT):
                sp.dma_start(h[:, t, :], x_tiles[t]).then_inc(x_landed[t], 16)

            def load(block_no, u, src, turn=None):
                at = 0 if turn is None else turn
                if raw_last[block_no, u]:
                    sp.wait_ge(lo_done[u], raw_last[block_no, u] + 4 * at)
                sp.dma_start(raw_view(block_no, u), src).then_inc(raw_landed[block_no % 2][u], 16)

            def ffn_block(gate, up, down, base, b, turn=None):
                c0 = 256 * b if turn is None else 512 * turn + 256 * b
                for u, w in ((0, gate), (1, up)):
                    load(base + b, u, w.rearrange("(c p) n -> p c n", p=P)[:, :, bass.ds(c0, 256)], turn)
                load(base + b, 2, down[bass.ds(c0, 256), :].rearrange("(t p) n -> p t n", p=P), turn)

            def late_loads():
                sp.dma_start(masks_in, W["const"][:, NCONST:]).then_inc(masks_landed, 16)
                at = 0
                for name in list(GAIN_ROWS)[1:]:
                    first, n = GAIN_ROWS[name]
                    if name in ("k_norm_2", "b_q_norm_2"):
                        for d in (0, HD):
                            sp.dma_start(rows_in[first:first + n, d:d + HD], W[name]).then_inc(rows_landed, 16)
                            at += 16
                    else:
                        src = W[name]
                        if len(src.shape) == 1:
                            src = src.rearrange("(r p) -> r p", p=P)
                        elif src.shape[1] != P:
                            src = src.rearrange("a (r p) -> (a r) p", p=P)
                        sp.dma_start(rows_in[first:first + n, 0:P], src).then_inc(rows_landed, 16)
                        at += 16
                sp.dma_start(rows_in[0:32, P:2 * P], W["cmp_pe_2"].rearrange("k (j e) d -> (k j) (e d)", e=2)
                               ).then_inc(rows_landed, 16)
                at += 16
                assert at == ROWS_COUNT

            for name in PHASES:
                base = T0[name] // 2
                if name.startswith("ffn"):
                    f = int(name[3:])
                    if f < 4:
                        gate, up, down = (W[k][f // 2, f % 2] for k in ("ffn_w_gate", "ffn_w_up", "ffn_w_down"))
                    else:
                        w_in = W["ffn_w_in_2"][(f - 4) // 2, f % 2]
                        gate, up, down = w_in[:, 0:F], w_in[:, F:2 * F], W["ffn_w_out_2"][(f - 4) // 2, f % 2]
                    for b in range(3):
                        ffn_block(gate, up, down, base, b)
                    if name == "ffn0":
                        late_loads()
                    with sp.Fori(0, (FFN_BLOCKS - 3) // 2) as m:
                        for b in (3, 4):
                            ffn_block(gate, up, down, base, b, m)
                else:
                    for b, blk in enumerate(units[name]):
                        for u in KINDS:
                            if blk[u] is not None:
                                load(base + b, u, blk[u]["src"])

            out_tiles = out.rearrange("b (t p) n -> (b t) p n", p=P)
            for t in range(NT):
                sp.wait_ge(h_ready, READY["out"][t])
                sp.dma_start(out_tiles[t], h[:, t, :]).then_inc(stored, 16)
            sp.wait_ge(stored, 16 * NT)

        @block.gpsimd
        def _(pool):
            def row(dram, n):
                return dram.rearrange("(a n) -> a n", a=1).to_broadcast([P, n])

            def small_loads():
                for name, src in (("fox_f", W["ab_w_in"][:, 2048:2056]), ("ml_if", W["a_w_in_2"][:, 2048:2064]),
                                  ("nsa_g", W["b_w_in_2"][:, NQ * HD:NQ * HD + 3 * NQ])):
                    c0, n = SMALL[name]
                    pool.dma_start(small_in[:, c0:c0 + KC * n].rearrange("p (c n) -> p c n", n=n),
                                   src.rearrange("(c p) n -> p c n", p=P)).then_inc(small_landed, 16)
                pool.dma_start(fox["bf"], row(W["ab_b_forget"], FOX_H)).then_inc(small_landed, 16)
                pool.dma_start(mls["bif"], row(W["a_b_if_2"], 2 * ML_H)).then_inc(small_landed, 16)
                pool.dma_start(fox["pw"], W["pool_w"].rearrange("g p n -> p g n")).then_inc(small_landed, 16)
                pool.dma_start(w2[:], W["cmp_w2_2"].rearrange("k (c p) n -> p k c n", p=P)).then_inc(w2_landed, 16)
                pool.dma_start(mla["posi"].bitcast(I32), W["positions"].rearrange("b (t p) -> p (b t)", p=P), allow_slow_non_contiguous=True
                               ).then_inc(w2_landed, 16)


            def power(o, a, n, wait, count, done):
                pool.wait_ge(wait, count)
                nc.gpsimd.tensor_tensor(o, a, cst("neg_half")[0:a.shape[0], 0:n], ALU.pow).then_inc(done, 1)

            pool.wait_ge(const_landed, 16)
            for n, name in enumerate(NORMS):
                if name == "final":
                    pool.wait_ge(h_ready, READY["ffn3"][1])
                    pool.dma_start(arena[:, 0:D], row(W["norm_final"], D)).then_inc(gfin_landed, 16)
                for t in range(NT):
                    power(rstd[:, t:t + 1], meansq[:, t:t + 1], 1, ms_ready, NT * n + t + 1, rstd_ready)
                if n == 0:
                    small_loads()
                if name == "mla":
                    power(mla["rs"].rearrange("p a b -> p (a b)"), mla["ms"].rearrange("p a b -> p (a b)"), 4, mx_ready, 1, mx_pow)
                if name == "mlstm":
                    power(cut(yf, 192, 16), cut(yf, 144, 16), 16, mx_ready, 2, mx_pow)
                if name == "kv":
                    power(nsa["rs"][:, 0:16], nsa["ms"][:, 0:16], 16, mx_ready, 3, mx_pow)
                    power(nsa["rs"][0:60, 16:17], nsa["ms"][0:60, 16:17], 1, mx_ready, 4, mx_pow)
                if name == "nsa":
                    for t in range(NT):
                        power(nsa["rs"][:, 16 * t:16 * t + 16], nsa["ms"][:, 16 * t:16 * t + 16], 16, mx_ready, 5 + t, mx_pow)

        @block.tensor
        def _(pe):
            mm = nc.tensor.matmul

            def keep_clock(n):
                for _ in range(n):
                    mm(X[1][:, :], ident_r, const_r[:, 0:512], start=True, stop=True)

            def turn_norm(name):
                k = TRANSPOSED[name]
                n = NORM[name]
                if k == 0:
                    pe.wait_ge(const_landed, 16)
                else:
                    if k == 1:
                        pe.wait_ge(gain_ready, 3)
                    keep_clock(8)
                for t in range(NT):
                    pe.wait_ge((y0_ready, y1_ready)[t], k + 1)
                    for b in range(4):
                        for i in range(2):
                            c = 2 * b + i
                            last = nc.tensor.transpose(NB[b][:, i * S + t * P:i * S + (t + 1) * P],
                                                       y[:, t, c * P:(c + 1) * P], ident)
                        if t == 1:
                            last.then_inc(turned, 1)
                    if k:
                        keep_clock((3, 5)[t])

            def wait_chunk(name, i):
                pe.wait_ge(xlo_done, KC * TRANSPOSED[name] + i + 1)

            def late_rows():
                pe.wait_ge(rows_landed, ROWS_COUNT)
                nc.tensor.transpose(X[0][:, 0:NGAIN], rows_in[0:NGAIN, 0:P], ident[0:NGAIN, 0:NGAIN])
                nc.tensor.transpose(X[0][:, P:P + 32], rows_in[0:32, P:2 * P], ident[0:32, 0:32]).then_inc(rows_turned, 1)

            def ffn(name):
                f, base = int(name[3:]), T0[name]

                def gate_up(k, turn=None, first=False):
                    at = 0 if turn is None else 4 * turn
                    t = base + k
                    bank = G[k % 2]
                    if k >= 2:
                        pe.wait_ge(hid_steps, 4 * (FT * f + k - 1) + 4 * at)
                    for u in (0, 1):
                        _, sh, sl = half_views(t, u)
                        pe.wait_ge(lo_done[u], n_of[t, u] + at)
                        for i, c in enumerate(CHUNKS):
                            if first and u == 0:
                                wait_chunk(name, i)
                            last = mm3(bank[:, u * S:(u + 1) * S], sh[:, c, :], sl[:, c, :], xh[:, c, :], xl[:, c, :],
                                       i == 0, i == KC - 1)
                        last.then_inc(used[u], 1)

                def down(k, turn=None, start=False, stop=False):
                    at = 0 if turn is None else 4 * turn
                    if start:
                        wait_chunk(name, 7)
                    t = base + k
                    _, sh, sl = half_views(t, 2)
                    pe.wait_ge(lo_done[2], n_of[t, 2] + at)
                    pe.wait_ge(hid_steps, 4 * (FT * f + k + 1) + 4 * at)
                    for i in range(NT):
                        for n in range(2):
                            tok, col = slice(i * P, (i + 1) * P), slice(n * 512, (n + 1) * 512)
                            last = mm3(A[2 * i + n][:, :], hidh[:, k % 2, tok], hidl[:, k % 2, tok], sh[:, 0, col],
                                       sl[:, 0, col], start, stop)
                            if stop and 2 * i + n < 3:
                                last.then_inc(acc_done, 1)
                    last.then_inc(used[2], 1)

                gate_up(0, first=True)
                gate_up(1)
                down(0, start=True)
                with pe.Fori(0, LOOPS) as m:
                    for k in range(2, 6):
                        gate_up(k, m)
                        down(k - 1, m)
                if name == "ffn0":
                    late_rows()
                down(FT - 1, stop=True)

            tl = [0]

            def tlin(name, entry, firsts):
                tile, u, _, _ = entry
                t = T0[name] + tile
                _, sh, sl = half_views(t, u)
                q = tl[0]
                tl[0] += 1
                if q >= 4:
                    pe.wait_ge(tlin_out, q - 3)
                pe.wait_ge(lo_done[u], n_of[t, u])
                for i, c in enumerate(CHUNKS):
                    if firsts:
                        wait_chunk(name, i)
                    last = mm3(TB[q % 4][:, 0:S], sh[:, c, :], sl[:, c, :], xh[:, c, :], xl[:, c, :], i == 0, i == KC - 1)
                last.then_inc(used[u], 1)

            def rows(name, entry, banks, seen, total):
                tile, u, c0, nch, g = entry
                t = T0[name] + tile
                _, sh, sl = half_views(t, u)
                pe.wait_ge(lo_done[u], n_of[t, u])
                n = sh.shape[2]
                for j in range(nch):
                    c = c0 + j
                    start, stop = seen[g] == 0, seen[g] == total - 1
                    for i in range(NT):
                        for w0 in range(0, n, 512):
                            w1 = min(w0 + 512, n)
                            tok = slice(i * P, (i + 1) * P)
                            last = mm3(banks[g][i][w0 // 512][:, 0:w1 - w0], xh[:, c, tok], xl[:, c, tok],
                                       sh[:, j, w0:w1], sl[:, j, w0:w1], start, stop)
                    seen[g] += 1
                last.then_inc(used[u], 1)

            def small(k, key, bank, bank_cols):
                c0, n = SMALL[key]
                pe.wait_ge(small_ready, 1)
                sh = small_h[:, c0:c0 + KC * n].rearrange("p (c n) -> p c n", n=n)
                sl = small_l[:, c0:c0 + KC * n].rearrange("p (c n) -> p c n", n=n)
                for c in range(KC):
                    last = mm3(bank[0:n, 0:S], sh[:, c, :], sl[:, c, :], xh[:, c, :], xl[:, c, :], c == 0, c == KC - 1)
                last.then_inc(small_sum, 1)
                pe.wait_ge(small_out, k)
                for i in range(NT):
                    last = nc.tensor.transpose(bank_cols(i), small_t[0:n, i * P:(i + 1) * P], ident[0:n, 0:n])
                return last

            def w_out(name):
                for i, (tile, u, c) in enumerate(WOUT[name]):
                    t = T0[name] + tile
                    _, sh, sl = half_views(t, u)
                    pe.wait_ge(lo_done[u], n_of[t, u])
                    pe.wait_ge(o_lo, o_count(name, c))
                    for j in range(NT):
                        for n in range(2):
                            tok, col = slice(j * P, (j + 1) * P), slice(n * 512, (n + 1) * 512)
                            last = mm3(A[2 * j + n][:, :], mh[:, c, tok], ml[:, c, tok], sh[:, 0, col], sl[:, 0, col],
                                       i == 0, i == 7)
                            if i == 7 and 2 * j + n < 3:
                                last.then_inc(acc_done, 1)
                    last.then_inc(used[u], 1)

            def masked(bank, name, transposed):
                blocks = masks_r[name][:, 0:TRI] if transposed else masks_r[name][:, 2 * P:]
                return mm(bank[:, 0:TRI], ident_r, blocks, start=True, stop=False)

            def products(o, a, cols_a, b, cols_b, stop):
                a_parts = a if isinstance(a, tuple) else (a,)
                b_parts = b if isinstance(b, tuple) else (b,)
                pairs = [(x, z) for x in a_parts for z in b_parts]
                for n, (x, z) in enumerate(pairs):
                    last = mm(o, x[:, cols_a], z[:, cols_b], start=False, stop=stop and n == len(pairs) - 1)
                return last

            def row_sum(o, i, n, rows_):
                return mm(o, pick_r[0:32 + n, i:i + 1].to_broadcast([32 + n, P]), rows_, start=False, stop=False)

            def scores_of(bank, q, k, mask, rows_of=None):
                masked(bank, mask, False)
                for at, qs, n in ((0, slice(P, S), S), (S, slice(0, P), P)):
                    if rows_of:
                        rows_of(bank[:, at:at + n], slice(0, n))
                    last = products(bank[:, at:at + n], q, qs, k, slice(0, n), at == S)
                return last

            def transposed_scores(bank, q, k, mask, i, par):
                masked(bank, mask, True)
                for at, n, ks, qs in ((0, P, slice(P, S), slice(P, S)), (P, S, slice(0, P), slice(0, S))):
                    row_sum(bank[:, at:at + n], i, 4, hidh[0:36, par, qs])
                    last = products(bank[:, at:at + n], k, ks, q, qs, at == P)
                return last

            def weigh(bank, at, n, probs, v):
                mm(bank[:, at:at + n], probs[:, P:S], v[:, 0, :], start=True, stop=True)
                mm(bank[:, at + n:at + 2 * n], probs[:, S:TRI], v[:, 0, :], start=True, stop=False)
                return mm(bank[:, at + n:at + 2 * n], probs[:, 0:P], v[:, 1, :], start=False, stop=True)

            def attend(name, q_of, k_of, v_of, mask, probs, heads=None, rows_of=None, after=None,
                       group=None):
                s0, g0, groups = SCHED[name]
                w0, u0 = WPV[name], OUT[name]
                for what, g in schedule(groups):
                    if what == "scores":
                        if group:
                            group(g)
                        if heads:
                            heads(4 * g)
                        for i in range(4 * g, 4 * g + 4):
                            if heads and i % 4 < 3:
                                heads(i + 1)
                            if heads:
                                pe.wait_ge(qk_out, i + 1)
                            if s0 + i >= 2:
                                pe.wait_ge(max_done, s0 + i - 1)
                            row = rows_of and (lambda o, cols, i=i: rows_of(o, i, cols))
                            scores_of(G[i % 2], q_of(i), k_of(i), mask, row).then_inc(s_ready, 1)
                    if what == "turn":
                        pe.wait_ge(max_done, s0 + 4 * g + 4)
                        if w0 + 4 * g:
                            pe.wait_ge(e_done, w0 + 4 * g)
                        for t in range(NT):
                            for at in (0, 32):
                                last = mm(X[0][at:at + 4, t * P:(t + 1) * P], nmax[:, g % 2, t, :], ident, start=True,
                                          stop=True)
                        last.then_inc(max_turned, 1)
                        keep_clock(4)
                        pe.wait_ge(max_lo, g0 + g + 1)
                    if what == "values":
                        for i in range(4 * g, 4 * g + 5):
                            if i < 4 * g + 4:
                                if w0 + i >= 2:
                                    pe.wait_ge(e_done, w0 + i - 1)
                                transposed_scores(X[i % 2], q_of(i), k_of(i), mask, i % 4, g % 2).then_inc(st_ready, 1)
                            if i > 4 * g:
                                j = i - 1
                                pe.wait_ge(e_done, w0 + j + 1)
                                if j % 2 == 0 and j // 2 >= 2:
                                    pe.wait_ge(o_out, u0 + j // 2 - 1)
                                weigh(A[j // 2 % 2], 2 * (HD + 1) * (j % 2), HD + 1, probs(j), v_of(j)
                                      ).then_inc(pv_done, 1)
                        if after:
                            after(g)

            def turn_out(name, o, first, chunks):
                pe.wait_ge(o_out, OUT[name] + OUT_BANKS[name])
                pe.wait_ge(e_done, WPV[name] + STEPS[name])
                for b in range(chunks // 2):
                    for i in range(2):
                        c = 2 * b + i
                        for t in range(NT):
                            last = nc.tensor.transpose(TB[b][:, i * S + t * P:i * S + (t + 1) * P],
                                                       o[:, t, c * P:(c + 1) * P], ident)
                    last.then_inc(o_turned, 1)

            pe.wait_ge(const_landed, 16)
            pe.wait_ge(gain0_landed, 16)
            nc.tensor.transpose(X[0][:, 0:FIRST_GAINS], rows_in[0:FIRST_GAINS, 0:P], ident[0:FIRST_GAINS, 0:FIRST_GAINS]
                                ).then_inc(gain0_turned, 1)

            def fox_mixer():
                turn_norm("fox")
                for i, e in enumerate(TLIN["fox"]):
                    tlin("fox", e, i == 0)
                seen = [0]
                for e in ROWS["fox"]:
                    rows("fox", e, [[[A[0]], [A[1]]]], seen, KC)
                small(1, "fox_f", A[3], lambda i: A[2][:, 8 * i:8 * i + 8]).then_inc(small_done, 1)
                for g in range(4):
                    pe.wait_ge(tlin_out, tl[0] - 3 + g)
                    pe.wait_ge(event("fox_diff"), 1)
                    pe.wait_ge(small_landed, SMALL_COUNT)
                    mm(TB[g][:, 0:S], fox["pw"][:, g, :], fox["diff"][:, g, :], start=True, stop=True
                       ).then_inc(event("fox_pooled"), 1)
                pe.wait_ge(event("fox_logf"), 1)
                running_sums(fox["logf"].rearrange("p (t n) -> p t n", t=NT), A[2][:, 16:32], A[3],
                             event("fox_sums"))
                pe.wait_ge(event("fox_rows"), 1)
                pe.wait_ge(o_lo, 4)
                attend("fox", lambda i: fox["q"][:, i // 2, :],
                       lambda i: (fox["k"], k_odd)[i % 2][:, i // 2, :],
                       lambda i: fox["v"][:, :, i, :], "causal", lambda i: PT[:, i % 2, :],
                       rows_of=lambda o, i, cols: row_sum(o, i, FOX_H, xh[0:32 + FOX_H, 0, cols]))
                turn_out("fox", fox["o"], 4, 4)
                w_out("fox")

            def running_sums(logf, by_token, by_head, done, extra=None):
                mm(by_token[:, 0:8], tri[:, 0:P], logf[:, 0, 0:8], start=True, stop=True)
                mm(by_token[:, 8:16], tri[:, P:S], logf[:, 0, 0:8], start=True, stop=False)
                mm(by_token[:, 8:16], tri[:, 0:P], logf[:, 1, 0:8], start=False, stop=True)
                for at in (0, 32):
                    mm(by_head[at:at + 8, 0:S], logf[:, 0, 0:8], tri, start=True, stop=False)
                    last = mm(by_head[at:at + 8, P:S], logf[:, 1, 0:8], tri[:, 0:P], start=False, stop=True)
                last.then_inc(done, 1)

            def mla_mixer():
                turn_norm("mla")
                wait_chunk("mla", 7)
                seen = [0]
                for e in ROWS["mla"]:
                    rows("mla", e, [[[A[0]], [A[1]]]], seen, KC)
                pe.wait_ge(event("mla_cn"), 2)
                for c in range(3):
                    for t in range(NT):
                        last = nc.tensor.transpose(TB[c][:, t * P:(t + 1) * P],
                                                   mla["cn"][:, t, c * P:(c + 1) * P], ident)
                    last.then_inc(event("mla_c_turned"), 1)
                cTh, cTl = (b[:, 0:3 * S].rearrange("p (c s) -> p c s", c=3) for b in (mhf, mlf))
                pe.wait_ge(event("mla_c_lo"), 3)
                for g, (tile, u, w0, c0, nch) in enumerate(MLA_B):
                    t = T0["mla"] + tile
                    _, sh, sl = half_views(t, u)
                    pe.wait_ge(lo_done[u], n_of[t, u])
                    for i in range(NT):
                        q = 2 * g + i
                        if q >= 4:
                            pe.wait_ge(event("mla_b_out"), q - 3)
                        for j in range(nch):
                            tok, col = slice(i * P, (i + 1) * P), slice(512 * w0, 512 * (w0 + 1))
                            last = mm3(A[q % 4][:, :], cTh[:, c0 + j, tok], cTl[:, c0 + j, tok], sh[:, j, col],
                                       sl[:, j, col], j == 0, j == nch - 1)
                        if i == NT - 1 and (g < 3 or w0 == 1):
                            last.then_inc(used[u], 1)
                        else:
                            last.then_inc(event("mla_b_done"), 1)
                pe.wait_ge(event("mla_b_out"), 14)
                pe.wait_ge(event("mla_roped"), 1)

                def heads(i):
                    if i >= 2:
                        pe.wait_ge(qk_out, i - 1)
                    for b, src in enumerate((mla["q"], mla["q"], mla["k"], mla["k"])):
                        last = nc.tensor.transpose(A[2 + i % 2][0:QK, b * P:(b + 1) * P],
                                                   src[:, b % 2, QK * i:QK * (i + 1)], ident)
                    last.then_inc(qk_turned, 1)

                qkT = lambda i: mla["qkT"][i // 4 % 2][0:QK, i % 4, :]
                attend("mla", lambda i: qkT(i)[:, 0:S], lambda i: qkT(i)[:, S:2 * S], lambda i: mla["v"][:, :, i, :],
                       "chunk64", lambda i: mla["PT"][:, i % 2, :], heads=heads)
                turn_out("mla", mla["o"], 0, KC)
                w_out("mla")

            def mlstm_mixer():
                turn_norm("mlstm")
                seen = [0]
                by_tile = sorted([(e[0], e[1], "t", e) for e in TLIN["mlstm"]] +
                                 [(e[0], e[1], "r", e) for e in ROWS["mlstm"]], key=lambda x: x[:2])
                for i, (tile, u, what, e) in enumerate(by_tile):
                    if what == "t":
                        tlin("mlstm", e, i == 0)
                    else:
                        rows("mlstm", e, [[[A[0], A[1]], [A[2], A[3]]]], seen, KC)
                pe.wait_ge(row_out, ROW_OUT["mlstm"])
                small(2, "ml_if", A[3], lambda i: A[0][:, 16 * i:16 * i + 16]).then_inc(small_done, 1)
                pe.wait_ge(event("ml_logf"), 1)
                logf = mls["logf"]
                running_sums(logf, A[1][:, 0:16], A[2], event("ml_sums"))
                for t in range(NT):
                    for at in (0, 32):
                        last = mm(A[3][at:at + 8, t * P:(t + 1) * P], mls["z"][:, t, 0:8], ident, start=True, stop=True)
                last.then_inc(event("ml_sums"), 1)
                pe.wait_ge(event("ml_top"), 1)
                for t in range(NT):
                    last = nc.tensor.transpose(A[1][:, 32 + 8 * t:40 + 8 * t], mls["top"][0:8, 0, P + t * P:P + (t + 1) * P],
                                               ident[0:8, 0:8])
                last.then_inc(event("ml_top_turned"), 1)
                pe.wait_ge(event("ml_top_lo"), 1)
                pe.wait_ge(event("ml_top_out"), 1)
                pe.wait_ge(tlin_out, tl[0])
                w0 = WPV["mlstm"]
                for i in range(ML_H + 1):
                    if i < ML_H:
                        if i >= 2:
                            pe.wait_ge(w_done, i - 1)
                        q, k = mls["q"][:, i // 2, :], (mls["k"], k_odd)[i % 2][:, i // 2, :]
                        masked(G[i % 2], "causal", True)
                        for at, n, ks, qs in ((0, P, slice(P, S), slice(P, S)), (P, S, slice(0, P), slice(0, S))):
                            mm(G[i % 2][:, at:at + n], pick_r[0:40, i:i + 1].to_broadcast([40, P]), hidh[0:40, 0, qs],
                               start=False, stop=at == P)
                            last = mm(X[i % 2][:, at:at + n], k[:, ks], q[:, qs], start=True, stop=True)
                        last.then_inc(st_ready, 1)
                    if i >= 1:
                        j = i - 1
                        pe.wait_ge(w_done, j + 1)
                        if j >= 2:
                            pe.wait_ge(o_out, OUT["mlstm"] + j - 1)
                        weigh(A[j % 2], 0, ML_DV + 1, PT[:, j % 2, :], mls["v"][:, :, j, :]).then_inc(pv_done, 1)
                pe.wait_ge(event("ml_y"), 2)
                for b in range(4):
                    for i in range(2):
                        for t in range(NT):
                            last = nc.tensor.transpose(TB[b][:, i * S + t * P:i * S + (t + 1) * P],
                                                       mls["o"][:, t, 2 * b + i, 0:ML_DV], ident)
                    last.then_inc(event("ml_turned"), 1)
                w_out("mlstm")

            def kv_stage():
                turn_norm("kv")
                wait_chunk("kv", 7)
                seen = [0, 0, 0]
                banks = [[[A[0]], [A[1]]], [[A[2]], [A[3]]], [[X[0]], [X[1]]]]
                for e in ROWS["kv"]:
                    rows("kv", e, banks, seen, KC)
                pe.wait_ge(event("kv_c_out"), 2)
                pe.wait_ge(row_out, ROW_OUT["kv"])
                turn_banks = [A[0], A[1], A[2], A[3]]
                for b in range(4):
                    for i in range(2):
                        for t in range(NT):
                            last = nc.tensor.transpose(turn_banks[b][:, i * S + t * P:i * S + (t + 1) * P],
                                                       nsa["kvc"][:, t, 2 * b + i, :], ident)
                    last.then_inc(event("kv_c_turned"), 1)
                pe.wait_ge(event("kv_dup"), 2)
                for b, bank in enumerate((X[0], X[1], G[0], G[1])):
                    for i in range(2):
                        for t in range(NT):
                            last = nc.tensor.transpose(bank[:, i * S + t * P:i * S + (t + 1) * P],
                                                       ksw_dup[:, t, 2 * b + i, :, :].rearrange("p d n -> p (d n)"),
                                                       ident)
                    last.then_inc(event("kv_k_turned"), 1)
                pe.wait_ge(event("kv_k_out"), 4)
                pe.wait_ge(event("kv_c_cols"), 4)
                for kind, part in ((0, [(4, 0, 0), (5, 0, 4), (4, 1, 8), (5, 1, 12)]),
                                   (1, [(4, 2, 0), (5, 2, 4), (6, 0, 8), (7, 0, 12)])):
                    pe.wait_ge(event("kv_blk_lo"), kind + 1)
                    bh, bl = (b[:, 960 * kind:960 * (kind + 1)].rearrange("p (j r) -> p j r", r=60) for b in (mhf, mlf))
                    for tile, u, j0 in part:
                        t = T0["kv"] + tile
                        _, sh, sl = half_views(t, u)
                        pe.wait_ge(lo_done[u], n_of[t, u])
                        for j in range(4):
                            last = mm3((G[0], A[0])[kind][0:60, 0:CMP_HID], bh[:, j0 + j, :], bl[:, j0 + j, :], sh[:, j, :],
                                       sl[:, j, :], j0 + j == 0, j0 + j == 15)
                        last.then_inc(used[u], 1)
                pe.wait_ge(w2_landed, 32)
                for kind in range(2):
                    pe.wait_ge(event("kv_act"), kind + 1)
                    for c in range(2):
                        last = nc.tensor.transpose((G[1], A[1])[kind][:, 60 * c:60 * (c + 1)],
                                                   nsa["hkr"][0:60, kind, c * P:(c + 1) * P], ident[0:60, 0:60])
                    last.then_inc(event("kv_h_turned"), 1)
                pe.wait_ge(event("kv_hk"), 1)
                for c in range(2):
                    last = mm(A[2][0:60, 0:HD], nsa["hk"][:, 0, c, :], w2[:, 0, c, :], start=c == 0, stop=c == 1)
                last.then_inc(event("kv_k2"), 1)
                pe.wait_ge(event("kv_hk"), 2)
                for at in range(0, P, CP):
                    for g in range(NKV):
                        for c in range(2):
                            last = mm(A[3][at:at + NCMP, HD * g:HD * (g + 1)], nsa["hk"][:, 1, c, NCMP * g:NCMP * (g + 1)],
                                      w2[:, 1, c, :], start=c == 0, stop=c == 1)
                last.then_inc(event("kv_v2"), 1)
                pe.wait_ge(event("kv_kcn"), 1)
                nc.tensor.transpose(X[0][:, 0:60], nsa["kcn"][0:60, :], ident[0:60, 0:60]).then_inc(event("kv_kc"), 1)

            def nsa_mixer():
                turn_norm("nsa")
                wait_chunk("nsa", 7)
                seen = [0]
                for e in ROWS["nsa"]:
                    rows("nsa", e, [[[A[0], A[1]], [A[2], A[3]]]], seen, KC)
                pe.wait_ge(row_out, ROW_OUT["nsa"])
                small(3, "nsa_g", A[3], lambda i: A[0][:, 48 * i:48 * (i + 1)]).then_inc(small_done, 1)
                keep_clock(16)
                pe.wait_ge(event("nsa_q"), 2)
                pe.wait_ge(event("kv_done"), 5)

                pe.wait_ge(event("nsa_kc_lo"), 1)
                pe.wait_ge(event("nsa_k_lo"), 2)

                def head(i):
                    return 4 * (i // 8) + i % 4, i // 4 % 2

                def k_of(i):
                    h_, br = head(i)
                    return mh[:, 4 * br + h_ // 4, :]

                def q_of(i):
                    return tuple(b[:, 4 * (i // 8 % 2) + i % 4, :] for b in (xh, xl))

                def turn_queries(kvg):
                    pe.wait_ge(event("nsa_qd"), kvg + 1)
                    for b in range(2):
                        for a in range(2):
                            for t in range(NT):
                                twice = nsa["qd"][:, 8 * (kvg % 2) + 4 * t + 2 * b + a, :, :].rearrange("p d n -> p (d n)")
                                last = nc.tensor.transpose(A[2 + b][:, a * S + t * P:a * S + (t + 1) * P], twice, ident)
                        last.then_inc(event("nsa_qd_turned"), 1)

                def queries(g):
                    kvg = g // 2
                    if g == 0:
                        turn_queries(0)
                    if g % 2:
                        if kvg + 1 < NKV:
                            pe.wait_ge(event("nsa_pl"), kvg + 1)
                            turn_queries(kvg + 1)
                        return
                    if kvg:
                        pe.wait_ge(event("nsa_oc_out"), kvg)
                    pe.wait_ge(event("nsa_qd_lo"), 4 * kvg + 4)
                    for t in range(NT):
                        for a in range(4):
                            o = A[2][:, P * t + CP * a:P * t + CP * (a + 1)]
                            q1, q2 = (b[:, 4 * (kvg % 2) + a, t * P:(t + 1) * P] for b in (xh, xl))
                            kc = small_h[:, CP * kvg:CP * (kvg + 1)]
                            mm(o, q1, kc, start=True, stop=False)
                            last = mm(o, q2, kc, start=False, stop=True)
                    last.then_inc(event("nsa_sc"), 1)

                def v_of(i):
                    h_, br = head(i)
                    return (nsa["vS"], nsa["vW"])[br][:, :, h_ // 4, :]

                def compressed(g):
                    if g % 2:
                        return
                    kvg = g // 2
                    pe.wait_ge(event("nsa_pc"), kvg + 1)
                    if kvg + 1 < NKV:
                        pe.wait_ge(event("nsa_qd_lo"), 4 * kvg + 8)
                    for t in range(NT):
                        last = nc.tensor.transpose(A[2][:, t * P:(t + 1) * P],
                                                   nsa["pc"][:, t, :, :].rearrange("p h c -> p (h c)"), ident)
                    last.then_inc(event("nsa_pc_turned"), 1)
                    pe.wait_ge(event("nsa_pc_out"), kvg + 1)
                    for t in range(NT):
                        last = mm(A[3][:, t * S:(t + 1) * S], nsa["cPT"][:, t, :],
                                  nsa["vC"][:, kvg, :, :].rearrange("p h n -> p (h n)"), start=True, stop=True)
                    last.then_inc(event("nsa_oc"), 1)

                attend("nsa", q_of, k_of, v_of, "causal", lambda i: PT[:, i % 2, :],
                       after=compressed, group=queries)
                pe.wait_ge(event("nsa_o"), NQ // 2)
                turn_out("nsa", nsa["o"], 0, KC)
                w_out("nsa")

            mixers = dict(fox=fox_mixer, mla=mla_mixer, mlstm=mlstm_mixer, kv=kv_stage, nsa=nsa_mixer)
            for name in PHASES:
                if name.startswith("ffn"):
                    turn_norm(name)
                    ffn(name)
                else:
                    mixers[name]()

        @block.scalar
        def _(act):
            A_ = nc.scalar.activation
            chain = [0]

            def link(ins):
                chain[0] += 1
                ins.then_inc(act_chain, 1)
                act.wait_ge(act_chain, chain[0])

            act.dma_start(const[:], W["const"][:, 0:NCONST]).then_inc(const_landed, 16)
            first, n = GAIN_ROWS["norm_ffn"]
            act.dma_start(rows_in[first:first + n, 0:P], W["norm_ffn"].rearrange("a (r p) -> (a r) p", p=P)
                          ).then_inc(gain0_landed, 16)

            def prep(name, tile, kinds=KINDS):
                for u in kinds:
                    prepare_hi(T0[name] + tile, u)

            def leftover(name):
                if name in PHASES[1:]:
                    last = PHASES[PHASES.index(name) - 1]
                    if last.startswith("ffn"):
                        prep(last, FT, (2,))

            def norm(name):
                n = NORM[name]
                for t in range(NT):
                    if n == 0:
                        act.wait_ge(x_landed[t], 16)
                    else:
                        act.wait_ge(h_ready, READY[name][t])
                    A_(y[:, t, :], h[:, t, :], ACT.Square, accum_out=sumsq[:, t:t + 1]).then_inc(sq_done, 1)
                if name == "final":
                    return
                k = TRANSPOSED[name]
                act.wait_ge(rstd_ready, NT * n + 2)
                act.wait_ge(sq_done, NT * n + 2)
                A_(y[:, 1, :], h[:, 1, :], ACT.Copy, scale=rstd[:, 1:2]).then_inc(y1_ready, 1)
                leftover(name)
                gains = {"ffn": ("norm_ffn", KC * int(name[3:])) if name[:3] == "ffn" and int(name[3:]) < 4 else
                                ("ffn_norm_2", KC * (int(name[3:]) - 4)) if name[:3] == "ffn" else None,
                         "fox": ("norm_mix", 0), "mla": ("norm_mix", KC), "mls": ("mix_norm_2", 0),
                         "nsa": ("mix_norm_2", KC), "kv": ("kv_norm_2", 0)}[name[:3]]
                for i, c in enumerate(CHUNKS):
                    act.wait_ge(turned, 4 * k + c // 2 + 1)
                    if c % 2:
                        act.wait_ge(xlo_done, KC * k + CHUNKS.index(c - 1) + 1)
                    A_(xh[:, c, :], NB[c // 2][:, c % 2 * S:(c % 2 + 1) * S], ACT.Copy,
                       scale=gcol(gains[0], gains[1] + c)).then_inc(xhi_done, 1)

            def ffn(name):
                f, base = int(name[3:]), T0[name]

                def sigmoid(k, turn=None):
                    at = 0 if turn is None else 4 * turn
                    act.wait_ge(used[1], n_of[base + k, 1] + at)
                    if FT * f + k >= 2:
                        act.wait_ge(hid_steps, 4 * (FT * f + k - 1) + at * 4)
                    elif turn is not None:
                        act.wait_ge(hid_steps, 1 + at * 4)
                    A_(sig[:, k % 2, :], G[k % 2][:, 0:S], ACT.Sigmoid).then_inc(sig_ready, 1)

                prep(name, 1)
                sigmoid(0)
                with act.Fori(0, LOOPS) as m:
                    for k in range(2, 6):
                        prepare_hi(base + k, 0, m)
                        prepare_hi(base + k, 1, m)
                        sigmoid(k - 1, m)
                        prepare_hi(base + k, 2, m)
                prep(name, FT, (0, 1))
                sigmoid(FT - 1)

            tl = [0]

            def tlin_evac(name, entry, target, func=ACT.Copy, scale=1.0):
                q = tl[0]
                tl[0] += 1
                wait_half(act, name, *entry[:2])
                A_(target, TB[q % 4][:, 0:S], func, scale=scale).then_inc(tlin_out, 1)

            def small_evac(k, n):
                act.wait_ge(small_sum, k)
                A_(small_t[0:n, :], A[3][0:n, 0:S], ACT.Copy).then_inc(small_out, 1)

            def keys_evac(name, entry, even):
                q = tl[0]
                tl[0] += 1
                wait_half(act, name, *entry[:2])
                c = entry[3]
                A_(even[0:HD, c, :], TB[q % 4][0:HD, 0:S], ACT.Copy)
                A_(k_odd[HD:P, c, :], TB[q % 4][HD:P, 0:S], ACT.Copy).then_inc(tlin_out, 1)

            def attend(name, probs, heads=None, bias=None, after=None):
                s0, g0, groups = SCHED[name]
                w0 = WPV[name]
                for what, g in schedule(groups):
                    if what == "scores":
                        for i in range(4 * g, 4 * g + 4):
                            if heads:
                                heads(i)
                    if what == "turn":
                        act.wait_ge(max_turned, g0 + g + 1)
                        for at in (0, 32):
                            last = A_(hidh[at:at + 4, g % 2, :], X[0][at:at + 4, 0:S], ACT.Copy)
                        last.then_inc(max_hi, 1)
                    if what == "values":
                        for i in range(4 * g, 4 * g + 4):
                            act.wait_ge(st_ready, w0 + i + 1)
                            if i >= 2:
                                act.wait_ge(pv_done, w0 + i - 1)
                            if bias is None:
                                last = A_(probs(i), X[i % 2][:, 0:TRI], ACT.Exp)
                            else:
                                for t, at, n in ((0, P, S), (1, 0, P)):
                                    last = A_(probs(i)[:, at:at + n], X[i % 2][:, at:at + n], ACT.Exp, bias=bias(i, t))
                            last.then_inc(e_done, 1)
                        if after:
                            after(g)

            def split_out(name, chunks):
                for n, c in enumerate(x for x in CHUNKS if x < chunks):
                    act.wait_ge(o_turned, TURNED_BEFORE[name] + c // 2 + 1)
                    if c % 2:
                        act.wait_ge(o_lo, o_count(name, c - 1 + KC - chunks))
                    A_(mh[:, c + KC - chunks, :], TB[c // 2][:, c % 2 * S:(c % 2 + 1) * S], ACT.Copy).then_inc(o_hi, 1)

            act.wait_ge(gain0_turned, 1)
            A_(gain[:, 0:FIRST_GAINS], X[0][:, 0:FIRST_GAINS], ACT.Copy).then_inc(gain_ready, 1)
            act.wait_ge(gain_ready, 1)

            def small_weights():
                act.wait_ge(rows_turned, 1)
                A_(gain[:, FIRST_GAINS:], X[0][:, FIRST_GAINS:NGAIN], ACT.Copy)
                A_(const_r[:, 0:P + 8], const[:, 0:P + 8], ACT.Copy)
                act.wait_ge(masks_landed, 16)
                for i, name in enumerate(MASKS):
                    src, dst = masks_in[:, 3 * P * i:3 * P * (i + 1)], masks_r[name]
                    A_(dst[:, P:4 * P], src, ACT.Copy)
                    A_(dst[:, 0:P], src[:, 0:P], ACT.Copy)
                    last = A_(dst[:, 4 * P:], src[:, 2 * P:], ACT.Copy)
                last.then_inc(gain_ready, 1)
                A_(pe_col[:], X[0][:, P:P + 32], ACT.Copy).then_inc(gain_ready, 1)
                act.wait_ge(small_landed, SMALL_COUNT)
                for i, (c0, n) in enumerate(SMALL.values()):
                    A_(small_h[:, c0:c0 + KC * n], small_in[:, c0:c0 + KC * n], ACT.Copy).then_inc(small_hi, 1)

            def fox_mixer():
                norm("fox")
                entries = TLIN["fox"]
                for tile in range(4):
                    prep("fox", tile + 1)
                    for e in entries[3 * tile:3 * tile + 3]:
                        _, _, what, c = e
                        if what == "k":
                            keys_evac("fox", e, fox["k"])
                            continue
                        dst = fox[what][:, c, :] if what != "u" else fox["u"][:, c, PADT:]
                        tlin_evac("fox", e, dst, scale=FOX_D ** -0.5 if what == "q" else 1.0)
                prep("fox", 5)
                prep("fox", 6, (0, 1))
                prep("fox", 7, (0, 1))
                wait_rows(act, "fox")
                for t in range(NT):
                    last = A_(fox["v"][:, t, :, 0:HD], A[t][:, :].rearrange("p (h n) -> p h n", n=HD), ACT.Copy)
                last.then_inc(row_out, 1)
                small_evac(1, FOX_H)
                act.wait_ge(event("fox_nz"), 1)
                link(A_(fox["e"], fox["nz"], ACT.Exp))
                A_(fox["e"], fox["e"], ACT.Ln, bias=1.0).then_inc(event("fox_ln"), 1)
                for g in range(4):
                    act.wait_ge(event("fox_pooled"), g + 1)
                    A_(mh[:, g, :], TB[g][:, 0:S], ACT.Copy, scale=gcol("pool_scale", g)).then_inc(o_hi, 1)
                act.wait_ge(event("fox_sums"), 1)
                for at in (0, 32):
                    last = A_(xh[at:at + FOX_H, 0, :], A[3][at:at + FOX_H, 0:S], ACT.Copy, scale=-1.0)
                last.then_inc(event("fox_sums_hi"), 1)
                act.wait_ge(event("fox_rows"), 1)
                attend("fox", lambda i: PT[:, i % 2, :], bias=lambda i, t: fox["nF"][:, t, i:i + 1])
                split_out("fox", 4)
                prep("fox", 6, (2,))
                prep("fox", 7, (2,))
                prep("fox", 8)

            def mla_mixer():
                norm("mla")
                prep("mla", 1)
                prep("mla", 2, (0, 1))
                wait_rows(act, "mla")
                for t in range(NT):
                    A_(mla["cin"][:, t, :], A[t][:, 0:MLA_IN], ACT.Copy).then_inc(event("mla_cin"), 1)
                act.wait_ge(event("mla_cin"), 2)
                for t in range(NT):
                    for i, (c0, c1) in enumerate(((0, Q_LORA), (Q_LORA, Q_LORA + KV_LORA))):
                        A_(mla["cn"][:, t, c0:c1], mla["cin"][:, t, c0:c1], ACT.Square,
                           accum_out=mla["ss"][:, t, i:i + 1]).then_inc(event("mla_sq"), 1)
                act.wait_ge(event("mla_ang"), 2)
                A_(mla["sin"], mla["rs_in"], ACT.Sin).then_inc(event("mla_cs"), 1)
                A_(mla["cos"], mla["rc_in"], ACT.Sin).then_inc(event("mla_cs"), 1)
                for c in range(3):
                    act.wait_ge(event("mla_c_turned"), c + 1)
                    g = gcol("mla_q_norm", c) if c < 2 else gcol("mla_kv_norm", 0)
                    A_(mhf[:, c * S:(c + 1) * S], TB[c][:, 0:S], ACT.Copy, scale=g).then_inc(event("mla_c_hi"), 1)
                for g in range(7):
                    if g < 3:
                        for t in range(NT):
                            q = 2 * g + t
                            wait_latent(act, q)
                            A_(mla["q"][:, t, 512 * g:512 * (g + 1)], A[q % 4][:, :], ACT.Copy, scale=QK ** -0.5
                               ).then_inc(event("mla_b_out"), 1)
                    else:
                        for t in range(NT):
                            q = 2 * g + t
                            h0 = 4 * (g - 3)
                            wait_latent(act, q)
                            src = A[q % 4][:, :].rearrange("p (h n) -> p h n", h=4)
                            k = mla["k"][:, t, :].rearrange("p (h n) -> p h n", n=QK)[:, h0:h0 + 4, 0:NOPE]
                            v = mla["v"][:, t, h0:h0 + 4, 0:MLA_V]
                            A_(k, src[:, :, 0:NOPE], ACT.Copy)
                            A_(v, src[:, :, NOPE:], ACT.Copy).then_inc(event("mla_b_out"), 1)
                    if g == 0:
                        prep("mla", 2, (2,))
                        prep("mla", 3)
                    if g == 3:
                        prep("mla", 4, (0,))
                    if g == 5:
                        prep("mla", 4, (1,))
                        prep("mla", 5, (0,))
                act.wait_ge(event("mla_roped"), 1)

                def heads(i):
                    act.wait_ge(qk_turned, i + 1)
                    if i >= 8:
                        act.wait_ge(st_ready, WPV["mla"] + 4 * (i // 4 - 1))
                    A_(mla["qkT"][i // 4 % 2][0:QK, i % 4, :], A[2 + i % 2][0:QK, :], ACT.Copy).then_inc(qk_out, 1)

                attend("mla", lambda i: mla["PT"][:, i % 2, :], heads=heads)
                split_out("mla", KC)
                prep("mla", 4, (2,))
                prep("mla", 5, (1, 2))
                prep("mla", 6)

            def mlstm_mixer():
                norm("mlstm")
                by = {}
                for e in TLIN["mlstm"]:
                    by.setdefault(e[0], []).append(e)
                for tile in range(8):
                    prep("mlstm", tile + 1)
                    for e in by.get(tile, []):
                        _, _, what, c = e
                        if what == "k":
                            keys_evac("mlstm", e, mls["k"])
                            continue
                        tlin_evac("mlstm", e, mls[what][:, c, :], ACT.Sigmoid if what == "og" else ACT.Copy,
                                  ML_DK ** -0.5 if what == "q" else 1.0)
                    if tile == 5:
                        wait_rows(act, "mlstm")
                        for t in range(NT):
                            for n in range(2):
                                last = A_(mls["v"][:, t, 4 * n:4 * n + 4, 0:ML_DV],
                                          A[2 * t + n][:, :].rearrange("p (h n) -> p h n", n=ML_DV), ACT.Copy)
                        last.then_inc(row_out, 1)
                small_evac(2, 2 * ML_H)
                prep("mlstm", 9)
                act.wait_ge(event("ml_nz"), 1)
                link(A_(mls["e"], mls["nz"], ACT.Exp))
                A_(mls["e"], mls["e"], ACT.Ln, bias=1.0).then_inc(event("ml_ln"), 1)

                act.wait_ge(event("ml_top"), 1)
                for at in (0, 32):
                    last = A_(hidh[at:at + ML_H, 0, :], mls["top"][at:at + ML_H, 0, P:], ACT.Copy, scale=-1.0)
                last.then_inc(event("ml_top_hi"), 1)
                act.wait_ge(event("ml_top_out"), 1)
                A_(mls["b"], mls["m"], ACT.Exp, scale=-1.0).then_inc(event("ml_em"), 1)
                w0 = WPV["mlstm"]
                for i in range(ML_H + 1):
                    if i < ML_H:
                        act.wait_ge(st_ready, w0 + i + 1)
                        if i >= 2:
                            act.wait_ge(pv_done, w0 + i - 1)
                        for t, at, n in ((0, P, S), (1, 0, P)):
                            last = A_(PT[:, i % 2, at:at + n], G[i % 2][:, at:at + n], ACT.Exp, bias=mls["R"][:, t, i:i + 1])
                        last.then_inc(e_done, 1)
                    if i >= 1:
                        j = i - 1
                        act.wait_ge(pv_done, w0 + j + 1)
                        A_(mls["o"][:, :, j, :], A[j % 2][:, 0:2 * (ML_DV + 1)].rearrange("p (t n) -> p t n", t=NT),
                           ACT.Copy).then_inc(o_out, 1)
                        act.wait_ge(o_out, OUT["mlstm"] + j + 1)
                        for t in range(NT):
                            if t + j:
                                act.wait_ge(event("ml_sq"), NT * j + t)
                            A_(mls["junk"], mls["o"][:, t, j, 0:ML_DV], ACT.Square, accum_out=mls["ssq"][:, t, j:j + 1]
                               ).then_inc(event("ml_sq"), 1)
                for b in range(4):
                    for i in range(2):
                        c = 2 * b + i
                        act.wait_ge(event("ml_mix"), c + 1)
                        A_(mh[:, c, :], mls["sc"][:, c % 2, 0:S], ACT.Copy).then_inc(o_hi, 1)
                prep("mlstm", 10)
                prep("mlstm", 11)
                prep("mlstm", 12)

            def kv_stage():
                norm("kv")
                for tile in range(1, 4):
                    prep("kv", tile)
                wait_rows(act, "kv", 0)
                for t in range(NT):
                    for d in range(2):
                        last = A_(nsa["kvc"][:, t, :, HD * d:HD * (d + 1)],
                                  A[t][:, :].rearrange("p (g n) -> p g n", n=HD), ACT.Copy)
                    last.then_inc(event("kv_c_out"), 1)
                for br, (banks, v) in enumerate((((A[2], A[3]), nsa["vS"]), ((X[0], X[1]), nsa["vW"]))):
                    wait_rows(act, "kv", 1 + br)
                    for t in range(NT):
                        A_(nsa["ksw"][:, t, 4 * br:4 * br + 4, :], banks[t][:, 0:S].rearrange("p (g n) -> p g n", n=HD),
                           ACT.Copy).then_inc(event("kv_ksw"), 1)
                        last = A_(v[:, t, :, 0:HD], banks[t][:, S:2 * S].rearrange("p (g n) -> p g n", n=HD), ACT.Copy)
                    last.then_inc(row_out, 1)
                prep("kv", 4)
                prep("kv", 5)
                for b in range(4):
                    act.wait_ge(event("kv_c_turned"), b + 1)
                    src = A[b][:, :].rearrange("p (g s) -> p g s", g=2)
                    dst = nsa["cT"][:, 2 * b:2 * b + 2, :]
                    A_(dst[0:HD, :, :], src[0:HD, :, :], ACT.Copy)
                    A_(dst[HD:P, :, 0:S - 1], src[HD:P, :, 1:S], ACT.Copy).then_inc(event("kv_c_cols"), 1)
                for b, bank in enumerate((X[0], X[1], G[0], G[1])):
                    act.wait_ge(event("kv_k_turned"), b + 1)
                    dst = (nsa["kS"], nsa["kW"])[b // 2][:, 2 * (b % 2):2 * (b % 2) + 2, :]
                    A_(dst, bank[:, :].rearrange("p (g s) -> p g s", g=2), ACT.Copy,
                       scale=gcol("k_norm_2", 1 + b // 2)).then_inc(event("kv_k_out"), 1)
                for kind in range(2):
                    act.wait_ge(event("kv_blk"), kind + 1)
                    A_(mhf[:, 960 * kind:960 * (kind + 1)], nsa["blk"].rearrange("p j r -> p (j r)"), ACT.Copy
                       ).then_inc(event("kv_blk_hi"), 1)
                prep("kv", 6)
                for kind in range(2):
                    wait_half(act, "kv", *((5, 1), (7, 0))[kind])
                    A_(nsa["hkr"][0:60, kind, :], (G[0], A[0])[kind][0:60, 0:CMP_HID], ACT.Sigmoid).then_inc(event("kv_sig"), 1)
                    if kind == 0:
                        prep("kv", 7)
                for kind in range(2):
                    act.wait_ge(event("kv_h_turned"), kind + 1)
                    A_(nsa["hk"][:, kind, :, :].rearrange("p c n -> p (c n)"), (G[1], A[1])[kind][:, 0:120], ACT.Copy
                       ).then_inc(event("kv_hk"), 1)
                act.wait_ge(event("kv_k2"), 1)
                A_(nsa["kcn"][0:60, 0:HD], A[2][0:60, 0:HD], ACT.Square, accum_out=nsa["ss"][0:60, 16:17]
                   ).then_inc(event("kv_k2sq"), 1)
                act.wait_ge(event("kv_v2"), 1)
                act.wait_ge(event("kv_zero"), 2)
                for r in range(4):
                    at = slice(CP * r, CP * r + NCMP)
                    A_(nsa["vC"][at, :, r, :], A[3][at, 0:S].rearrange("p (g n) -> p g n", n=HD), ACT.Copy
                       ).then_inc(event("kv_done"), 1)
                act.wait_ge(event("kv_kc"), 1)
                A_(nsa["kC"][:, :, 0:NCMP], X[0][:, 0:60].rearrange("p (g c) -> p g c", g=NKV), ACT.Copy,
                   scale=gcol("k_norm_2", 0)).then_inc(event("kv_done"), 1)
                prep("kv", 8)

            def nsa_mixer():
                norm("nsa")
                prep("nsa", 1)
                prep("nsa", 2)
                prep("nsa", 3)
                for b, k in enumerate((nsa["kS"], nsa["kW"])):
                    A_(mh[:, 4 * b:4 * b + 4, :], k, ACT.Copy).then_inc(event("nsa_k_hi"), 1)
                wait_rows(act, "nsa")
                for t in range(NT):
                    for n in range(2):
                        last = A_(nsa["q"][:, t, 512 * n:512 * (n + 1)], A[2 * t + n][:, :], ACT.Copy)
                last.then_inc(row_out, 1)
                small_evac(3, 3 * NQ)
                prep("nsa", 4, (0,))
                prep("nsa", 5, (0,))
                act.wait_ge(small_done, 3)
                for t in range(NT):
                    last = A_(nsa["g"][:, t, :], A[0][:, 48 * t:48 * (t + 1)], ACT.Sigmoid)
                last.then_inc(event("nsa_gates"), 1)

                A_(small_h[:, 0:NKV * CP], nsa["kC"].rearrange("p g c -> p (g c)"), ACT.Copy).then_inc(event("nsa_kc_hi"), 1)
                act.wait_ge(event("nsa_scale"), 1)
                def compressed(g):
                    if g % 2 == 0:
                        act.wait_ge(event("nsa_pc_turned"), g // 2 + 1)
                        A_(nsa["cPT"], A[2][:, 0:S].rearrange("p (t n) -> p t n", t=NT), ACT.Copy
                           ).then_inc(event("nsa_pc_out"), 1)

                def twice(kvg):
                    for t in range(NT):
                        act.wait_ge(event("nsa_q"), t + 1)
                        src = nsa["q"][:, t, S * kvg:S * (kvg + 1)].rearrange("p (h n) -> p h n", n=HD)
                        at = 8 * (kvg % 2) + 4 * t
                        last = A_(nsa["qd"][:, at:at + 4, :, :], src.unsqueeze(2).to_broadcast([P, 4, 2, HD]), ACT.Copy)
                    last.then_inc(event("nsa_qd"), 1)

                act.wait_ge(event("nsa_k_lo"), 2)
                twice(0)

                def queries_hi(kvg):
                    for n, a in enumerate((0, 2, 1, 3)):
                        act.wait_ge(event("nsa_qd_turned"), 2 * kvg + a // 2 + 1)
                        if a % 2:
                            act.wait_ge(event("nsa_qd_lo"), 4 * kvg + n - 1)
                        A_(xh[:, 4 * (kvg % 2) + a, :], A[2 + a // 2][:, a % 2 * S:(a % 2 + 1) * S], ACT.Copy,
                           scale=nsa["sc"][:, 0:1]).then_inc(event("nsa_qd_hi"), 1)
                    if kvg + 1 < NKV:
                        twice(kvg + 1)

                def queries(i):
                    if i % 4:
                        return
                    g = i // 4
                    if g == 0:
                        queries_hi(0)
                    if g % 2 == 0:
                        act.wait_ge(event("nsa_pl"), g // 2 + 1)
                        A_(nsa["pc"], nsa["pc"], ACT.Exp).then_inc(event("nsa_pe"), 1)
                    elif g // 2 + 1 < NKV:
                        queries_hi(g // 2 + 1)

                attend("nsa", lambda i: PT[:, i % 2, :], heads=queries, after=compressed)
                split_out("nsa", KC)
                prep("nsa", 4, (1,))
                prep("nsa", 5, (1,))
                prep("nsa", 6)

            mixers = dict(fox=fox_mixer, mla=mla_mixer, mlstm=mlstm_mixer, kv=kv_stage, nsa=nsa_mixer)
            for name in PHASES:
                if name == "ffn4":
                    norm("final")
                if name.startswith("ffn"):
                    norm(name)
                    if name == "ffn0":
                        prep(name, 0)
                    ffn(name)
                    if name == "ffn0":
                        small_weights()
                else:
                    mixers[name]()

        @block.vector
        def _(dve):
            V = nc.vector
            chain = [0]

            def link(ins):
                chain[0] += 1
                ins.then_inc(dve_chain, 1)
                dve.wait_ge(dve_chain, chain[0])

            def prep(name, tile, kinds=KINDS):
                for u in kinds:
                    prepare_lo(T0[name] + tile, u)

            def wide(ap, *shape):
                return ap.to_broadcast([ap.shape[0], *shape])

            def residual(name, scale):
                r = RESIDUAL[name]
                for t in range(NT):
                    for n in range(2):
                        i = 2 * t + n
                        if i < 3:
                            dve.wait_ge(acc_done, 3 * r + i + 1)
                        else:
                            wait_half(dve, name, *((FT - 1, 2) if name[:3] == "ffn" else WOUT[name][-1][:2]))
                        col = h[:, t, 512 * n:512 * (n + 1)]
                        V.scalar_tensor_tensor(col, A[i][:, :], scale, col, ALU.mult, ALU.add).then_inc(h_ready, 1)

            def leftover(name):
                if name in PHASES[1:]:
                    last = PHASES[PHASES.index(name) - 1]
                    if last.startswith("ffn"):
                        prep(last, FT, (2,))

            def norm(name):
                n = NORM[name]
                for t in range(NT):
                    dve.wait_ge(sq_done, NT * n + t + 1)
                    V.tensor_scalar(meansq[:, t:t + 1], sumsq[:, t:t + 1], 1.0 / D, EPS, ALU.mult, ALU.add
                                    ).then_inc(ms_ready, 1)
                    if t == 0 and name != "final":
                        dve.wait_ge(rstd_ready, NT * n + 1)
                        V.tensor_scalar(y[:, 0, :], h[:, 0, :], rstd[:, 0:1], None, ALU.mult).then_inc(y0_ready, 1)
                if name == "final":
                    dve.wait_ge(gfin_landed, 16)
                    for t in range(NT):
                        dve.wait_ge(rstd_ready, NT * n + t + 1)
                        V.scalar_tensor_tensor(h[:, t, :], h[:, t, :], rstd[:, t:t + 1], arena[:, 0:D], ALU.mult, ALU.mult
                                               ).then_inc(h_ready, 1)
                    return
                k = TRANSPOSED[name]
                leftover(name)
                f = int(name[3:]) if name[:3] == "ffn" else -1
                g, g0 = (("norm_ffn", KC * f) if 0 <= f < 4 else ("ffn_norm_2", KC * (f - 4)) if f >= 4 else
                         {"fox": ("norm_mix", 0), "mla": ("norm_mix", KC), "mlstm": ("mix_norm_2", 0),
                          "nsa": ("mix_norm_2", KC), "kv": ("kv_norm_2", 0)}[name])
                for i, c in enumerate(CHUNKS):
                    dve.wait_ge(xhi_done, KC * k + i + 1)
                    V.scalar_tensor_tensor(xl[:, c, :], NB[c // 2][:, c % 2 * S:(c % 2 + 1) * S], gcol(g, g0 + c),
                                           xh[:, c, :].bitcast(F32), ALU.mult, ALU.subtract).then_inc(xlo_done, 1)

            def small_weights():
                for i, (c0, n) in enumerate(SMALL.values()):
                    dve.wait_ge(small_hi, i + 1)
                    last = V.tensor_tensor(small_l[:, c0:c0 + KC * n], small_in[:, c0:c0 + KC * n],
                                           small_h[:, c0:c0 + KC * n].bitcast(F32), ALU.subtract)
                last.then_inc(small_ready, 1)

            def ffn(name):
                f, base = int(name[3:]), T0[name]

                def hidden(k, turn=None):
                    at = 0 if turn is None else 4 * turn
                    n, bank = FT * f + k, G[k % 2]
                    dve.wait_ge(sig_ready, n + 1 + at)
                    if n >= 1:
                        dve.wait_ge(hid_steps, 4 * n + 4 * at)
                    V.tensor_tensor(gated, bank[:, 0:S], sig[:, k % 2, :], ALU.mult).then_inc(hid_steps, 1)
                    dve.wait_ge(hid_steps, 4 * n + 1 + 4 * at)
                    V.tensor_tensor(hid, bank[:, S:2 * S], gated, ALU.mult).then_inc(hid_steps, 1)
                    dve.wait_ge(hid_steps, 4 * n + 2 + 4 * at)
                    V.tensor_copy(hidh[:, k % 2, :], hid).then_inc(hid_steps, 1)
                    dve.wait_ge(hid_steps, 4 * n + 3 + 4 * at)
                    V.tensor_tensor(hidl[:, k % 2, :], hid, hidh[:, k % 2, :].bitcast(F32), ALU.subtract
                                    ).then_inc(hid_steps, 1)

                prep(name, 1)
                hidden(0)
                with dve.Fori(0, LOOPS) as m:
                    for k in range(2, 6):
                        prepare_lo(base + k, 0, m)
                        prepare_lo(base + k, 1, m)
                        hidden(k - 1, m)
                        prepare_lo(base + k, 2, m)
                prep(name, FT, (0, 1))
                hidden(FT - 1)
                if name == "ffn0":
                    small_weights()
                residual(name, 0.5)

            def low(dst, src, hi, done):
                return V.tensor_tensor(dst, src, hi.bitcast(F32), ALU.subtract).then_inc(done, 1)

            def attend(name, o, gate=None, between=None, heads=None, after=None):
                s0, g0, groups = SCHED[name]
                w0, u0 = WPV[name], OUT[name]
                for what, g in schedule(groups):
                    if what == "scores":
                        if heads:
                            heads(g)
                        for i in range(4 * g, 4 * g + 4):
                            dve.wait_ge(s_ready, s0 + i + 1)
                            for t, at, n in ((0, S, P), (1, 0, S)):
                                last = V.tensor_reduce(nmax[:, g % 2, t, i % 4:i % 4 + 1], G[i % 2][:, at:at + n], AX.X,
                                                       ALU.max, negate=True)
                            last.then_inc(max_done, 1)
                        if between:
                            between(g)
                    if what == "turn":
                        dve.wait_ge(max_hi, g0 + g + 1)
                        low(hidh[32:36, g % 2, :], X[0][32:36, 0:S], hidh[32:36, g % 2, :], max_lo)
                    if what == "values":
                        for p in (2 * g, 2 * g + 1):
                            dve.wait_ge(pv_done, w0 + 2 * p + 2)
                            values = A[p % 2][:, 0:4 * (HD + 1)].rearrange("p (a t n) -> p a t n", a=2, t=NT)
                            z = zinv.rearrange("p (a t) -> p a t", a=2)
                            if u0 + p:
                                dve.wait_ge(o_out, u0 + p)
                            link(V.reciprocal(z, values[:, :, :, HD]))
                            if gate:
                                gate(p, values, z)
                            else:
                                part = o[:, :, P * p:P * (p + 1)].rearrange("p t (a n) -> p a t n", a=2)
                                V.tensor_tensor(part, values[:, :, :, 0:HD], wide(z.unsqueeze(3), 2, NT, HD), ALU.mult
                                                ).then_inc(o_out, 1)
                        if after:
                            after(g)

            def split_out(name, chunks):
                for c in (x for x in CHUNKS if x < chunks):
                    to = c + KC - chunks
                    dve.wait_ge(o_hi, o_count(name, to))
                    low(ml[:, to, :], TB[c // 2][:, c % 2 * S:(c % 2 + 1) * S], mh[:, to, :], o_lo)

            def fox_mixer():
                norm("fox")
                V.memset(fox["v"][:, :, :, HD:], 1.0)
                V.memset(fox["k"][HD:P, :, :], 0.0)
                V.memset(k_odd[0:HD, :, :], 0.0)
                prep("fox", 1)
                prep("fox", 2)
                dve.wait_ge(tlin_out, 5)
                u, s1, s2, df, fix = (fox[k] for k in ("u", "s1", "s2", "diff", "fix"))
                body = slice(PADT, UP)
                back = lambda x, n: x[:, :, PADT - n:UP - n]
                link(V.tensor_tensor(s1[:, :, body], u[:, :, body], back(u, 1), ALU.add))
                link(V.tensor_tensor(s2[:, 1:4, body], s1[:, 1:4, body], back(s1[:, 1:4, :], 2), ALU.add))
                link(V.tensor_tensor(s1[:, 2:4, body], s2[:, 2:4, body], back(s2[:, 2:4, :], 4), ALU.add))
                link(V.tensor_tensor(s2[:, 3:4, body], s1[:, 3:4, body], back(s1[:, 3:4, :], 8), ALU.add))
                inv = cst("inv_count", 4, PADT)
                for g, w in enumerate(POOL_W):
                    win = (s1, s2)[g % 2][:, g, :]
                    V.scalar_tensor_tensor(df[:, g, :], win[:, body], 1.0 / w, u[:, g, body], ALU.mult, ALU.subtract)
                    last = V.tensor_tensor(fix[:, PADT * g:PADT * (g + 1)], win[:, PADT:2 * PADT], inv[:, g, :], ALU.mult)
                link(last)
                V.tensor_tensor(df[:, :, 0:PADT], fix.rearrange("p (g n) -> p g n", g=4), u[:, :, PADT:2 * PADT],
                                ALU.subtract).then_inc(event("fox_diff"), 1)
                for tile in (3, 4, 5):
                    prep("fox", tile)
                prep("fox", 6, (0, 1))
                prep("fox", 7, (0, 1))
                dve.wait_ge(small_done, 1)
                for t in range(NT):
                    last = V.tensor_tensor(fox["z"][:, 8 * t:8 * t + 8], A[2][:, 8 * t:8 * t + 8], fox["bf"], ALU.add)
                link(last)
                V.scalar_tensor_tensor(fox["nz"], fox["z"], -1.0, fox["z"], ALU.mult, ALU.min).then_inc(event("fox_nz"), 1)
                dve.wait_ge(event("fox_ln"), 1)
                V.scalar_tensor_tensor(fox["logf"], fox["z"], 0.0, fox["e"], ALU.min, ALU.subtract
                                       ).then_inc(event("fox_logf"), 1)
                for g in range(4):
                    dve.wait_ge(o_hi, g + 1)
                    V.scalar_tensor_tensor(ml[:, g, :], TB[g][:, 0:S], gcol("pool_scale", g),
                                           mh[:, g, :].bitcast(F32), ALU.mult, ALU.subtract
                                           ).then_inc(o_lo, 1)
                dve.wait_ge(event("fox_sums"), 1)
                V.tensor_scalar(fox["nF"].rearrange("p t n -> p (t n)"), A[2][:, 16:32], -1.0, None, ALU.mult)
                dve.wait_ge(event("fox_sums_hi"), 1)
                V.scalar_tensor_tensor(xh[32:40, 0, :], A[3][32:40, 0:S], -1.0, xh[32:40, 0, :].bitcast(F32),
                                       ALU.mult, ALU.subtract).then_inc(event("fox_rows"), 1)
                attend("fox", fox["o"])
                split_out("fox", 4)
                prep("fox", 6, (2,))
                prep("fox", 7, (2,))
                prep("fox", 8)
                residual("fox", 1.0)

            def mla_mixer():
                norm("mla")
                V.memset(mla["v"][:, :, :, MLA_V:], 1.0)
                prep("mla", 1)
                prep("mla", 2, (0, 1))
                dve.wait_ge(w2_landed, 32)
                link(V.tensor_copy(mla["pos"], mla["posi"].bitcast(I32)))
                for t in range(NT):
                    last = V.tensor_scalar(mla["ang"][:, t, :], cst("inv_freq"), mla["pos"][:, t:t + 1], None, ALU.mult)
                link(last)
                two_pi, big = 2.0 * np.pi, 1.5 * 2.0 ** 23
                parts = (6.28125, 0.0019350051879882812, two_pi - 6.28125 - 0.0019350051879882812)
                for off, dst in ((0.0, mla["rs_in"]), (0.25, mla["rc_in"])):
                    link(V.tensor_scalar(mla["turn"], mla["ang"], 1.0 / two_pi, off, ALU.mult, ALU.add))
                    link(V.tensor_scalar(mla["turn"], mla["turn"], big, big, ALU.add, ALU.subtract))
                    src = mla["ang"]
                    for c in parts:
                        link(V.scalar_tensor_tensor(dst, mla["turn"], -c, src, ALU.mult, ALU.add))
                        src = dst
                    if off:
                        link(V.tensor_scalar(dst, dst, np.pi / 2, None, ALU.add))
                    V.tensor_scalar(dst, dst, -3.1415925, 3.1415925, ALU.max, ALU.min).then_inc(event("mla_ang"), 1)
                    dve.wait_ge(event("mla_ang"), 1 if off == 0.0 else 2)
                dve.wait_ge(event("mla_sq"), 4)
                for i, n in enumerate((Q_LORA, KV_LORA)):
                    last = V.tensor_scalar(mla["ms"][:, :, i], mla["ss"][:, :, i], 1.0 / n, EPS, ALU.mult, ALU.add)
                last.then_inc(mx_ready, 1)
                dve.wait_ge(mx_pow, 1)
                for t in range(NT):
                    for i, (c0, c1) in enumerate(((0, Q_LORA), (Q_LORA, Q_LORA + KV_LORA))):
                        last = V.tensor_scalar(mla["cn"][:, t, c0:c1], mla["cin"][:, t, c0:c1], mla["rs"][:, t, i:i + 1],
                                               None, ALU.mult)
                    last.then_inc(event("mla_cn"), 1)
                for c in range(3):
                    g = gcol("mla_q_norm", c) if c < 2 else gcol("mla_kv_norm", 0)
                    dve.wait_ge(event("mla_c_hi"), c + 1)
                    V.scalar_tensor_tensor(mlf[:, c * S:(c + 1) * S], TB[c][:, 0:S], g,
                                           mhf[:, c * S:(c + 1) * S].bitcast(F32), ALU.mult, ALU.subtract
                                           ).then_inc(event("mla_c_lo"), 1)
                dve.wait_ge(event("mla_cs"), 2)
                R2 = ROPE // 2

                def rotate(x1, x2, o1, o2, cos, sin, t1, t2, done=None):
                    V.tensor_tensor(t1, x1, sin, ALU.mult)
                    link(V.tensor_tensor(t2, x2, sin, ALU.mult))
                    V.tensor_tensor(o1, x1, cos, ALU.mult)
                    link(V.tensor_tensor(o2, x2, cos, ALU.mult))
                    V.tensor_tensor(o1, o1, t2, ALU.subtract)
                    last = V.tensor_tensor(o2, o2, t1, ALU.add)
                    last.then_inc(done, 1) if done is not None else link(last)

                at = Q_LORA + KV_LORA
                cin, kr = mla["cin"], mla["kr"]
                rotate(cin[:, :, at:at + R2], cin[:, :, at + R2:at + ROPE], kr[:, :, 0:R2], kr[:, :, R2:ROPE],
                       mla["cos"], mla["sin"], mla["t1"][:, 0:NT, :], mla["t2"][:, 0:NT, :])
                for t in range(NT):
                    k = mla["k"][:, t, :].rearrange("p (h n) -> p h n", n=QK)[:, :, NOPE:QK]
                    last = V.tensor_copy(k, wide(kr[:, t, :].unsqueeze(1), MLA_H, ROPE))
                prep("mla", 2, (2,))
                prep("mla", 3)
                prep("mla", 4, (0,))
                dve.wait_ge(event("mla_b_out"), 6)
                for t in range(NT):
                    q = mla["q"][:, t, :].rearrange("p (h n) -> p h n", n=QK)
                    x1, x2 = q[:, :, NOPE:NOPE + R2], q[:, :, NOPE + R2:QK]
                    rotate(x1, x2, x1, x2, wide(mla["cos"][:, t, :].unsqueeze(1), MLA_H, R2),
                           wide(mla["sin"][:, t, :].unsqueeze(1), MLA_H, R2), mla["t1"], mla["t2"],
                           event("mla_roped") if t == NT - 1 else None)
                prep("mla", 4, (1,))
                prep("mla", 5, (0,))
                attend("mla", mla["o"])
                split_out("mla", KC)
                prep("mla", 4, (2,))
                prep("mla", 5, (1, 2))
                prep("mla", 6)
                residual("mla", 1.0)

            def mlstm_mixer():
                norm("mlstm")
                V.memset(mls["v"][:, :, :, ML_DV:], 1.0)
                V.memset(mls["k"][HD:P, :, :], 0.0)
                V.memset(k_odd[0:HD, :, :], 0.0)
                link(V.memset(mls["top"][0:40], 0.0))
                for tile in range(1, 10):
                    prep("mlstm", tile)
                z, F_, top = mls["z"], mls["F"], mls["top"][0:40]
                dve.wait_ge(small_done, 2)
                for t in range(NT):
                    last = V.tensor_tensor(z[:, t, :], A[0][:, 16 * t:16 * t + 16], mls["bif"], ALU.add)
                link(last)
                V.scalar_tensor_tensor(mls["nz"], z[:, :, 8:16], -1.0, z[:, :, 8:16], ALU.mult, ALU.min).then_inc(event("ml_nz"), 1)
                dve.wait_ge(event("ml_ln"), 1)
                V.scalar_tensor_tensor(mls["logf"], z[:, :, 8:16], 0.0, mls["e"], ALU.min, ALU.subtract
                                       ).then_inc(event("ml_logf"), 1)
                dve.wait_ge(event("ml_sums"), 2)
                link(V.tensor_copy(F_, A[1][:, 0:16].rearrange("p (t n) -> p t n", t=NT)))
                V.tensor_tensor(mls["R"], z[:, :, 0:8], F_, ALU.subtract)
                for at in (0, 32):
                    last = V.tensor_copy(mls["li"][at:at + 8, :], A[3][at:at + 8, 0:S])
                link(last)
                for at in (0, 32):
                    last = V.scalar_tensor_tensor(top[at:at + 8, 0, P:], A[2][at:at + 8, 0:S], -1.0,
                                                  mls["li"][at:at + 8, :], ALU.mult, ALU.add)
                link(last)
                for n in range(8):
                    src, dst, back = top[:, n % 2, P:], top[:, 1 - n % 2, P:], top[:, n % 2, P - 2 ** n:P + S - 2 ** n]
                    if n == 0:
                        last = V.scalar_tensor_tensor(dst, src, 0.0, back, ALU.max, ALU.max)
                    else:
                        last = V.tensor_tensor(dst, src, back, ALU.max)
                    link(last) if n < 7 else last.then_inc(event("ml_top"), 1)
                dve.wait_ge(event("ml_top_hi"), 1)
                V.scalar_tensor_tensor(hidh[32:40, 0, :], top[32:40, 0, P:], -1.0, hidh[32:40, 0, :].bitcast(F32), ALU.mult,
                                       ALU.subtract).then_inc(event("ml_top_lo"), 1)
                dve.wait_ge(event("ml_top_turned"), 1)
                V.tensor_tensor(mls["m"], A[1][:, 32:48].rearrange("p (t n) -> p t n", t=NT), F_, ALU.add
                                ).then_inc(event("ml_top_out"), 1)
                for i in range(ML_H):
                    dve.wait_ge(e_done, WPV["mlstm"] + i + 1)
                    V.tensor_tensor(PT[:, i % 2, :], PT[:, i % 2, :], X[i % 2][:, 0:TRI], ALU.mult).then_inc(w_done, 1)
                dve.wait_ge(event("ml_em"), 1)
                dve.wait_ge(o_out, OUT["mlstm"] + ML_H)
                den = mls["o"][:, :, :, ML_DV]
                link(V.scalar_tensor_tensor(mls["den"], den, -1.0, den, ALU.mult, ALU.max))
                link(V.tensor_tensor(mls["c"], mls["den"], mls["b"], ALU.max))
                link(V.reciprocal(mls["c"], mls["c"]))
                dve.wait_ge(event("ml_sq"), NT * ML_H)
                link(V.tensor_tensor(mls["a"], mls["ssq"], mls["c"], ALU.mult))
                link(V.tensor_tensor(mls["a"], mls["a"], mls["c"], ALU.mult))
                V.tensor_scalar(mls["a"], mls["a"], 1.0 / ML_DV, EPS, ALU.mult, ALU.add).then_inc(mx_ready, 1)
                dve.wait_ge(mx_pow, 2)
                link(V.tensor_tensor(mls["c"], mls["c"], mls["d"], ALU.mult))
                for t in range(NT):
                    o = mls["o"][:, t, :, 0:ML_DV]
                    V.tensor_tensor(o, o, wide(mls["c"][:, t, :].unsqueeze(2), ML_H, ML_DV), ALU.mult
                                    ).then_inc(event("ml_y"), 1)
                for c in range(ML_H):
                    dve.wait_ge(event("ml_turned"), c // 2 + 1)
                    if c >= 2:
                        dve.wait_ge(o_lo, 16 + c - 1)
                    sc = mls["sc"][:, c % 2, 0:S]
                    V.scalar_tensor_tensor(sc, TB[c // 2][:, c % 2 * S:(c % 2 + 1) * S], gcol("a_g_head_2", c),
                                           mls["og"][:, c, :], ALU.mult, ALU.mult).then_inc(event("ml_mix"), 1)
                    if c >= 1:
                        ml_lo(c - 1)
                ml_lo(ML_H - 1)
                for tile in (10, 11, 12):
                    prep("mlstm", tile)
                residual("mlstm", 1.0)

            def ml_lo(c):
                dve.wait_ge(o_hi, 16 + c + 1)
                low(ml[:, c, :], mls["sc"][:, c % 2, 0:S], mh[:, c, :], o_lo)

            def kv_stage():
                norm("kv")
                V.memset(nsa["kC"], 0.0).then_inc(event("kv_zero"), 1)
                V.memset(nsa["vS"][:, :, :, HD:], 1.0)
                V.memset(nsa["vW"][:, :, :, HD:], 1.0)
                for tile in range(1, 4):
                    prep("kv", tile)
                dve.wait_ge(event("kv_ksw"), 4)
                k = nsa["ksw"].rearrange("p t g n -> p (t g) n")
                sq = yf[:, 0:1024].rearrange("p (r n) -> p r n", n=HD)
                link(V.tensor_tensor(sq, k, k, ALU.mult))
                link(V.tensor_reduce(nsa["ss"][:, 0:16], sq, AX.X, ALU.add))
                V.tensor_scalar(nsa["ms"][:, 0:16], nsa["ss"][:, 0:16], 1.0 / HD, EPS, ALU.mult, ALU.add
                                ).then_inc(mx_ready, 1)
                dve.wait_ge(mx_pow, 3)
                dup = yf.rearrange("p (r d n) -> p r d n", d=2, n=HD)
                for d in range(2):
                    V.tensor_tensor(dup[:, :, d, :], k, wide(nsa["rs"][:, 0:16].unsqueeze(2), 16, HD), ALU.mult
                                    ).then_inc(event("kv_dup"), 1)
                prep("kv", 4)
                prep("kv", 5)
                dve.wait_ge(event("kv_dup"), 2)
                blk = nsa["blk"]
                for kind in range(2):
                    dve.wait_ge(event("kv_c_cols"), 4 if kind else 2)
                    for jh in range(2):
                        src = nsa["cT"][:, 4 * kind:4 * kind + 4, 16 * jh:16 * jh + CMP_STRIDE * NCMP]
                        src = src.rearrange("p g (c j e) -> p j g c e", c=NCMP, e=2)[:, :, :, :, 0]
                        pos = pe_col[:, 16 * kind + 8 * jh:16 * kind + 8 * jh + 8]
                        pos = wide(pos.unsqueeze(2).unsqueeze(3), 8, NKV, NCMP)
                        dst = blk[:, 8 * jh:8 * jh + 8, :].rearrange("p j (g c) -> p j g c", g=NKV)
                        last = V.tensor_tensor(dst, src, pos, ALU.add)
                    last.then_inc(event("kv_blk"), 1)
                    at = slice(960 * kind, 960 * (kind + 1))
                    dve.wait_ge(event("kv_blk_hi"), kind + 1)
                    low(mlf[:, at], blk.rearrange("p j r -> p (j r)"), mhf[:, at], event("kv_blk_lo"))
                    dve.wait_ge(event("kv_blk_lo"), kind + 1)
                prep("kv", 6)
                V.memset(nsa["vC"], 0.0).then_inc(event("kv_zero"), 1)
                for kind in range(2):
                    dve.wait_ge(event("kv_sig"), kind + 1)
                    x = nsa["hkr"][0:60, kind, :]
                    V.tensor_tensor(x, x, (G[0], A[0])[kind][0:60, 0:CMP_HID], ALU.mult).then_inc(event("kv_act"), 1)
                    if kind == 0:
                        prep("kv", 7)
                dve.wait_ge(event("kv_k2sq"), 1)
                V.tensor_scalar(nsa["ms"][0:60, 16:17], nsa["ss"][0:60, 16:17], 1.0 / HD, EPS, ALU.mult, ALU.add
                                ).then_inc(mx_ready, 1)
                dve.wait_ge(mx_pow, 4)
                for d in range(2):
                    last = V.tensor_scalar(nsa["kcn"][0:60, HD * d:HD * (d + 1)], A[2][0:60, 0:HD],
                                           nsa["rs"][0:60, 16:17], None, ALU.mult)
                last.then_inc(event("kv_kcn"), 1)
                prep("kv", 8)

            def nsa_mixer():
                norm("nsa")
                prep("nsa", 1)
                prep("nsa", 2)
                prep("nsa", 3)
                V.tensor_scalar(nsa["sc"][:, 0:1], gcol("b_q_norm_2", 0), HD ** -0.5, None, ALU.mult
                                ).then_inc(event("nsa_scale"), 1)
                for b, k in enumerate((nsa["kS"], nsa["kW"])):
                    dve.wait_ge(event("nsa_k_hi"), b + 1)
                    low(mh[HD:P, 4 * b:4 * b + 4, :], k[HD:P, :, :], mh[HD:P, 4 * b:4 * b + 4, :], event("nsa_k_lo"))
                dve.wait_ge(row_out, 5)
                rt = lambda x, t: x[:, 16 * t:16 * t + 16]
                for t in range(NT):
                    link(V.tensor_tensor(y[:, t, :], nsa["q"][:, t, :], nsa["q"][:, t, :], ALU.mult))
                    link(V.tensor_reduce(rt(nsa["ss"], t), y[:, t, :].rearrange("p (r n) -> p r n", n=HD), AX.X, ALU.add))
                    V.tensor_scalar(rt(nsa["ms"], t), rt(nsa["ss"], t), 1.0 / HD, EPS, ALU.mult, ALU.add).then_inc(mx_ready, 1)
                prep("nsa", 4, (0,))
                prep("nsa", 5, (0,))
                for t in range(NT):
                    dve.wait_ge(mx_pow, 5 + t)
                    q = nsa["q"][:, t, :].rearrange("p (r n) -> p r n", n=HD)
                    V.tensor_tensor(q, q, wide(nsa["rs"][:, 16 * t:16 * t + 16].unsqueeze(2), NQ, HD), ALU.mult
                                    ).then_inc(event("nsa_q"), 1)
                dve.wait_ge(event("nsa_gates"), 1)
                for t in range(NT):
                    last = V.tensor_scalar(nsa["g"][:, t, 0:NQ], nsa["g"][:, t, 0:NQ], cst("cmp_row_ok")[:, t:t + 1], None,
                                           ALU.mult)
                link(last)
                dve.wait_ge(event("nsa_kc_hi"), 1)
                low(small_h[HD:P, 0:NKV * CP], nsa["kC"][HD:P, :, :].rearrange("p g c -> p (g c)"), small_h[HD:P, 0:NKV * CP],
                    event("nsa_kc_lo"))
                pc, g = nsa["pc"], nsa["g"]
                pcr = pc.rearrange("p t h c -> p (t h) c")
                ss, ms, rs = (nsa[k][:, 0:8] for k in ("ss", "ms", "rs"))

                def compressed_scores(kvg):
                    dve.wait_ge(event("nsa_sc"), kvg + 1)
                    if kvg:
                        dve.wait_ge(event("nsa_oc"), kvg)
                    link(V.tensor_tensor(pc, A[2][:, 0:S].rearrange("p (t h c) -> p t h c", t=NT, c=CP),
                                         wide(cst("cmp_mask", NT, CP).unsqueeze(2), NT, 4, CP), ALU.add))
                    link(V.tensor_reduce(ss, pcr, AX.X, ALU.max))
                    V.tensor_tensor(pcr, pcr, wide(ss.unsqueeze(2), 8, CP), ALU.subtract).then_inc(event("nsa_pl"), 1)

                def compressed_probs(group):
                    if group % 2 == 0:
                        return
                    kvg = group // 2
                    dve.wait_ge(event("nsa_pe"), kvg + 1)
                    link(V.tensor_reduce(ms, pcr, AX.X, ALU.add))
                    link(V.reciprocal(rs, ms))
                    r = rs.rearrange("p (t h) -> p t h", t=NT)
                    link(V.tensor_tensor(r, r, g[:, :, 4 * kvg:4 * kvg + 4], ALU.mult))
                    V.tensor_tensor(pcr, pcr, wide(rs.unsqueeze(2), 8, CP), ALU.mult).then_inc(event("nsa_pc"), 1)

                def compressed_values(group):
                    if group % 2 == 0:
                        kvg = group // 2
                        dve.wait_ge(event("nsa_oc"), kvg + 1)
                        dve.wait_ge(o_out, OUT["nsa"] + 4 * kvg + 2)
                        part = nsa["o"][:, :, S * kvg:S * (kvg + 1)]
                        V.tensor_tensor(part, part, A[3][:, :].rearrange("p (t n) -> p t n", t=NT), ALU.add
                                        ).then_inc(event("nsa_oc_out"), 1)

                def gated(p, values, z):
                    kvg, br = p // 4, p // 2 % 2
                    h0 = 4 * kvg + 2 * (p % 2)
                    link(V.tensor_tensor(z, z, g[:, :, NQ * (1 + br) + h0:NQ * (1 + br) + h0 + 2].rearrange("p t a -> p a t"),
                                         ALU.mult))
                    part = nsa["o"][:, :, HD * h0:HD * (h0 + 2)].rearrange("p t (a n) -> p a t n", a=2)
                    rows_ = wide(z.unsqueeze(3), 2, NT, HD)
                    if br == 0:
                        V.tensor_tensor(part, values[:, :, :, 0:HD], rows_, ALU.mult).then_inc(o_out, 1)
                        return
                    tmp, n = nsa["tmp"], 2 * kvg + p % 2
                    if n:
                        dve.wait_ge(event("nsa_o"), n)
                    V.tensor_tensor(tmp, values[:, :, :, 0:HD], rows_, ALU.mult).then_inc(o_out, 1)
                    dve.wait_ge(o_out, OUT["nsa"] + p + 1)
                    dve.wait_ge(event("nsa_oc_out"), kvg + 1)
                    V.tensor_tensor(part, part, tmp, ALU.add).then_inc(event("nsa_o"), 1)

                def queries_lo(kvg):
                    for n, a in enumerate((0, 2, 1, 3)):
                        dve.wait_ge(event("nsa_qd_hi"), 4 * kvg + n + 1)
                        V.scalar_tensor_tensor(xl[:, 4 * (kvg % 2) + a, :], A[2 + a // 2][:, a % 2 * S:(a % 2 + 1) * S],
                                               nsa["sc"][:, 0:1], xh[:, 4 * (kvg % 2) + a, :].bitcast(F32), ALU.mult,
                                               ALU.subtract).then_inc(event("nsa_qd_lo"), 1)

                def queries(g):
                    if g == 0:
                        queries_lo(0)
                    if g % 2 == 0:
                        compressed_scores(g // 2)
                    elif g // 2 + 1 < NKV:
                        queries_lo(g // 2 + 1)

                attend("nsa", nsa["o"], gated, compressed_probs, queries, compressed_values)
                split_out("nsa", KC)
                prep("nsa", 4, (1,))
                prep("nsa", 5, (1,))
                prep("nsa", 6)
                residual("nsa", 1.0)

            for x in ("u", "s1", "s2"):
                last = V.memset(fox[x][:, :, 0:PADT], 0.0)
            link(last)
            mixers = dict(fox=fox_mixer, mla=mla_mixer, mlstm=mlstm_mixer, kv=kv_stage, nsa=nsa_mixer)
            for name in PHASES:
                if name == "ffn4":
                    norm("final")
                if name.startswith("ffn"):
                    norm(name)
                    if name == "ffn0":
                        prep(name, 0)
                    ffn(name)
                else:
                    mixers[name]()


STEPS = {"fox": FOX_H, "mla": MLA_H, "nsa": 2 * NQ}
OUT_BANKS = {"fox": FOX_H // 2, "mla": MLA_H // 2, "nsa": NQ}
TURNED_BEFORE = {"fox": 0, "mla": 2, "nsa": 6}


def o_count(name, c):
    base = {"fox": 0, "mla": 8, "mlstm": 16, "nsa": 24}[name]
    if name == "mlstm" or name == "fox" and c < 4:
        return base + c + 1
    if name == "fox":
        return base + 4 + CHUNKS.index(c - 4) + 1
    return base + CHUNKS.index(c) + 1


ROW_OUT = {"mlstm": 2, "kv": 4, "nsa": 5}
ROWS_COUNT = 16 * (len(GAIN_ROWS) - 1 + 2 + 1)
SMALL_COUNT = 16 * 6

_OUT = (1, S, D)


def kernel(**inputs):
    import concourse.bacc as bacc
    from concourse.bass_utils import run_bass_kernel_spmd

    nc = bacc.Bacc("TRN2", target_bir_lowering=False, num_devices=1)
    arrays, W = {}, {}

    def given(name, a):
        arrays[f"in_{name}"] = a
        return nc.dram_tensor(f"in_{name}", a.shape, mybir.dt.from_np(a.dtype), kind="ExternalInput").ap()

    for name, a in inputs.items():
        a = np.ascontiguousarray(a)
        W[name] = given(name, a)
    W["const"] = given("const", shape_constants())
    for name in ("ab_w_in", "ab_b_forget", "pool_w", "pool_scale", "ab_w_out", "mla_w_in", "mla_q_norm", "mla_kv_norm",
                 "mla_w_q_b", "mla_w_kv_b", "mla_w_out", "a_w_in_2", "a_b_if_2", "a_g_head_2", "a_w_out_2",
                 "b_w_in_2", "b_q_norm_2", "b_w_out_2"):
        W[name] = W[name][0]
    W["a_b_if_2"] = W["a_b_if_2"].rearrange("a b -> (a b)")
    W["b_q_norm_2"] = W["b_q_norm_2"].rearrange("(a n) -> a n", a=1)
    W["norm_ffn"] = W["norm_ffn"].rearrange("a b d -> (a b) d")
    W["ffn_norm_2"] = W["ffn_norm_2"].rearrange("a b d -> (a b) d")
    out = nc.dram_tensor("out", _OUT, F32, kind="ExternalOutput").ap()
    blocks_program(nc, W, out)
    r = run_bass_kernel_spmd(nc, [arrays], core_ids=[0])
    return r.results[0]["out"]
```
